# Optimizing a Trainium2 kernel written in Bass

```python
import jax
import jax.numpy as jnp
from jax import lax
import numpy as np
import math
import jax, jax.numpy as jnp

D_MODEL = 1024
BATCH = 1
SEQ = 512
DEPTH = 2

CHUNK = 64
HEAD_DIM = 64
N_HEADS_A = 8
N_IDX_HEADS = 8
D_IDX = 64
TOPK_MAX = 256
Q_BLOCK = 128
N_HEADS_B = 8
N_PAST_CHUNKS = 8
BAND = (N_PAST_CHUNKS + 1) * CHUNK
REL_LO = -(CHUNK - 1)
REL_HI = 256
N_REL = REL_HI - REL_LO + 1
ROT_DIM = HEAD_DIM // 4
ROPE_THETA = 500000.0
D_FF = -(-8 * D_MODEL // (3 * 256)) * 256
EPS = 1e-6
W_A = N_HEADS_A * HEAD_DIM
W_B = N_HEADS_B * HEAD_DIM
INDEX_SCALE = (D_IDX ** -0.5) * (N_IDX_HEADS ** -0.5)
IN_SIZES = (W_A, HEAD_DIM, HEAD_DIM, N_IDX_HEADS * D_IDX, D_IDX, N_IDX_HEADS,
            W_B, W_B, W_B, D_MODEL, D_MODEL)
D_IN = sum(IN_SIZES)


def rms_norm(x, g):
    xf = x.astype(jnp.float32)
    y = xf * lax.rsqrt(jnp.mean(xf * xf, axis=-1, keepdims=True) + EPS)
    return (y * g.astype(jnp.float32)).astype(x.dtype)

def rope_tables(positions):
    inv_freq = ROPE_THETA ** (-jnp.arange(0, ROT_DIM, 2, dtype=jnp.float32) / ROT_DIM)
    ang = positions.astype(jnp.float32)[..., None] * inv_freq
    return jnp.cos(ang)[:, :, None, :], jnp.sin(ang)[:, :, None, :]

def partial_rope(x, cos, sin):
    half = ROT_DIM // 2
    xr = x[..., :ROT_DIM].astype(jnp.float32)
    x1, x2 = xr[..., :half], xr[..., half:]
    rot = jnp.concatenate([x1 * cos - x2 * sin, x2 * cos + x1 * sin], axis=-1)
    return jnp.concatenate([rot.astype(x.dtype), x[..., ROT_DIM:]], axis=-1)

def to_blocks(a, size):
    b, s = a.shape[:2]
    return a.reshape(b, s // size, size, *a.shape[2:]).swapaxes(0, 1)

def from_blocks(a):
    n, b, size = a.shape[:3]
    return a.swapaxes(0, 1).reshape(b, n * size, *a.shape[3:])

def split_cols(z):
    offs, acc = [], 0
    for w in IN_SIZES[:-1]:
        acc += w
        offs.append(acc)
    return jnp.split(z, offs, axis=-1)

def sparse_indexed_attention(q, k, v, q_idx, k_idx, w_idx):
    s_len = q.shape[1]
    top_k = min(TOPK_MAX, s_len // 4)
    key_pos = jnp.arange(s_len)

    def block(args):
        qb, qib, wb, bid = args
        t = bid * Q_BLOCK + jnp.arange(Q_BLOCK)
        limit = (t // CHUNK + 1) * CHUNK
        admissible = key_pos[None, :] < limit[:, None]
        logits = jnp.einsum('bqhd,bsd->bqhs', qib, k_idx).astype(jnp.float32)
        score = jnp.einsum('bqh,bqhs->bqs', wb.astype(jnp.float32), jax.nn.relu(logits)) * INDEX_SCALE
        score = jnp.where(admissible[None], score, -jnp.inf)
        _, sel = lax.top_k(score, top_k)
        valid = sel < limit[None, :, None]
        kg = jax.vmap(lambda kb, ib: kb[ib])(k, sel)
        vg = jax.vmap(lambda vb, ib: vb[ib])(v, sel)
        s = jnp.einsum('bqhd,bqkd->bqhk', qb, kg).astype(jnp.float32) * (HEAD_DIM ** -0.5)
        s = jnp.where(valid[:, :, None, :], s, -jnp.inf)
        p = jax.nn.softmax(s, axis=-1).astype(vg.dtype)
        return jnp.einsum('bqhk,bqkd->bqhd', p, vg)

    n_blk = s_len // Q_BLOCK
    out = lax.map(block, (to_blocks(q, Q_BLOCK), to_blocks(q_idx, Q_BLOCK),
                          to_blocks(w_idx, Q_BLOCK), jnp.arange(n_blk)))
    return from_blocks(out)

def chunked_band_attention(q, k, v, rel_bias):
    s_len = q.shape[1]
    pad = N_PAST_CHUNKS * CHUNK
    kp = jnp.pad(k, ((0, 0), (pad, 0), (0, 0), (0, 0)))
    vp = jnp.pad(v, ((0, 0), (pad, 0), (0, 0), (0, 0)))
    i = jnp.arange(CHUNK)[:, None]
    j = jnp.arange(BAND)
    rel = jnp.clip(i - j[None, :] + pad, REL_LO, REL_HI) - REL_LO
    bias = rel_bias[:, rel].astype(jnp.float32)

    def chunk(args):
        qc, c = args
        kb = lax.dynamic_slice_in_dim(kp, c * CHUNK, BAND, axis=1)
        vb = lax.dynamic_slice_in_dim(vp, c * CHUNK, BAND, axis=1)
        valid = j >= (N_PAST_CHUNKS - c) * CHUNK
        s = jnp.einsum('bqhd,bkhd->bhqk', qc, kb).astype(jnp.float32) * (HEAD_DIM ** -0.5) + bias[None]
        s = jnp.where(valid[None, None, None, :], s, -jnp.inf)
        p = jax.nn.softmax(s, axis=-1).astype(vb.dtype)
        return jnp.einsum('bhqk,bkhd->bqhd', p, vb)

    out = lax.map(chunk, (to_blocks(q, CHUNK), jnp.arange(s_len // CHUNK)))
    return from_blocks(out)

def first_inputs(seed: int = 0) -> dict:
    key = jax.random.key(seed)
    ks = jax.random.split(key, 20)
    f32 = jnp.float32
    D = D_MODEL
    nrm = lambda k, shape, scale: jax.random.normal(k, shape, f32) * scale
    x = nrm(ks[0], (BATCH, SEQ, D), 1.0)
    c = nrm(ks[1], (BATCH, D), 1.0)
    offset = jax.random.randint(ks[2], (BATCH, 1), 0, 4096, dtype=jnp.int32)
    positions = (offset + jnp.arange(SEQ, dtype=jnp.int32)[None, :]).astype(jnp.int32)
    return {
        'x': x,
        'c': c,
        'positions': positions,
        'w_ada': nrm(ks[3], (DEPTH, D, 6 * D), 0.5 * D ** -0.5),
        'b_ada': nrm(ks[4], (DEPTH, 6 * D), 0.02),
        'g_mix': 1.0 + nrm(ks[5], (DEPTH, D), 0.02),
        'w_in': nrm(ks[6], (DEPTH, D, D_IN), D ** -0.5),
        'b_in': nrm(ks[7], (DEPTH, D_IN), 0.02),
        'qn_a': 1.0 + nrm(ks[8], (DEPTH, HEAD_DIM), 0.02),
        'kn_a': 1.0 + nrm(ks[9], (DEPTH, HEAD_DIM), 0.02),
        'qn_b': 1.0 + nrm(ks[10], (DEPTH, HEAD_DIM), 0.02),
        'kn_b': 1.0 + nrm(ks[11], (DEPTH, HEAD_DIM), 0.02),
        'rel_bias': nrm(ks[12], (DEPTH, N_HEADS_B, N_REL), 0.1),
        'w_oa': nrm(ks[13], (DEPTH, W_A, D), W_A ** -0.5),
        'w_ob': nrm(ks[14], (DEPTH, W_B, D), W_B ** -0.5),
        'w_out': nrm(ks[15], (DEPTH, D, D), D ** -0.5),
        'g_ffn': 1.0 + nrm(ks[16], (DEPTH, D), 0.02),
        'w_gu': nrm(ks[17], (DEPTH, D, 2 * D_FF), D ** -0.5),
        'w_down': nrm(ks[18], (DEPTH, D_FF, D), D_FF ** -0.5),
    }

def first_block(x, c, positions, w_ada, b_ada, g_mix, w_in, b_in, qn_a, kn_a, qn_b, kn_b,
              rel_bias, w_oa, w_ob, w_out, g_ffn, w_gu, w_down):
    b, s_len, _ = x.shape
    cos, sin = rope_tables(positions)
    c_act = jax.nn.silu(c)
    for l in range(DEPTH):
        mod = c_act @ w_ada[l] + b_ada[l]
        sh_m, sc_m, gt_m, sh_f, sc_f, gt_f = jnp.split(mod, 6, axis=-1)

        h = rms_norm(x, g_mix[l]) * (1.0 + sc_m[:, None]) + sh_m[:, None]
        z = h @ w_in[l] + b_in[l]
        qa, ka, va, qi, ki, wi, qb, kb, vb, ga, gb = split_cols(z)

        qa = partial_rope(rms_norm(qa.reshape(b, s_len, N_HEADS_A, HEAD_DIM), qn_a[l]), cos, sin)
        ka = partial_rope(rms_norm(ka.reshape(b, s_len, 1, HEAD_DIM), kn_a[l]), cos, sin)[:, :, 0]
        qi = partial_rope(qi.reshape(b, s_len, N_IDX_HEADS, D_IDX), cos, sin)
        ki = partial_rope(ki.reshape(b, s_len, 1, D_IDX), cos, sin)[:, :, 0]
        y_a = sparse_indexed_attention(qa, ka, va, qi, ki, wi).reshape(b, s_len, W_A) @ w_oa[l]

        qb = rms_norm(qb.reshape(b, s_len, N_HEADS_B, HEAD_DIM), qn_b[l])
        kb = rms_norm(kb.reshape(b, s_len, N_HEADS_B, HEAD_DIM), kn_b[l])
        vb = vb.reshape(b, s_len, N_HEADS_B, HEAD_DIM)
        y_b = chunked_band_attention(qb, kb, vb, rel_bias[l]).reshape(b, s_len, W_B) @ w_ob[l]

        merged = jax.nn.sigmoid(ga) * y_a + jax.nn.sigmoid(gb) * y_b
        x = x + gt_m[:, None] * (merged @ w_out[l])

        h2 = rms_norm(x, g_ffn[l]) * (1.0 + sc_f[:, None]) + sh_f[:, None]
        gate, up = jnp.split(h2 @ w_gu[l], 2, axis=-1)
        x = x + gt_f[:, None] * ((jax.nn.silu(gate) * up) @ w_down[l])
    return x


DEPTH_2 = 1

QBLK = 128
ATT_HEADS = 16
ATT_HEAD_DIM = 64
ATT_WIDTH = ATT_HEADS * ATT_HEAD_DIM
POOL_WINDOWS = (2, 4, 8, 16)
POOL_GROUPS = len(POOL_WINDOWS)
POOL_WIDTH = D_MODEL
POOL_GROUP_DIM = POOL_WIDTH // POOL_GROUPS
SSM_EXPAND = 2
SSM_INNER = SSM_EXPAND * D_MODEL
SSM_HEAD_DIM = 64
SSM_HEADS = SSM_INNER // SSM_HEAD_DIM
SSM_GROUPS = 4
SSM_HEADS_PER_GROUP = SSM_HEADS // SSM_GROUPS
SSM_STATE = 128
SSM_CONV = 4
SSM_CONV_DIM = SSM_INNER + 2 * SSM_GROUPS * SSM_STATE
N_BRANCHES = 3
N_EXPERTS = 16
N_EXPERT_GROUPS = 4
EXPERTS_PER_GROUP = N_EXPERTS // N_EXPERT_GROUPS
TOP_K = 2
EXPERT_DFF = 512
MOE_BLOCK = 256
DEEPNORM_ALPHA = (2 * DEPTH_2) ** 0.25
DEEPNORM_BETA = (8 * DEPTH_2) ** -0.25
LN_EPS = 1e-5
RMS_EPS = 1e-6
IN_SPLITS = (ATT_WIDTH, ATT_WIDTH, ATT_WIDTH, ATT_HEADS, POOL_WIDTH,
             SSM_INNER, SSM_CONV_DIM, SSM_HEADS, N_BRANCHES * D_MODEL)
IN_WIDTH = sum(IN_SPLITS)


def layer_norm(x, g=None, b=None):
    x32 = x.astype(jnp.float32)
    mu = jnp.mean(x32, axis=-1, keepdims=True)
    xc = x32 - mu
    y = xc * lax.rsqrt(jnp.mean(xc * xc, axis=-1, keepdims=True) + LN_EPS)
    if g is not None:
        y = y * g + b
    return y.astype(x.dtype)

def split_columns(proj):
    points, acc = [], 0
    for w in IN_SPLITS[:-1]:
        acc += w
        points.append(acc)
    return jnp.split(proj, points, axis=-1)

def forgetting_attention(q, k, v, log_f):
    S = q.shape[1]
    scale = ATT_HEAD_DIM ** -0.5
    F = jnp.transpose(jnp.cumsum(log_f, axis=1), (0, 2, 1))
    q, k, v = (jnp.transpose(t, (0, 2, 1, 3)) for t in (q, k, v))
    outs = []
    for blk in range(S // QBLK):
        s0, s1 = blk * QBLK, (blk + 1) * QBLK
        logits = jnp.einsum('bhqd,bhkd->bhqk', q[:, :, s0:s1], k[:, :, :s1]).astype(jnp.float32) * scale
        logits = logits + F[:, :, s0:s1, None] - F[:, :, None, :s1]
        mask = jnp.arange(s0, s1)[:, None] >= jnp.arange(s1)[None, :]
        p = jax.nn.softmax(jnp.where(mask, logits, -jnp.inf), axis=-1)
        outs.append(jnp.einsum('bhqk,bhkd->bhqd', p.astype(v.dtype), v[:, :, :s1]))
    o = jnp.concatenate(outs, axis=2)
    B_ = o.shape[0]
    return jnp.transpose(o, (0, 2, 1, 3)).reshape(B_, S, ATT_WIDTH)

def multiscale_pool(u, w_pool, pool_scale):
    Bsz, S, _ = u.shape
    u32 = u.astype(jnp.float32).reshape(Bsz, S, POOL_GROUPS, POOL_GROUP_DIM)
    cs = jnp.cumsum(u32, axis=1)
    pos = jnp.arange(1, S + 1, dtype=jnp.float32)[:, None]
    pooled = []
    for g, w in enumerate(POOL_WINDOWS):
        csg = cs[:, :, g]
        lagged = jnp.pad(csg, ((0, 0), (w, 0), (0, 0)))[:, :S]
        pooled.append((csg - lagged) / jnp.minimum(pos, float(w)) - u32[:, :, g])
    pooled = jnp.stack(pooled, axis=2)
    y = jnp.einsum('bsgc,gcd->bsgd', pooled, w_pool.astype(jnp.float32)).reshape(Bsz, S, POOL_WIDTH)
    return (y * pool_scale).astype(u.dtype)

def causal_depthwise_conv(u, w, b):
    out = lax.conv_general_dilated(
        u, w[:, None, :].astype(u.dtype), window_strides=(1,),
        padding=[(SSM_CONV - 1, 0)], dimension_numbers=('NWC', 'WIO', 'NWC'),
        feature_group_count=u.shape[-1])
    return out + b

def ssd_mixer(z, xbc, dt_raw, conv_w, conv_b, dt_bias, a_log, d_skip, norm_w, w_o):
    Bsz, S, _ = z.shape
    nc = S // CHUNK
    G, R, P, N, L = SSM_GROUPS, SSM_HEADS_PER_GROUP, SSM_HEAD_DIM, SSM_STATE, CHUNK
    f32 = jnp.float32
    xbc = jax.nn.silu(causal_depthwise_conv(xbc, conv_w, conv_b))
    xs, bm, cm = jnp.split(xbc, [SSM_INNER, SSM_INNER + G * N], axis=-1)
    xs = xs.astype(f32).reshape(Bsz, nc, L, G, R, P)
    bm = bm.astype(f32).reshape(Bsz, nc, L, G, N)
    cm = cm.astype(f32).reshape(Bsz, nc, L, G, N)
    dt = jax.nn.softplus(dt_raw.astype(f32) + dt_bias).reshape(Bsz, nc, L, G, R)
    a = -jnp.exp(a_log.astype(f32)).reshape(G, R)
    a_cs = jnp.cumsum(dt * a, axis=2)
    causal = jnp.tril(jnp.ones((L, L), bool))[:, :, None, None]
    seg = a_cs[:, :, :, None] - a_cs[:, :, None, :]
    decay = jnp.where(causal, jnp.exp(jnp.where(causal, seg, 0.0)), 0.0)
    cb = jnp.einsum('bclgn,bcsgn->bclsg', cm, bm)
    scores = cb[..., None] * decay * dt[:, :, None]
    y_diag = jnp.einsum('bclsgr,bcsgrp->bclgrp', scores, xs)
    decay_end = jnp.exp(a_cs[:, :, -1:] - a_cs)
    states = jnp.einsum('bcsgn,bcsgr,bcsgrp->bcgrpn', bm, decay_end * dt, xs)
    chunk_decay = jnp.exp(a_cs[:, :, -1])

    def step(h, inp):
        st, dec = inp
        return dec[..., None, None] * h + st, h

    h0 = jnp.zeros((Bsz, G, R, P, N), states.dtype)
    _, h_prev = lax.scan(step, h0, (jnp.moveaxis(states, 1, 0), jnp.moveaxis(chunk_decay, 1, 0)))
    h_prev = jnp.moveaxis(h_prev, 0, 1)
    y_off = jnp.einsum('bclgn,bcgrpn->bclgrp', cm, h_prev) * jnp.exp(a_cs)[..., None]
    y = y_diag + y_off + d_skip.astype(f32).reshape(G, R)[:, :, None] * xs
    y = y.reshape(Bsz, S, SSM_INNER) * jax.nn.silu(z.astype(f32))
    yg = y.reshape(Bsz, S, G, SSM_INNER // G)
    yg = yg * lax.rsqrt(jnp.mean(yg * yg, axis=-1, keepdims=True) + RMS_EPS)
    y = yg.reshape(Bsz, S, SSM_INNER) * norm_w
    return y.astype(z.dtype) @ w_o

def hybrid_mixer(h, w_in, b_forget, w_attn_o, w_pool, pool_scale, conv_w, conv_b,
                 dt_bias, a_log, d_skip, ssm_norm_w, w_ssm_o, w_out):
    Bsz, S, _ = h.shape
    proj = h @ w_in
    q, k, v, f_raw, u_pool, z, xbc, dt_raw, gate_raw = split_columns(proj)
    log_f = jax.nn.log_sigmoid(f_raw.astype(jnp.float32) + b_forget)
    hs = (Bsz, S, ATT_HEADS, ATT_HEAD_DIM)
    y_att = forgetting_attention(q.reshape(hs), k.reshape(hs), v.reshape(hs), log_f) @ w_attn_o
    y_pool = multiscale_pool(u_pool, w_pool, pool_scale)
    y_ssm = ssd_mixer(z, xbc, dt_raw, conv_w, conv_b, dt_bias, a_log, d_skip, ssm_norm_w, w_ssm_o)
    gates = jax.nn.sigmoid(gate_raw.astype(jnp.float32)).reshape(Bsz, S, N_BRANCHES, D_MODEL)
    merged = gates[:, :, 0] * y_att + gates[:, :, 1] * y_pool + gates[:, :, 2] * y_ssm
    return merged.astype(h.dtype) @ w_out

def grouped_moe(h, w_router, b_router, w1, w3, w2):
    Bsz, S, D = h.shape
    N = Bsz * S
    NK = N * TOP_K
    ht = h.reshape(N, D)
    probs = jax.nn.softmax((ht @ w_router).astype(jnp.float32), axis=-1)
    sel = probs + b_router
    group_score = lax.top_k(sel.reshape(N, N_EXPERT_GROUPS, EXPERTS_PER_GROUP), TOP_K)[0].sum(-1)
    g_idx = jnp.argmax(group_score, axis=-1)
    in_group = (jnp.arange(N_EXPERTS) // EXPERTS_PER_GROUP)[None, :] == g_idx[:, None]
    _, e_idx = lax.top_k(jnp.where(in_group, sel, -jnp.inf), TOP_K)
    gate_w = jnp.take_along_axis(probs, e_idx, axis=1)
    gate_w = gate_w / jnp.sum(gate_w, axis=-1, keepdims=True)
    e_flat = e_idx.reshape(NK)
    tok_flat = jnp.repeat(jnp.arange(N, dtype=jnp.int32), TOP_K)
    w_flat = gate_w.reshape(NK)
    order = jnp.argsort(e_flat)
    e_sorted, tok_sorted, w_sorted = e_flat[order], tok_flat[order], w_flat[order]
    counts = jnp.bincount(e_flat, length=N_EXPERTS)
    starts = jnp.cumsum(counts) - counts
    padded = ((counts + MOE_BLOCK - 1) // MOE_BLOCK) * MOE_BLOCK
    pends = jnp.cumsum(padded)
    pstarts = pends - padded
    dest = pstarts[e_sorted] + (jnp.arange(NK) - starts[e_sorted])
    P = NK + N_EXPERTS * MOE_BLOCK
    nblk = P // MOE_BLOCK
    slot_tok = jnp.full((P,), N, jnp.int32).at[dest].set(tok_sorted)
    slot_w = jnp.zeros((P,), jnp.float32).at[dest].set(w_sorted)
    blk_expert = jnp.minimum(
        jnp.searchsorted(pends, jnp.arange(nblk) * MOE_BLOCK, side='right'), N_EXPERTS - 1)
    x_pad = jnp.concatenate([ht, jnp.zeros((1, D), ht.dtype)], axis=0)
    xs = x_pad[slot_tok].reshape(nblk, MOE_BLOCK, D)

    def expert_block(args):
        xb, e = args
        return (jax.nn.silu(xb @ w1[e]) * (xb @ w3[e])) @ w2[e]

    ys = lax.map(expert_block, (xs, blk_expert)).reshape(P, D) * slot_w[:, None]
    out = jax.ops.segment_sum(ys, slot_tok, num_segments=N + 1)[:N]
    return out.reshape(Bsz, S, D).astype(h.dtype)

def second_inputs(seed: int = 0) -> dict:
    key = jax.random.key(seed)
    ks = jax.random.split(key, 26)

    def nrm(k, shape, scale):
        return jax.random.normal(k, shape, jnp.float32) * scale

    col_scale = jnp.concatenate([
        jnp.ones((2 * ATT_WIDTH,), jnp.float32),
        jnp.full((ATT_WIDTH,), DEEPNORM_BETA, jnp.float32),
        jnp.ones((IN_WIDTH - 3 * ATT_WIDTH,), jnp.float32)])
    dt0 = jnp.exp(jax.random.uniform(ks[9], (DEPTH_2, SSM_HEADS), jnp.float32,
                                     minval=math.log(1e-3), maxval=math.log(1e-1)))
    return {
        'x': nrm(ks[0], (BATCH, SEQ, D_MODEL), 1.0),
        'c': nrm(ks[1], (BATCH, D_MODEL), 1.0),
        'w_in': nrm(ks[2], (DEPTH_2, D_MODEL, IN_WIDTH), D_MODEL ** -0.5) * col_scale,
        'b_forget': 4.0 + nrm(ks[3], (DEPTH_2, ATT_HEADS), 0.5),
        'w_attn_o': nrm(ks[4], (DEPTH_2, ATT_WIDTH, D_MODEL), DEEPNORM_BETA * ATT_WIDTH ** -0.5),
        'w_pool': nrm(ks[5], (DEPTH_2, POOL_GROUPS, POOL_GROUP_DIM, POOL_GROUP_DIM), DEEPNORM_BETA * POOL_GROUP_DIM ** -0.5),
        'pool_scale': 1.0 + nrm(ks[6], (DEPTH_2, POOL_WIDTH), 0.1),
        'conv_w': nrm(ks[7], (DEPTH_2, SSM_CONV, SSM_CONV_DIM), SSM_CONV ** -0.5),
        'conv_b': nrm(ks[8], (DEPTH_2, SSM_CONV_DIM), 0.02),
        'dt_bias': dt0 + jnp.log(-jnp.expm1(-dt0)),
        'a_log': jnp.log(jax.random.uniform(ks[10], (DEPTH_2, SSM_HEADS), jnp.float32, minval=1.0, maxval=16.0)),
        'd_skip': 1.0 + nrm(ks[11], (DEPTH_2, SSM_HEADS), 0.1),
        'ssm_norm_w': 1.0 + nrm(ks[12], (DEPTH_2, SSM_INNER), 0.1),
        'w_ssm_o': nrm(ks[13], (DEPTH_2, SSM_INNER, D_MODEL), DEEPNORM_BETA * SSM_INNER ** -0.5),
        'w_out': nrm(ks[14], (DEPTH_2, D_MODEL, D_MODEL), DEEPNORM_BETA * D_MODEL ** -0.5),
        'w_ada': nrm(ks[15], (DEPTH_2, D_MODEL, 6 * D_MODEL), D_MODEL ** -0.5),
        'b_ada': nrm(ks[16], (DEPTH_2, 6 * D_MODEL), 0.02),
        'ln_mix_g': 1.0 + nrm(ks[17], (DEPTH_2, D_MODEL), 0.1),
        'ln_mix_b': nrm(ks[18], (DEPTH_2, D_MODEL), 0.02),
        'ln_ffn_g': 1.0 + nrm(ks[19], (DEPTH_2, D_MODEL), 0.1),
        'ln_ffn_b': nrm(ks[20], (DEPTH_2, D_MODEL), 0.02),
        'w_router': nrm(ks[21], (D_MODEL, N_EXPERTS), D_MODEL ** -0.5),
        'b_router': nrm(ks[22], (N_EXPERTS,), 0.01),
        'w_exp_gate': nrm(ks[23], (DEPTH_2, N_EXPERTS, D_MODEL, EXPERT_DFF), DEEPNORM_BETA * D_MODEL ** -0.5),
        'w_exp_up': nrm(ks[24], (DEPTH_2, N_EXPERTS, D_MODEL, EXPERT_DFF), DEEPNORM_BETA * D_MODEL ** -0.5),
        'w_exp_down': nrm(ks[25], (DEPTH_2, N_EXPERTS, EXPERT_DFF, D_MODEL), DEEPNORM_BETA * EXPERT_DFF ** -0.5),
    }

def second_block(x, c, w_in, b_forget, w_attn_o, w_pool, pool_scale, conv_w, conv_b,
              dt_bias, a_log, d_skip, ssm_norm_w, w_ssm_o, w_out, w_ada, b_ada,
              ln_mix_g, ln_mix_b, ln_ffn_g, ln_ffn_b, w_router, b_router,
              w_exp_gate, w_exp_up, w_exp_down):
    cond = jax.nn.silu(c)
    for l in range(DEPTH_2):
        mod = cond @ w_ada[l] + b_ada[l]
        sh_m, sc_m, g_m, sh_f, sc_f, g_f = jnp.split(mod[:, None, :], 6, axis=-1)
        h = layer_norm(x) * (1.0 + sc_m) + sh_m
        mix = hybrid_mixer(h, w_in[l], b_forget[l], w_attn_o[l], w_pool[l], pool_scale[l],
                           conv_w[l], conv_b[l], dt_bias[l], a_log[l], d_skip[l],
                           ssm_norm_w[l], w_ssm_o[l], w_out[l])
        x = layer_norm(DEEPNORM_ALPHA * x + g_m * mix, ln_mix_g[l], ln_mix_b[l])
        h = layer_norm(x) * (1.0 + sc_f) + sh_f
        ffn = grouped_moe(h, w_router, b_router, w_exp_gate[l], w_exp_up[l], w_exp_down[l])
        x = layer_norm(DEEPNORM_ALPHA * x + g_f * ffn, ln_ffn_g[l], ln_ffn_b[l])
    return x


def setup_inputs(seed=0):
    out = dict(first_inputs(seed))
    for name, value in second_inputs(seed + 1).items():
        if name != "x":
            out[name + "_2"] = value
    return out


def reference(
    x, c, positions, w_ada, b_ada, g_mix, w_in, b_in, qn_a, kn_a, qn_b, kn_b, rel_bias, w_oa,
    w_ob, w_out, g_ffn, w_gu, w_down, c_2, w_in_2, b_forget_2, w_attn_o_2, w_pool_2,
    pool_scale_2, conv_w_2, conv_b_2, dt_bias_2, a_log_2, d_skip_2, ssm_norm_w_2, w_ssm_o_2,
    w_out_2, w_ada_2, b_ada_2, ln_mix_g_2, ln_mix_b_2, ln_ffn_g_2, ln_ffn_b_2, w_router_2,
    b_router_2, w_exp_gate_2, w_exp_up_2, w_exp_down_2,
):
    x = first_block(
        x, c, positions, w_ada, b_ada, g_mix, w_in, b_in, qn_a, kn_a, qn_b, kn_b, rel_bias,
        w_oa, w_ob, w_out, g_ffn, w_gu, w_down,
    )
    return second_block(
        x, c_2, w_in_2, b_forget_2, w_attn_o_2, w_pool_2, pool_scale_2, conv_w_2, conv_b_2,
        dt_bias_2, a_log_2, d_skip_2, ssm_norm_w_2, w_ssm_o_2, w_out_2, w_ada_2, b_ada_2,
        ln_mix_g_2, ln_mix_b_2, ln_ffn_g_2, ln_ffn_b_2, w_router_2, b_router_2, w_exp_gate_2,
        w_exp_up_2, w_exp_down_2,
    )


_drawn_inputs = setup_inputs


def setup_inputs(seed=0):
    import zlib

    import numpy as np

    out = dict(_drawn_inputs(seed))
    spreads = {}
    factors = {'g_mix': 8.0,
     'b_in': 5.912,
     'qn_a': 8.0,
     'kn_a': 8.0,
     'qn_b': 8.0,
     'kn_b': 8.0,
     'rel_bias': 8.0,
     'g_ffn': 6.229,
     'b_forget_2': 56.264,
     'pool_scale_2': 38.312,
     'conv_b_2': 58.595,
     'd_skip_2': 64.0,
     'ssm_norm_w_2': 39.888,
     'b_ada_2': 4.354,
     'ln_ffn_b_2': 2.848,
     'b_router_2': 3.211,
     'w_attn_o_2': 8.0,
     'dt_bias_2': 6.555,
     'a_log_2': 7.026}
    for name, (base, spread) in spreads.items():
        noise = np.random.default_rng([zlib.crc32(name.encode()), seed]).standard_normal(out[name].shape)
        drawn = base * np.exp(spread * noise) if base else spread * noise
        out[name] = jnp.asarray(drawn.astype(out[name].dtype))
    for name, factor in factors.items():
        out[name] = (out[name] * factor).astype(out[name].dtype)
    return out
```

```python
import numpy as np
import concourse.bass as bass
from concourse import mybir
from contextlib import ExitStack, contextmanager

F32 = mybir.dt.float32
I32 = mybir.dt.int32
ALU = mybir.AluOpType
ACT = mybir.ActivationFunctionType
AX = mybir.AxisListType
ds = bass.ds

P = 128
D, SEQ, KC = 1024, 512, 8
QT = SEQ // P
LAYERS = 2
HD = 64
FF_T = 2816 // P
FF = FF_T * P
TOP_K = 128
IDX_SCALE = 64 ** -0.5 * 8 ** -0.5
EPS, LN_EPS = 1e-6, 1e-5
ALPHA = 2 ** 0.25
NEG = -1e30
TAKEN = -3e38
E_N, E_FF = 16, 512
WINDOWS = (2, 4, 8, 16)

QA, KA, VA, QI, KI, WI, QB, KB, VB, GA, GB = 0, 512, 576, 640, 1152, 1216, 1224, 1736, 2248, 2760, 3784
Q2, K2, V2, F2, U2, Z2, XBC2, DT2, G2 = 0, 1024, 2048, 3072, 3088, 4112, 6160, 9232, 9264


def column_map(parts):
    at, out = 0, {}
    for name, n in parts:
        out[name] = (at, at + n)
        at += n
    return out, at


VEC1, NV1 = column_map([("b_ada", 48), ("g_mix", 8), ("g_ffn", 8), ("qa", 4), ("qi", 4), ("ka", 1), ("ki", 1),
                        ("va", 1), ("wi", 1), ("qb", 4), ("kb", 4), ("vb", 4), ("ga", 8), ("gb", 8),
                        ("qn_a", 1), ("kn_a", 1), ("qn_b", 1), ("kn_b", 1)])
SP_N = 38
VEC2, NV2 = column_map([("b_ada", 48), ("pool_scale", 8), ("ln_mix_g", 8), ("ln_mix_b", 8), ("ln_ffn_g", 8),
                        ("ln_ffn_b", 8), ("b_forget", 1), ("dt_bias", 1), ("a_log", 1), ("ssm", 4 * SP_N),
                        ("w_router", KC * E_N), ("b_router", E_N)])
CST, NCST = column_map([("ident", P), ("blockones", P), ("ones", P), ("rope", P), ("last", P), ("adm", SEQ),
                        ("causal", SEQ), ("tri", P), ("recip", 4 * 16), ("inv_freq", 1), 
                        ("revidx", E_N)])


class Plan:

    def __init__(self, stages, start=None):
        self.stages, self.inc, self.base, at = stages, {}, {}, dict(start or {})
        for name, turns, inc in stages:
            self.inc[name], self.base[name] = inc, dict(at)
            for k, n in inc.items():
                at[k] = at.get(k, 0) + n * turns
        self.total = at

    def at(self, stage, counter, turn=0, layer=0):
        value = self.base[stage].get(counter, 0) + turn * self.inc[stage].get(counter, 0)
        return layer * self.total.get(counter, 0) + value


LAYER = Plan([
    ("ada", 6, dict(slot=1, lin=1)),
    ("norm1", 1, dict(aux=1)),
    ("misc", 1, dict(slot=1, lin=2, aux=5, prep=4, nrm=1, rope=1)),
    ("idx", 1, dict(slot=2, lin=2, aux=4, prep=4, s=12, iu=24)),
    ("A", 1, dict(slot=2, lin=2, aux=8, prep=4, nrm=4, rope=4, s=16, u=32, o=4)),
    ("B", 1, dict(slot=2, lin=6, aux=12, prep=12, nrm=8, s=16, u=32, o=4)),
    ("gates", 4, dict(slot=1, lin=4, sg=4)),
    ("out", 1, dict(slot=1, lin=4)),
    ("norm2", 1, dict(aux=1)),
    ("gu", 11, dict(slot=1, lin=2, sg=2)),
    ("down", 4, dict(slot=1, lin=1)),
])
SECOND = Plan([
    ("ada", 6, dict(slot=1, lin=1)),
    ("ln1", 1, dict(aux=2)),
    ("fd", 1, dict(slot=1, lin=1, aux=4)),
    ("att", 4, dict(slot=1, lin=3, aux=2, prep=6, s=8, u=16, o=2)),
    ("attout", 4, dict(slot=1, lin=2, sg=2)),
    ("pool", 4, dict(slot=1, lin=3, sg=2)),
    ("ssd", 4, dict(slot=2, lin=5, aux=1, sg=4)),
    ("ssdout", 4, dict(slot=1, lin=2, sg=2)),
    ("out", 1, dict(slot=1, lin=4)),
    ("ln2", 1, dict(aux=2)),
    ("ln3", 1, dict(aux=2)),
    ("router", 1, dict(aux=2)),
    ("moe", 8, dict(slot=3, lin=16, aux=2, sg=8)),
    ("ln4", 1, dict(aux=2)),
], {k: LAYERS * n for k, n in LAYER.total.items()})

SLOTS_1 = ([KC * 512] * 12 + [2 * KC * P, KC * 72] + [KC * P] * 8 + [3 * KC * P] * 4 + [2 * KC * P + 8 * P] * 8
           + [KC * 512] * 2 + [2 * KC * P] * 22 + [FF_T * P] * 8)
SLOTS_2 = ([KC * 512] * 12 + [KC * 16, KC * 32] + [3 * KC * P] * 8 + [2 * KC * P] * 8
           + [KC * 256, KC * 256 + 512] * 4 + [KC * 512, KC * 256, KC * 256, KC * 256] * 4 + [KC * P + 16 * P] * 8
           + [KC * 512] * 2 + [KC * 512] * 48)
W1_TOTAL = sum(SLOTS_1) * P
assert len(SLOTS_1) == 2 * LAYER.total["slot"], (len(SLOTS_1), LAYER.total)
assert len(SLOTS_2) == 2 * (SECOND.total["slot"] - LAYERS * LAYER.total["slot"])


class Steps:

    def __init__(self, eng, sem):
        self.eng, self.sem, self.n = eng, sem, 0

    def __call__(self, ins):
        self.n += 1
        ins.then_inc(self.sem, 1)
        self.eng.wait_ge(self.sem, self.n)

    def tell(self, ins, signal):
        self(ins)
        self.eng.sem_inc(signal, 1)

    def restart(self):
        if self.n:
            self.eng.sem_clear(self.sem)
            self.n = 0

    @contextmanager
    def loop(self, start, end):
        self.restart()
        with self.eng.Fori(start, end) as i:
            yield i
            self.restart()


def two_blocks(nc, w_all, vec1_all, vec2_all, consts, x_in, pos_in, cond, rel, out):
    ctx = ExitStack()
    with ctx:
        sems = {}

        def sem(name):
            if name not in sems:
                sems[name] = ctx.enter_context(nc.semaphore(name))
            return sems[name]

        def sb(name, *shape, dt=F32):
            t = ctx.enter_context(nc.sbuf_tensor(name, [P, *shape], dt))
            return t[:, :, :] if len(shape) == 2 else t[:, :]

        x = sb("x", KC, SEQ)
        h = sb("h", KC, SEQ)
        ring = [sb("ring0", 4096), sb("ring1", 4096)]
        cst = sb("cst", NCST)
        vec = sb("vec", NV1)
        vec2 = sb("vec2", NV2)
        mod = sb("mod", 48)
        gain = sb("gain", 16)
        csil = sb("csil", 16)
        cosT, sinT = sb("cosT", SEQ), sb("sinT", SEQ)
        rstd = sb("rstd", SEQ)
        tmp = sb("tmp", SEQ)
        sg = [sb("sg0", SEQ), sb("sg1", SEQ)]
        abuf = sb("abuf", 14, SEQ)
        qT, kT = [abuf[:, 0, :], abuf[:, 1, :]], [abuf[:, 2, :], abuf[:, 3, :]]
        vtok = [abuf[:, 4 + b, :].rearrange("p (a b) -> p a b", b=P) for b in range(2)]
        raw = [abuf[:, 6, :], abuf[:, 7, :]]
        sm, pr, pts = ([abuf[:, n, :], abuf[:, n + 1, :]] for n in (8, 10, 12))
        sq, rs = sb("sq", SEQ), sb("rs", SEQ)
        nmax, esum, rcp = sb("nmax", 8), sb("esum", 8), sb("rcp", 8)
        ARENA = 22800
        arena = sb("arena", ARENA)
        cursor = [0]

        def part(*shape):
            n = int(np.prod(shape))
            v = arena[:, cursor[0]:cursor[0] + n]
            cursor[0] += n
            assert cursor[0] <= ARENA, cursor[0]
            if len(shape) == 2:
                v = v.rearrange("p (a b) -> p a b", b=shape[1])
            return v

        attA, attB = part(4, SEQ), part(4, SEQ)
        mask, score = part(QT, SEQ), part(QT, SEQ)
        merged = part(KC, SEQ)
        hid = arena[:, 0:FF_T * SEQ].rearrange("p (a b) -> p a b", b=SEQ)
        relb = part(8, SEQ)
        kaT, kiT, va = part(SEQ), part(SEQ), part(QT, HD)
        wtok, top8 = part(QT, 8), part(8)
        cursor[0] = 0
        merged2 = part(KC, SEQ)
        negF, ftok = part(SEQ), part(QT, 16)
        dtT, acs = part(SEQ), part(SEQ)
        dt_tok, acs_tok, te_tok, cd_tok = part(QT, 32), part(QT, 32), part(QT, 32), part(QT, 32)
        shared_end = cursor[0]
        att2 = part(KC, SEQ)
        fsel = [part(2, P), part(2, P)]
        fq = [part(QT, 2), part(QT, 2)]
        ub = [part(16 + SEQ), part(16 + SEQ)]
        level = [part(16 + SEQ), part(16 + SEQ)]
        pooled = [part(SEQ), part(SEQ)]
        cursor[0] = shared_end
        yT = part(16, SEQ)
        xdt, xde, hst = part(QT, SEQ), part(3, SEQ), part(3, SEQ)
        cin = [hst.rearrange("p a b -> p (a b)")[:, 515 * b:515 * b + 515] for b in range(2)]
        yg, xsT = abuf[:, 0:4, :], abuf[:, 4:8, :]
        seg, wgt, ea, bmT = sm, pr, abuf[:, 12, :], abuf[:, 13, :]
        cv = pr
        cmT = part(SEQ)
        btok, cbm = part(QT, P), part(QT, P)
        selh, selp = part(8, P), part(4, P)
        gpar = part(SP_N)
        dtg, acsg, teg, cdg = part(QT, 8), part(QT, 8), part(QT, 8), part(QT, 8)
        cursor[0] = shared_end
        moe = part(KC, SEQ)
        hid2 = part(4, SEQ)
        gw, gwT, gwb = part(QT, E_N), part(SEQ), [part(SEQ), part(SEQ)]
        esel = [part(P), part(P)]
        rt = [part(QT, E_N) for _ in range(8)]

        banks = ctx.enter_context(nc.psum_tensor("banks", [P, 8, SEQ], F32))[:, :, :]
        lin, aux = [banks[:, 0, :], banks[:, 1, :]], banks[:, 2, :]
        sc_b, pt_b, ob = [banks[:, 3, :], banks[:, 4, :]], [banks[:, 5, :], banks[:, 6, :]], banks[:, 7, :]

        def col(name, i=0, n=1):
            at = CST[name][0] + i
            return cst[:, at:at + n]

        def v1(name, i=0, n=1):
            at = VEC1[name][0] + i
            return vec[:, at:at + n]

        def v1d(name, i, n=1):
            return vec[:, ds(i + VEC1[name][0], n)]

        def v2(name, i=0, n=1):
            at = VEC2[name][0] + i
            return vec2[:, at:at + n]

        def v2d(name, i, n=1):
            return vec2[:, ds(i + VEC2[name][0], n)]

        ident, blockones, ones, rope, last = (col(n, 0, P) for n in ("ident", "blockones", "ones", "rope", "last"))
        adm, causal, tri = col("adm", 0, SEQ), col("causal", 0, SEQ), col("tri", 0, P)

        boot, c_in, vec_in, rel_in, out_done = (sem(n) for n in ("boot", "c_in", "vec_in", "rel_in", "out_done"))
        slot_full, slot_free = [sem("slot_full0"), sem("slot_full1")], [sem("slot_free0"), sem("slot_free1")]
        lin_full, lin_free = [sem("lin_full0"), sem("lin_full1")], [sem("lin_free0"), sem("lin_free1")]
        s_full, s_free = [sem("s_full0"), sem("s_full1")], [sem("s_free0"), sem("s_free1")]
        aux_full, aux_free, o_free = sem("aux_full"), sem("aux_free"), sem("o_free")

        def done(eng, name, n):
            eng.wait_ge(sem(name), n + 3)

        def free(eng, name, n):
            eng.wait_ge(sem(name), n + 1)

        def hold(eng):
            eng.sem_inc(sem("held"), 1)

        block = ctx.enter_context(nc.Block())

        @block.sync
        def _(sp):
            def stream(plan, stage, sizes, turn, layer, offset):
                for n, size in enumerate(sizes):
                    use = plan.at(stage, "slot", turn, layer) + n // 2
                    sp.wait_ge(slot_free[n % 2], use + 1)
                    src = w_all[ds(offset, size * P)].rearrange("(p n) -> p n", p=P)
                    sp.dma_start(ring[n % 2][:, 0:size], src).then_inc(slot_full[n % 2], 16)
                    offset = offset + size * P

            def run(plan, sizes_all, stages, layer, offset, loops):
                at = 0
                for stage, turns, inc in stages:
                    n = 2 * inc.get("slot", 0)
                    if not n:
                        continue
                    if stage in loops:
                        sizes = sizes_all[at:at + n]
                        with sp.Fori(0, turns) as i:
                            stream(plan, stage, sizes, i, layer, offset + i * (sum(sizes) * P))
                        offset = offset + turns * sum(sizes) * P
                        at += n * turns
                    else:
                        for i in range(turns):
                            sizes = sizes_all[at:at + n]
                            stream(plan, stage, sizes, i, layer, offset)
                            offset = offset + sum(sizes) * P
                            at += n
                assert at == len(sizes_all)

            with sp.Fori(0, LAYERS) as layer:
                run(LAYER, SLOTS_1, LAYER.stages, layer, layer * W1_TOTAL,
                    ("ada", "gates", "gu", "down"))
            run(SECOND, SLOTS_2, SECOND.stages, 0, LAYERS * W1_TOTAL,
                ("ada", "att", "attout", "ssd", "ssdout", "moe"))

        @block.tensor
        def _(pe):
            for name in ("t_done", "pv_done", "yd_done"):
                pe.sem_inc(sem(name), 2)

            def hk(k):
                return h[:, k, :]

            def slot_wait(p, use):
                pe.wait_ge(slot_full[p], (use + 1) * 16)

            def product(b, count, w, rhs, kc, m=P):
                pe.wait_ge(lin_free[b], count + 1)
                for k in range(kc):
                    mm = pe.matmul(lin[b][0:m, :], w(k), rhs(k), start=(k == 0), stop=(k == kc - 1))
                mm.then_inc(lin_full[b], 1)

            def packed(p, at, m=P):
                return lambda k: ring[p][:, at + k * m:at + (k + 1) * m]

            def wide(p, ct, n=512):
                return lambda k: ring[p][:, k * n + ct * P:k * n + (ct + 1) * P]

            def ada(plan, c0, i, layer):
                for b in range(2):
                    slot_wait(b, plan.at("ada", "slot", i, layer))
                    pe.wait_ge(lin_free[b], plan.at("ada", "lin", i, layer) + 1)
                    for ct in range(4):
                        for k in range(KC):
                            mm = pe.matmul(lin[b][:, ct:ct + 1], wide(b, ct)(k), csil[:, c0 + k:c0 + k + 1],
                                           start=(k == 0), stop=(k == KC - 1))
                    mm.then_inc(lin_full[b], 1)

            def column_sums(a, src, chunks):
                pe.wait_ge(aux_free, a + 1)
                for k in range(chunks):
                    mm = pe.matmul(aux, ones, src(k), start=(k == 0), stop=(k == chunks - 1))
                mm.then_inc(aux_full, 1)

            def aux_product(a, lhsT, rhs, m=P, n=SEQ):
                pe.wait_ge(aux_free, a + 1)
                pe.matmul(aux[0:m, 0:n], lhsT, rhs, start=True, stop=True).then_inc(aux_full, 1)

            def aux_transposes(a, src, rows, stride):
                pe.wait_ge(aux_free, a + 1)
                hold(pe)
                for t in range(QT):
                    mm = pe.transpose(aux[:, t * stride:t * stride + rows], src[0:rows, t * P:(t + 1) * P],
                                      ident[0:rows, 0:rows])
                mm.then_inc(aux_full, 1)

            def head_norm(a, n):
                pe.wait_ge(sem("sq_done"), n + 1)
                aux_product(a, blockones, sq)

            def rotate(a, src):
                aux_product(a, rope, src)

            def rotate_normed(a, n, dst):
                pe.wait_ge(sem("normed"), n + 1)
                rotate(a, dst)

            def scores(g, bank_use, q, k, w, extra=None):
                h2, i = divmod(g, QT)
                lo = HD * h2
                b = g % 2
                pe.wait_ge(s_free[b], bank_use + 1)
                mm = pe.matmul(sc_b[b][:, 0:w], q[lo:lo + HD, i * P:(i + 1) * P], k[lo:lo + HD, 0:w],
                               start=True, stop=extra is None)
                if extra is not None:
                    mm = pe.matmul(sc_b[b][:, 0:w], extra[0:16, h2, :], negF[0:16, 0:w], start=False, stop=True)
                mm.then_inc(s_full[b], 1)

            def attention(u, s, o, q, k, v, extra=None):
                def turn_over(g):
                    i = g % QT
                    done(pe, "pn_done", u + g)
                    free(pe, "pts_done", u + g)
                    for kt in range(i + 1):
                        mm = pe.transpose(pt_b[g % 2][:, kt * P:(kt + 1) * P], pr[g % 2][:, kt * P:(kt + 1) * P], ident)
                    mm.then_inc(sem("t_done"), 1)

                def values(g):
                    h2, i = divmod(g, QT)
                    done(pe, "pts_done", u + g)
                    if g == 0:
                        pe.wait_ge(o_free, o + 1)
                    for kt in range(i + 1):
                        mm = pe.matmul(ob[HD * h2:HD * h2 + HD, i * P:(i + 1) * P], v(kt, h2),
                                       pts[g % 2][:, kt * P:(kt + 1) * P], start=(kt == 0), stop=(kt == i))
                    mm.then_inc(sem("pv_done"), 1)

                for g in range(2):
                    scores(g, s + g // 2, q, k, P * (g % QT + 1), extra)
                for g in range(8):
                    turn_over(g)
                    if g + 2 < 8:
                        scores(g + 2, s + (g + 2) // 2, q, k, P * ((g + 2) % QT + 1), extra)
                    if g:
                        values(g - 1)
                values(7)

            pe.wait_ge(sem("c_ready"), 1)
            with pe.Fori(0, LAYERS) as layer:
                at = lambda stage, counter, turn=0: LAYER.at(stage, counter, turn, layer)
                with pe.Fori(0, 6) as i:
                    ada(LAYER, 0, i, layer)

                pe.wait_ge(sem("x_squared"), layer * 2 + 1)
                column_sums(at("norm1", "aux"), hk, KC)
                pe.wait_ge(sem("h_ready"), layer * 2 + 1)

                s, l, a, n = at("misc", "slot"), at("misc", "lin"), at("misc", "aux"), at("misc", "nrm")
                r = at("misc", "prep")
                slot_wait(0, s)
                product(0, l, packed(0, 0), hk, KC)
                product(1, l, packed(0, KC * P), hk, KC)
                head_norm(a, n)
                rotate_normed(a + 1, at("misc", "rope"), kaT)
                done(pe, "raw_done", r + 1)
                rotate(a + 2, raw[1])
                slot_wait(1, s)
                product(0, l + 1, packed(1, 0, HD), hk, KC, HD)
                product(1, l + 1, packed(1, KC * HD, 8), hk, KC, 8)
                done(pe, "raw_done", r + 2)
                aux_transposes(a + 3, raw[0], HD, HD)
                done(pe, "raw_done", r + 3)
                aux_transposes(a + 4, raw[1], 8, 8)

                for j in range(4):
                    b = j % 2
                    slot_wait(b, at("idx", "slot") + j // 2)
                    product(b, at("idx", "lin") + j // 2, packed(b, 0), hk, KC)
                    done(pe, "raw_done", at("idx", "prep") + j)
                    rotate(at("idx", "aux") + j, raw[b])
                    done(pe, "prep_done", at("idx", "prep") + j)
                    for g in range(6):
                        h2, i = g // 3, g % 3 + 1
                        pe.wait_ge(s_free[g % 2], at("idx", "s") + 3 * j + g // 2 + 1)
                        pe.matmul(sc_b[g % 2][:, 0:P * (i + 1)], qT[b][HD * h2:HD * h2 + HD, i * P:(i + 1) * P],
                                  kiT[HD * h2:HD * h2 + HD, 0:P * (i + 1)], start=True, stop=True)\
                            .then_inc(s_full[g % 2], 1)

                for j in range(4):
                    b = j % 2
                    slot_wait(b, at("A", "slot") + j // 2)
                    product(b, at("A", "lin") + j // 2, packed(b, 0), hk, KC)
                    head_norm(at("A", "aux") + 2 * j, at("A", "nrm") + j)
                    rotate_normed(at("A", "aux") + 2 * j + 1, at("A", "rope") + j, qT[b])
                    done(pe, "prep_done", at("A", "prep") + j)
                    attention(at("A", "u") + 8 * j, at("A", "s") + 4 * j, at("A", "o") + j, qT[b], kaT,
                              lambda kt, h2: va[:, kt, :])

                for j in range(4):
                    b = j % 2
                    slot_wait(b, at("B", "slot") + j // 2)
                    for n in range(3):
                        t = 3 * j + n
                        product(t % 2, at("B", "lin") + t // 2, packed(b, n * KC * P), hk, KC)
                    for n in range(2):
                        head_norm(at("B", "aux") + 3 * j + n, at("B", "nrm") + 2 * j + n)
                    t = 3 * j + 2
                    done(pe, "raw_done", at("B", "prep") + t)
                    aux_transposes(at("B", "aux") + t, raw[t % 2], P, P)
                    done(pe, "prep_done", at("B", "prep") + t)
                    attention(at("B", "u") + 8 * j, at("B", "s") + 4 * j, at("B", "o") + j, qT[b], kT[b],
                              lambda kt, h2: vtok[b][:, kt, HD * h2:HD * h2 + HD])

                pe.wait_ge(o_free, at("B", "o") + 5)
                hold(pe)
                with pe.Fori(0, 4) as i:
                    for p in range(2):
                        slot_wait(p, at("gates", "slot", i))
                        l = at("gates", "lin", i) + 2 * p
                        product(0, l, packed(p, 0), hk, KC)
                        product(1, l, packed(p, KC * P), hk, KC)
                        product(0, l + 1, packed(p, 2 * KC * P), lambda k: attA[:, k, :], 4)
                        product(1, l + 1, packed(p, 2 * KC * P + 4 * P), lambda k: attB[:, k, :], 4)
                pe.wait_ge(sem("merged_done"), layer + 1)
                for t in range(8):
                    if t % 4 == 0:
                        slot_wait(t // 4, at("out", "slot"))
                    product(t % 2, at("out", "lin") + t // 2, wide(t // 4, t % 4), lambda k: merged[:, k, :], KC)

                pe.wait_ge(sem("x_squared"), layer * 2 + 2)
                column_sums(at("norm2", "aux"), hk, KC)
                pe.wait_ge(sem("h_ready"), layer * 2 + 2)
                hold(pe)
                with pe.Fori(0, 11) as i:
                    for p in range(2):
                        slot_wait(p, at("gu", "slot", i))
                        product(0, at("gu", "lin", i) + p, packed(p, 0), hk, KC)
                        product(1, at("gu", "lin", i) + p, packed(p, KC * P), hk, KC)
                pe.wait_ge(sem("hid_done"), layer + 1)
                hold(pe)
                with pe.Fori(0, 4) as i:
                    for p in range(2):
                        slot_wait(p, at("down", "slot", i))
                        product(p, at("down", "lin", i), packed(p, 0), lambda k: hid[:, k, :], FF_T)

            at = lambda stage, counter, turn=0: SECOND.at(stage, counter, turn)
            H0 = 2 * LAYERS

            def layer_norm(stage, n):
                pe.wait_ge(sem("x_ready"), 5 + n)
                column_sums(at(stage, "aux"), lambda k: x[:, k, :], KC)
                pe.wait_ge(sem("centred_squared"), n + 1)
                column_sums(at(stage, "aux") + 1, lambda k: merged2[:, k, :], KC)

            with pe.Fori(0, 6) as i:
                ada(SECOND, 8, i, 0)
            layer_norm("ln1", 0)
            pe.wait_ge(sem("h_ready"), H0 + 1)

            slot_wait(0, at("fd", "slot"))
            product(0, at("fd", "lin"), packed(0, 0, 16), hk, KC, 16)
            slot_wait(1, at("fd", "slot"))
            product(1, at("fd", "lin"), packed(1, 0, 32), hk, KC, 32)
            pe.wait_ge(sem("f_done"), 1)
            aux_transposes(at("fd", "aux"), negF, 16, 16)
            pe.wait_ge(sem("acs_done"), 1)
            aux_transposes(at("fd", "aux") + 1, dtT, 32, 32)
            aux_transposes(at("fd", "aux") + 2, acs, 32, 32)
            pe.wait_ge(sem("acs_tok_done"), 1)
            aux_product(at("fd", "aux") + 3, last, acs_tok.rearrange("p a b -> p (a b)"), P, QT * 32)

            with pe.Fori(0, 4) as i:
                for b in range(2):
                    slot_wait(b, at("att", "slot", i))
                    for n in range(3):
                        t = 3 * b + n
                        product(t % 2, at("att", "lin", i) + t // 2, packed(b, n * KC * P), hk, KC)
                    t = 3 * b + 2
                    done(pe, "raw_done", at("att", "prep", i) + t)
                    aux_transposes(at("att", "aux", i) + b, raw[t % 2], P, P)
                    done(pe, "prep_done", at("att", "prep", i) + t)
                    attention(at("att", "u", i) + 8 * b, at("att", "s", i) + 4 * b, at("att", "o", i) + b,
                              qT[b], kT[b], lambda kt, h2: vtok[b][:, kt, HD * h2:HD * h2 + HD], fsel[b])
            pe.wait_ge(o_free, at("att", "o") + 9)
            with pe.Fori(0, 4) as i:
                for p in range(2):
                    slot_wait(p, at("attout", "slot", i))
                    product(0, at("attout", "lin", i) + p, packed(p, 0), hk, KC)
                    product(1, at("attout", "lin", i) + p, packed(p, KC * P), lambda k: att2[:, k, :], KC)

            for g in range(4):
                l = at("pool", "lin", g)
                slot_wait(0, at("pool", "slot", g))
                product(0, l, wide(0, 0, 256), hk, KC)
                product(1, l, wide(0, 1, 256), hk, KC)
                slot_wait(1, at("pool", "slot", g))
                product(0, l + 1, wide(1, 0, 256), hk, KC)
                pe.wait_ge(sem("pooled_done"), g + 1)
                wp = lambda ct: (lambda k: ring[1][:, KC * 256 + k * 256 + ct * P:KC * 256 + k * 256 + (ct + 1) * P])
                product(1, l + 1, wp(0), lambda k: pooled[k], 2)
                product(0, l + 2, wide(1, 1, 256), hk, KC)
                product(1, l + 2, wp(1), lambda k: pooled[k], 2)

            with pe.Fori(0, 4) as i:
                l, s = at("ssd", "lin", i), at("ssd", "slot", i)
                slot_wait(0, s)
                for t in range(4):
                    product(t % 2, l + t // 2, wide(0, t), hk, KC)
                slot_wait(1, s)
                for t in range(2):
                    product(t, l + 2, wide(1, t, 256), hk, KC)
                done(pe, "silu_done", i * 6 + 3)
                for c in range(QT):
                    free(pe, "xd_done", i * 4 + c)
                    for t in range(4):
                        mm = pe.transpose(pt_b[c % 2][:, t * P:(t + 1) * P], xsT[:, t, c * P:(c + 1) * P], ident)
                    mm.then_inc(sem("xt_done"), 1)
                done(pe, "silu_done", i * 6 + 5)
                pe.wait_ge(sem("yp_done"), i * 4 + 1)
                for c in range(QT):
                    mm = pe.transpose(ob[:, c * P:(c + 1) * P], bmT[:, c * P:(c + 1) * P], ident)
                mm.then_inc(sem("bt_done"), 1)
                done(pe, "seg_done", i * 8 - 1)
                for c in range(QT):
                    mm = pe.matmul(sc_b[0][:, c * P:(c + 1) * P], bmT[:, c * P:(c + 1) * P],
                                   cmT[:, c * P:(c + 1) * P], start=True, stop=True)
                mm.then_inc(sem("cb_done"), 1)
                pe.wait_ge(sem("btok_done"), i + 1)
                done(pe, "xd_done", i * 4 + 3)
                for c in range(3):
                    if c == 2:
                        pe.wait_ge(sem("hst_done"), i * 3 + 1)
                    pe.matmul(pt_b[c % 2], btok[:, c, :], xde[:, c, :], start=True, stop=True)\
                        .then_inc(sem("st_done"), 1)
                pe.wait_ge(sem("cbm_done"), i + 1)

                def decay_row(hh):
                    free(pe, "seg_done", i * 8 + hh)
                    pe.matmul(sc_b[hh % 2], selh[0:32, hh, :], acs[0:32, :], start=True, stop=True)\
                        .then_inc(sem("bc_done"), 1)

                decay_row(0)
                decay_row(1)
                pe.wait_ge(sem("hst_done"), i * 3 + 3)
                for j in range(4):
                    pe.wait_ge(sem("yp_done"), i * 4 + j + 1)
                    pe.matmul(pt_b[1], selp[0:32, j, :], acs[0:32, :], start=True, stop=True)\
                        .then_inc(sem("eab_done"), 1)
                    for h2 in range(2):
                        for c in range(3):
                            mm = pe.matmul(pt_b[0][HD * h2:HD * h2 + HD, (c + 1) * P:(c + 2) * P],
                                           hst[:, c, (2 * j + h2) * HD:(2 * j + h2 + 1) * HD],
                                           cmT[:, (c + 1) * P:(c + 2) * P], start=True, stop=True)
                    mm.then_inc(sem("yoff_done"), 1)
                    for h2 in range(2):
                        hh = 2 * j + h2
                        done(pe, "wgt_done", i * 8 + hh)
                        for c in range(QT):
                            mm = pe.matmul(ob[HD * h2:HD * h2 + HD, c * P:(c + 1) * P],
                                           xdt[:, c, hh * HD:(hh + 1) * HD], wgt[hh % 2][:, c * P:(c + 1) * P],
                                           start=True, stop=True)
                        mm.then_inc(sem("yd_done"), 1)
                        if hh + 2 < 8:
                            decay_row(hh + 2)
                slot_wait(0, s + 1)
                for t in range(2):
                    product(t, l + 3, wide(0, t, 256), hk, KC)
                slot_wait(1, s + 1)
                for t in range(2):
                    product(t, l + 4, wide(1, t, 256), hk, KC)
                pe.wait_ge(sem("yg_squared"), i + 1)
                column_sums(at("ssd", "aux", i), lambda k: xdt[:, k, :], 4)

            pe.wait_ge(sem("yT_done"), 4)
            with pe.Fori(0, 4) as i:
                for p in range(2):
                    slot_wait(p, at("ssdout", "slot", i))
                    product(0, at("ssdout", "lin", i) + p, packed(p, 0), hk, KC)
                    product(1, at("ssdout", "lin", i) + p, packed(p, KC * P), lambda k: yT[:, k, :], 16)
            pe.wait_ge(sem("merged2_done"), 1)
            for t in range(8):
                if t % 4 == 0:
                    slot_wait(t // 4, at("out", "slot"))
                product(t % 2, at("out", "lin") + t // 2, wide(t // 4, t % 4), lambda k: merged2[:, k, :], KC)
            layer_norm("ln2", 1)
            layer_norm("ln3", 2)
            pe.wait_ge(sem("h_ready"), H0 + 2)

            pe.wait_ge(aux_free, at("router", "aux") + 1)
            for t in range(QT):
                for k in range(KC):
                    mm = pe.matmul(aux[:, t * E_N:(t + 1) * E_N], h[:, k, t * P:(t + 1) * P],
                                   v2("w_router", k * E_N, E_N), start=(k == 0), stop=(k == KC - 1))
            mm.then_inc(aux_full, 1)
            pe.wait_ge(sem("gw_done"), 1)
            pe.wait_ge(aux_free, at("router", "aux") + 2)
            for t in range(QT):
                mm = pe.transpose(aux[0:E_N, t * P:(t + 1) * P], gw[:, t, :], ident)
            mm.then_inc(aux_full, 1)
            pe.wait_ge(sem("gwT_done"), 1)

            with pe.Fori(0, 8) as i:
                for ex in range(2):
                    s, l = at("moe", "slot", i), at("moe", "lin", i) + 8 * ex
                    n0 = 3 * ex
                    pg, pu, pd = n0 % 2, (n0 + 1) % 2, n0 % 2
                    pe.wait_ge(sem("esel_done"), i * 2 + ex + 1)
                    aux_product(at("moe", "aux", i) + ex, esel[ex][0:E_N, :], gwT[0:E_N, :])
                    slot_wait(pg, s + n0 // 2)
                    for t in range(4):
                        product(0, l + t, wide(pg, t), hk, KC)
                        if t == 0:
                            slot_wait(pu, s + (n0 + 1) // 2)
                        product(1, l + t, wide(pu, t), hk, KC)
                    slot_wait(pd, s + (n0 + 2) // 2)
                    pe.wait_ge(sem("hidw_done"), i * 8 + 4 * ex + 5)
                    for t in range(8):
                        product(t % 2, l + 4 + t // 2,
                                lambda k: ring[pd][:, k * D + t * P:k * D + (t + 1) * P], lambda k: hid2[:, k, :], 4)
            layer_norm("ln4", 3)

        @block.scalar
        def _(act):
            mine = Steps(act, sem("act_steps"))
            tell = mine.tell
            for dst, src in ((cst[:, :], consts), (csil[:, :], cond), (raw[0].bitcast(I32), pos_in),
                             (x[:, :, :], x_in), (vec2[:, :], vec2_all)):
                act.dma_start(dst, src).then_inc(boot, 16)
            for s in (slot_free[0], slot_free[1], o_free):
                act.sem_inc(s, 1)
            for name in ("exp_done", "pts_done", "raw_done", "rl_done", "silu_done"):
                act.sem_inc(sem(name), 2)

            act.wait_ge(boot, 80)
            tell(act.activation(csil[:, :], csil[:, :], ACT.Silu), sem("c_ready"))
            act.wait_ge(sem("angle_done"), 1)
            mine(act.activation(sinT[:, :], tmp[:, :], ACT.Sin))
            tell(act.activation(cosT[:, :], tmp[:, :], ACT.Sin, scale=0.5), sem("sin_done"))

            def root(out, scale, eps, a):
                act.wait_ge(aux_full, a + 1)
                tell(act.activation(out, aux, ACT.Sqrt, scale=scale, bias=eps), sem("root_done"))

            def affine(dst, scaled, scale, shift, signal):
                for k in range(KC):
                    act.wait_ge(sem("scaled"), scaled + k + 1)
                    mine(act.activation(dst[:, k, :], dst[:, k, :], ACT.Identity, scale=scale(k), bias=shift(k)))
                act.sem_inc(signal, 1)

            def rms_norm(n, a, gain0, shift0):
                act.wait_ge(sem("x_ready"), n + 1)
                for half in range(2):
                    mine(act.activation(h[:, 4 * half:4 * half + 4, :], x[:, 4 * half:4 * half + 4, :], ACT.Square))
                act.sem_inc(sem("x_squared"), 1)
                root(rstd[:, :], 1.0 / D, EPS, a)
                affine(h, n * KC, lambda k: gain[:, gain0 + k:gain0 + k + 1],
                       lambda k: mod[:, shift0 + k:shift0 + k + 1], sem("h_ready"))

            def take_tile(b, count, slot=None):
                act.wait_ge(lin_full[b], count + 1)
                if slot is not None:
                    act.sem_inc(slot_free[slot], 1)

            def project(b, count, r, par, bias, m=P, slot=None, dst=None, scale=1.0):
                take_tile(b, count, slot)
                free(act, "prep_done", r)
                dst = raw[par] if dst is None else dst
                tell(act.activation(dst[0:m, :], lin[b][0:m, :], ACT.Identity, bias=bias, scale=scale), sem("raw_done"))

            def head_root(a):
                act.wait_ge(aux_full, a + 1)
                tell(act.activation(rs[:, :], aux, ACT.Sqrt, scale=1.0 / HD, bias=EPS), sem("rs_done"))

            def attention(u, dst):
                def evacuate(g):
                    w = P * (g % QT + 1)
                    done(act, "t_done", u + g)
                    free(act, "pv_done", u + g)
                    tell(act.activation(pts[g % 2][:, 0:w], pt_b[g % 2][:, 0:w], ACT.Copy), sem("pts_done"))

                for g in range(8):
                    w = P * (g % QT + 1)
                    done(act, "nmax_done", u + g)
                    free(act, "t_done", u + g)
                    tell(act.activation(pr[g % 2][:, 0:w], sm[g % 2][:, 0:w], ACT.Exp, bias=nmax[:, g:g + 1],
                                   accum_out=esum[:, g:g + 1]), sem("exp_done"))
                    if g:
                        evacuate(g - 1)
                evacuate(7)
                done(act, "pv_done", u + 7)
                tell(act.activation(dst, ob, ACT.Copy), o_free)

            def gate(b, count, n, par, func, bias=0.0, slot=None):
                take_tile(b, count, slot)
                act.wait_ge(sem("sg_free"), n + 1)
                tell(act.activation(sg[par][:, :], lin[b], func, bias=bias), sem("sg_done"))

            with mine.loop(0, LAYERS) as layer:
                at = lambda stage, counter, turn=0: LAYER.at(stage, counter, turn, layer)
                act.dma_start(vec[:, :], vec1_all[ds(layer * (P * NV1), P * NV1)].rearrange("(p n) -> p n", p=P))\
                    .then_inc(vec_in, 16)
                act.dma_start(relb, rel[ds(layer * (P * 8 * SEQ), P * 8 * SEQ)]
                              .rearrange("(p a b) -> p a b", p=P, a=8)).then_inc(rel_in, 16)
                act.wait_ge(vec_in, layer * 16 + 16)
                rms_norm(layer * 2, at("norm1", "aux"), 0, 0)

                l, r = at("misc", "lin"), at("misc", "prep")
                project(0, l, r, 0, v1("ka"))
                project(1, l, r + 1, 1, v1("ki"), slot=0)
                head_root(at("misc", "aux"))
                project(0, l + 1, r + 2, 0, v1("va")[0:HD], HD)
                project(1, l + 1, r + 3, 1, v1("wi")[0:8], 8, slot=1)

                for j in range(4):
                    b = j % 2
                    project(b, at("idx", "lin") + j // 2, at("idx", "prep") + j, b, v1("qi", j), slot=b)
                    for g in range(6):
                        w = P * (g % 3 + 2)
                        act.wait_ge(s_full[g % 2], at("idx", "s") + 3 * j + g // 2 + 1)
                        free(act, "acc_done", at("idx", "iu") + 6 * j + g)
                        tell(act.activation(sm[g % 2][:, 0:w], sc_b[g % 2][:, 0:w], ACT.Relu), sem("rl_done"))

                for j in range(4):
                    b = j % 2
                    project(b, at("A", "lin") + j // 2, at("A", "prep") + j, b, v1("qa", j), slot=b)
                    head_root(at("A", "aux") + 2 * j)
                    attention(at("A", "u") + 8 * j, attA[:, j, :])

                for j in range(4):
                    l, r = at("B", "lin"), at("B", "prep")
                    t = 3 * j
                    project(t % 2, l + t // 2, r + t, t % 2, v1("qb", j))
                    project((t + 1) % 2, l + (t + 1) // 2, r + t + 1, (t + 1) % 2, v1("kb", j))
                    head_root(at("B", "aux") + t)
                    head_root(at("B", "aux") + t + 1)
                    project(t % 2, l + (t + 2) // 2, r + t + 2, t % 2, v1("vb", j), slot=j % 2)
                    attention(at("B", "u") + 8 * j, attB[:, j, :])

                with mine.loop(0, 4) as i:
                    for p in range(2):
                        l, n = at("gates", "lin", i) + 2 * p, at("gates", "sg", i) + 2 * p
                        gate(0, l, n, 0, ACT.Sigmoid, v1d("ga", 2 * i + p))
                        gate(1, l, n + 1, 1, ACT.Sigmoid, v1d("gb", 2 * i + p))
                rms_norm(layer * 2 + 1, at("norm2", "aux"), 8, 24)
                with mine.loop(0, 11) as i:
                    for p in range(2):
                        gate(0, at("gu", "lin", i) + p, at("gu", "sg", i) + p, p, ACT.Silu)

            at = lambda stage, counter, turn=0: SECOND.at(stage, counter, turn)
            SC0 = 2 * LAYERS * KC

            def layer_norm(stage, n, dst, scale, shift, signal):
                act.wait_ge(sem("centred"), n + 1)
                tell(act.activation(merged2, dst[:, :, :], ACT.Square), sem("centred_squared"))
                root(rstd[:, :], 1.0 / D, LN_EPS, at(stage, "aux") + 1)
                affine(dst, SC0 + n * KC, scale, shift, signal)

            mod_at = lambda k0: (lambda k: mod[:, k0 + k:k0 + k + 1])
            gain_at = lambda k0: (lambda k: gain[:, k0 + k:k0 + k + 1])
            v2_at = lambda name: (lambda k: v2(name, k))
            layer_norm("ln1", 0, h, gain_at(0), mod_at(0), sem("h_ready"))

            for n, (m, bias) in enumerate(((16, v2("b_forget")[0:16]), (32, v2("dt_bias")[0:32]))):
                take_tile(n, at("fd", "lin"), slot=n)
                tell(act.activation(raw[n][0:m, :], lin[n][0:m, :], ACT.Identity, bias=bias), sem("fd_raw"))
                act.wait_ge(sem("fd_raw"), n + 1)
                tell(act.activation(sm[n][0:m, :], raw[n][0:m, :], ACT.Abs), sem("fd_act"))
                act.wait_ge(sem("fd_act"), 3 * n + 1)
                tell(act.activation(sm[n][0:m, :], sm[n][0:m, :], ACT.Exp, scale=-1.0), sem("fd_act"))
                act.wait_ge(sem("fd_act"), 3 * n + 2)
                tell(act.activation(sm[n][0:m, :], sm[n][0:m, :], ACT.Ln, bias=1.0), sem("fd_act"))
            tell(act.activation(gain[0:32, 0:1], v2("a_log")[0:32], ACT.Exp), sem("a_done"))
            act.wait_ge(aux_full, at("fd", "aux") + 4)
            tell(act.activation(cd_tok.rearrange("p a b -> p (a b)"), aux[:, 0:QT * 32], ACT.Exp), sem("cd_done"))
            act.wait_ge(sem("te_diff"), 1)
            tell(act.activation(te_tok, te_tok, ACT.Exp), sem("te_exp"))

            with mine.loop(0, 4) as i:
                for b in range(2):
                    l, r = at("att", "lin", i), at("att", "prep", i) + 3 * b
                    for n, dst in enumerate((qT[b], kT[b], raw[b])):
                        t = 3 * b + n
                        project(t % 2, l + t // 2, r + n, b, 0.0, slot=b if n == 2 else None, dst=dst,
                                scale=HD ** -0.5 if n == 0 else 1.0)
                    attention(at("att", "u", i) + 8 * b, att2[:, ds(2 * i + b, 1), :])
            with mine.loop(0, 4) as i:
                for p in range(2):
                    gate(0, at("attout", "lin", i) + p, at("attout", "sg", i) + p, p, ACT.Sigmoid)
            for g in range(4):
                l = at("pool", "lin", g)
                for t in range(2):
                    take_tile(t, l, slot=0 if t == 1 else None)
                    act.wait_ge(sem("ub_free"), 2 * g + t + 1)
                    tell(act.activation(ub[t][:, 16:16 + SEQ], lin[t], ACT.Copy), sem("ub_done"))
                gate(0, l + 1, at("pool", "sg", g), 0, ACT.Sigmoid)
                gate(0, l + 2, at("pool", "sg", g) + 1, 1, ACT.Sigmoid)

            with mine.loop(0, 4) as i:
                l = at("ssd", "lin", i)

                def conv_in(t):
                    take_tile(t % 2, l + t // 2, slot={3: 0, 5: 1}.get(t))
                    free(act, "conv_done", i * 6 + t)
                    tell(act.activation(cin[t % 2][:, 3:], lin[t % 2], ACT.Copy), sem("cin_done"))

                def conv_out(t):
                    done(act, "conv_done", i * 6 + t)
                    dst = xsT[:, t, :] if t < 4 else (bmT, cmT)[t - 4]
                    tell(act.activation(dst, cv[t % 2], ACT.Silu, bias=gpar[:, 5 * t + 4:5 * t + 5]), sem("silu_done"))

                act.wait_ge(sem("gpar_done"), i + 1)
                for t in range(6):
                    conv_in(t)
                    if t:
                        conv_out(t - 1)
                conv_out(5)
                for j in range(4):
                    act.wait_ge(sem("eab_done"), i * 4 + j + 1)
                    act.wait_ge(sem("yp_done"), i * 4 + j + 1)
                    tell(act.activation(ea, pt_b[1], ACT.Exp), sem("ea_done"))
                    for hh in (2 * j, 2 * j + 1):
                        done(act, "seg_done", i * 8 + hh)
                        tell(act.activation(seg[hh % 2], seg[hh % 2], ACT.Exp), sem("e_done"))
                for t in range(4):
                    gate(t % 2, l + 3 + t // 2, at("ssd", "sg", i) + t, t % 2, ACT.Silu,
                         slot={1: 0, 3: 1}.get(t))
                act.wait_ge(sem("yz_done"), i + 1)
                tell(act.activation(xdt, yg, ACT.Square), sem("yg_squared"))
                root(rstd[:, :], 1.0 / SEQ, EPS, at("ssd", "aux", i))
            with mine.loop(0, 4) as i:
                for p in range(2):
                    gate(0, at("ssdout", "lin", i) + p, at("ssdout", "sg", i) + p, p, ACT.Sigmoid)

            layer_norm("ln2", 1, x, v2_at("ln_mix_g"), v2_at("ln_mix_b"), sem("x_ready"))
            layer_norm("ln3", 2, h, gain_at(8), mod_at(24), sem("h_ready"))
            act.wait_ge(sem("logit_done"), 1)
            tell(act.activation(rt[0], rt[0], ACT.Exp), sem("probs_exp"))
            act.wait_ge(aux_full, at("router", "aux") + 2)
            tell(act.activation(gwT[0:E_N, :], aux[0:E_N, :], ACT.Copy), sem("gwT_done"))
            act.wait_ge(sem("gwT_done"), 1)
            act.sem_inc(aux_free, 1)
            with mine.loop(0, 8) as i:
                for ex in range(2):
                    l, n = at("moe", "lin", i) + 8 * ex, at("moe", "sg", i) + 4 * ex
                    act.wait_ge(aux_full, at("moe", "aux", i) + ex + 1)
                    act.wait_ge(sem("hidw_done"), i * 8 + 4 * ex + 1)
                    tell(act.activation(gwb[ex], aux, ACT.Copy), sem("gwb_done"))
                    for t in range(4):
                        gate(0, l + t, n + t, t % 2, ACT.Silu, slot=(3 * ex) % 2 if t == 3 else None)
            layer_norm("ln4", 3, x, v2_at("ln_ffn_g"), v2_at("ln_ffn_b"), sem("x_final"))
            act.wait_ge(sem("x_final"), 1)
            act.dma_start(out, x[:, :, :]).then_inc(out_done, 16)
            act.wait_ge(out_done, 16)

        @block.vector
        def _(dve):
            mine = Steps(dve, sem("dve_steps"))
            tell = mine.tell
            TT, TS, STT = dve.tensor_tensor, dve.tensor_scalar, dve.scalar_tensor_tensor
            MUL, ADD, SUB, MAX, MIN = ALU.mult, ALU.add, ALU.subtract, ALU.max, ALU.min

            for s in (lin_free[0], lin_free[1], aux_free, s_free[0], s_free[1], sem("yp_done")):
                dve.sem_inc(s, 1)
            for name in ("nmax_done", "prep_done", "acc_done", "conv_done", "seg_done", "xd_done", "sg_free",
                         "ub_free"):
                dve.sem_inc(sem(name), 2)

            TWO_PI = 2 * np.pi
            c1 = 6.28125
            c2 = float(np.float32(np.round((TWO_PI - c1) * 2 ** 20) / 2 ** 20))
            c3 = float(TWO_PI - c1 - c2)
            MAGIC = 1.5 * 2 ** 23
            ang, turns = sm[0], sm[1]
            dve.wait_ge(boot, 80)
            dve.sem_inc(sem("x_ready"), 1)
            mine(dve.tensor_copy(ang, raw[0].bitcast(I32)))
            mine(TS(ang, ang, col("inv_freq"), None, MUL))
            mine(TS(turns, ang, 1 / TWO_PI, MAGIC, MUL, ADD))
            mine(TS(turns, turns, MAGIC, None, SUB))
            for c in (c1, c2, c3):
                mine(STT(ang, turns, -c, ang, MUL, ADD))
            PI = 3.1415925
            tell(TS(tmp[:, :], ang, PI, -PI, MIN, MAX), sem("angle_done"))
            dve.wait_ge(sem("sin_done"), 1)
            mine(TT(cosT[:, :], cosT[:, :], cosT[:, :], MUL))
            mine(TS(cosT[:, :], cosT[:, :], -2.0, 1.0, MUL, ADD))
            mine.restart()

            def lin_wait(b, count):
                dve.wait_ge(lin_full[b], count + 1)

            def ada(plan, bias, i, layer):
                for b in range(2):
                    lin_wait(b, plan.at("ada", "lin", i, layer))
                    dve.sem_inc(slot_free[b], 1)
                    k0 = 8 * i + 4 * b
                    tell(TT(mod[:, ds(k0, 4)], lin[b][:, 0:4], bias("b_ada", k0, 4), ADD), lin_free[b])

            def gains(g_mix, g_ffn, signal, lin_counts):
                for b in range(2):
                    dve.wait_ge(lin_free[b], lin_counts + 1)
                for at0, k0, g in ((0, 8, g_mix), (8, 32, g_ffn)):
                    if g is None:
                        ins = TS(gain[:, at0:at0 + 8], mod[:, k0:k0 + 8], 1.0, None, ADD)
                    else:
                        ins = STT(gain[:, at0:at0 + 8], mod[:, k0:k0 + 8], 1.0, g, ADD, MUL)
                    mine(ins)

            def scale_tiles(dst, src, n_root, n_aux_free=True):
                dve.wait_ge(sem("root_done"), n_root + 1)
                tell(dve.reciprocal(rstd[:, :], rstd[:, :]), aux_free)

            def rms_norm(n, a, n_root):
                dve.wait_ge(sem("root_done"), n_root + 1)
                tell(dve.reciprocal(rstd[:, :], rstd[:, :]), aux_free)
                dve.wait_ge(aux_free, a + 2)
                for k in range(KC):
                    tell(TT(h[:, k, :], x[:, k, :], rstd[:, :], MUL), sem("scaled"))

            def layer_norm(stage, n, dst, n_root):
                a = SECOND.at(stage, "aux")
                dve.wait_ge(aux_full, a + 1)
                tell(TS(tmp[:, :], aux, 1.0 / D, None, MUL), aux_free)
                dve.wait_ge(aux_free, a + 2)
                tell(TT(dst[:, :, :], x[:, :, :], tmp[:, :].unsqueeze(1).broadcast_to([P, KC, SEQ]), SUB), sem("centred"))
                dve.wait_ge(sem("root_done"), n_root + 1)
                tell(dve.reciprocal(rstd[:, :], rstd[:, :]), aux_free)
                dve.wait_ge(aux_free, a + 3)
                for k in range(KC):
                    tell(TT(dst[:, k, :], dst[:, k, :], rstd[:, :], MUL), sem("scaled"))

            def norm_tile(a, n, r, par, b, count, dst, g, final):
                done(dve, "raw_done", r)
                dve.sem_inc(lin_free[b], 1)
                tell(TT(sq[:, :], raw[par], raw[par], MUL), sem("sq_done"))

            def norm_tile_end(a, n, par, dst, g, signal):
                dve.wait_ge(sem("rs_done"), n + 1)
                tell(dve.reciprocal(rs[:, :], rs[:, :]), aux_free)
                dve.wait_ge(aux_free, a + 2)
                tell(STT(dst, raw[par], g, rs[:, :], MUL, MUL), signal)

            def rotate(a, src, dst):
                dve.wait_ge(aux_full, a + 1)
                tell(TT(tmp[:, :], aux, sinT[:, :], MUL), aux_free)
                mine(TT(dst, src, cosT[:, :], MUL))
                dve.wait_ge(aux_free, a + 2)
                tell(TT(dst, dst, tmp[:, :], ADD), sem("prep_done"))

            def take_transposed(a, dst, src):
                dve.wait_ge(aux_full, a + 1)
                tell(dve.tensor_copy(dst, src), aux_free)
                dve.wait_ge(aux_free, a + 2)
                dve.sem_inc(sem("prep_done"), 1)

            def attention(u, s, masked):
                def reciprocal(g):
                    done(dve, "exp_done", u + g)
                    tell(dve.reciprocal(rcp[:, g:g + 1], esum[:, g:g + 1]), sem("rcp_done"))

                for g in range(8):
                    b, w = g % 2, P * (g % QT + 1)
                    dve.wait_ge(s_full[b], s + g // 2 + 1)
                    free(dve, "exp_done", u + g)
                    tell(masked(g, b, w), s_free[b])
                    dve.wait_ge(s_free[b], s + g // 2 + 2)
                    tell(dve.tensor_reduce(nmax[:, g:g + 1], sm[b][:, 0:w], AX.X, MAX, negate=True), sem("nmax_done"))
                    if g:
                        reciprocal(g - 1)
                reciprocal(7)

            with mine.loop(0, LAYERS) as layer:
                at = lambda stage, counter, turn=0: LAYER.at(stage, counter, turn, layer)
                dve.wait_ge(vec_in, layer * 16 + 16)
                hold(dve)
                with mine.loop(0, 6) as i:
                    ada(LAYER, v1d, i, layer)
                gains(v1("g_mix", 0, 8), v1("g_ffn", 0, 8), None, at("norm1", "lin"))
                rms_norm(layer * 2, at("norm1", "aux"), layer * 2)
                dve.wait_ge(rel_in, layer * 16 + 16)
                mine(dve.memset(relb[0:HD, :, SEQ - HD:SEQ], NEG))

                a, r = at("misc", "aux"), at("misc", "prep")
                done(dve, "raw_done", r)
                dve.sem_inc(lin_free[0], 1)
                tell(TT(sq[:, :], raw[0], raw[0], MUL), sem("sq_done"))
                norm_tile_end(a, at("misc", "nrm"), 0, kaT, v1("kn_a"), sem("normed"))
                dve.wait_ge(sem("normed"), at("misc", "rope") + 1)
                rotate(a + 1, kaT, kaT)
                done(dve, "raw_done", r + 1)
                dve.sem_inc(lin_free[1], 1)
                rotate(a + 2, raw[1], kiT)
                done(dve, "raw_done", r + 2)
                dve.sem_inc(lin_free[0], 1)
                take_transposed(a + 3, va, aux[:, 0:QT * HD].rearrange("p (a b) -> p a b", b=HD))
                done(dve, "raw_done", r + 3)
                dve.sem_inc(lin_free[1], 1)
                take_transposed(a + 4, wtok, aux[:, 0:QT * 8].rearrange("p (a b) -> p a b", b=8))

                for j in range(4):
                    b = j % 2
                    done(dve, "raw_done", at("idx", "prep") + j)
                    dve.sem_inc(lin_free[b], 1)
                    rotate(at("idx", "aux") + j, raw[b], qT[b])
                    for g in range(6):
                        h2, i = g // 3, g % 3 + 1
                        w = P * (i + 1)
                        n = at("idx", "iu") + 6 * j + g
                        done(dve, "rl_done", n)
                        dve.sem_inc(s_free[g % 2], 1)
                        weight = wtok[:, i, 2 * j + h2:2 * j + h2 + 1]
                        if j == 0 and h2 == 0:
                            ins = TS(score[:, i, 0:w], sm[g % 2][:, 0:w], weight, None, MUL)
                        else:
                            done(dve, "acc_done", n - 3)
                            ins = STT(score[:, i, 0:w], sm[g % 2][:, 0:w], weight, score[:, i, 0:w], MUL, ADD)
                        tell(ins, sem("acc_done"))
                done(dve, "acc_done", at("idx", "iu") + 23)
                mine(dve.tensor_copy(mask[:, 0, 0:P], adm[:, SEQ - P:SEQ]))
                for i in range(1, QT):
                    w = P * (i + 1)
                    mine(STT(score[:, i, 0:w], score[:, i, 0:w], IDX_SCALE, adm[:, SEQ - w:SEQ], MUL, ADD))
                mine.restart()
                for i in range(1, QT):
                    w = P * (i + 1)
                    with mine.loop(0, TOP_K // 8) as _round:
                        mine(dve.max(top8, score[:, i, 0:w]))
                        mine(dve.match_replace(score[:, i, 0:w], top8, score[:, i, 0:w], TAKEN))
                        mine.restart()
                    mine(TS(mask[:, i, 0:w], score[:, i, 0:w], 0.5 * TAKEN, NEG, ALU.is_gt, MUL))
                    mine.restart()

                for j in range(4):
                    b, a = j % 2, at("A", "aux") + 2 * j
                    done(dve, "raw_done", at("A", "prep") + j)
                    dve.sem_inc(lin_free[b], 1)
                    tell(TT(sq[:, :], raw[b], raw[b], MUL), sem("sq_done"))
                    norm_tile_end(a, at("A", "nrm") + j, b, qT[b], v1("qn_a"), sem("normed"))
                    dve.wait_ge(sem("normed"), at("A", "rope") + j + 1)
                    rotate(a + 1, qT[b], qT[b])
                    attention(at("A", "u") + 8 * j, at("A", "s") + 4 * j,
                              lambda g, b, w: STT(sm[b][:, 0:w], sc_b[b][:, 0:w], HD ** -0.5,
                                                  mask[:, g % QT, 0:w], MUL, ADD))
                for j in range(4):
                    b, a, r = j % 2, at("B", "aux") + 3 * j, at("B", "prep") + 3 * j
                    for n, (dst, g) in enumerate(((qT[b], v1("qn_b")), (kT[b], v1("kn_b")))):
                        t = 3 * j + n
                        done(dve, "raw_done", r + n)
                        dve.sem_inc(lin_free[t % 2], 1)
                        tell(TT(sq[:, :], raw[t % 2], raw[t % 2], MUL), sem("sq_done"))
                        norm_tile_end(a + n, at("B", "nrm") + 2 * j + n, t % 2, dst, g, sem("prep_done"))
                    t = 3 * j + 2
                    done(dve, "raw_done", r + 2)
                    dve.sem_inc(lin_free[t % 2], 1)
                    take_transposed(a + 2, vtok[b], aux.rearrange("p (a b) -> p a b", b=P))
                    attention(at("B", "u") + 8 * j, at("B", "s") + 4 * j,
                              lambda g, b, w: STT(sm[b][:, 0:w], sc_b[b][:, 0:w], HD ** -0.5,
                                                  relb[:, 2 * j + g // QT, SEQ - w:SEQ], MUL, ADD))

                mine.restart()
                with mine.loop(0, 4) as i:
                    for p in range(2):
                        l, n = at("gates", "lin", i) + 2 * p, at("gates", "sg", i) + 2 * p
                        for b in range(2):
                            dve.wait_ge(sem("sg_done"), n + b + 1)
                            dve.sem_inc(lin_free[b], 1)
                        lin_wait(0, l + 1)
                        tell(TT(tmp[:, :], sg[0][:, :], lin[0], MUL), lin_free[0])
                        lin_wait(1, l + 1)
                        dve.sem_inc(slot_free[p], 1)
                        tell(TT(sg[1][:, :], sg[1][:, :], lin[1], MUL), lin_free[1])
                        dve.wait_ge(lin_free[0], l + 3)
                        dve.sem_inc(sem("sg_free"), 1)
                        dve.wait_ge(lin_free[1], l + 3)
                        tell(TT(merged[:, ds(2 * i + p, 1), :].squeeze(1), tmp[:, :], sg[1][:, :], ADD), sem("sg_free"))
                dve.wait_ge(sem("sg_free"), at("out", "sg") + 2)
                dve.sem_inc(sem("merged_done"), 1)

                def residual(b, l, k, gate_col, slot=None):
                    lin_wait(b, l)
                    if slot is not None:
                        dve.sem_inc(slot_free[slot], 1)
                    tell(STT(x[:, k, :], lin[b], gate_col, x[:, k, :], MUL, ADD), lin_free[b])

                for t in range(8):
                    residual(t % 2, at("out", "lin") + t // 2, t, mod[:, 16 + t:17 + t], {3: 0, 7: 1}.get(t))
                for b in range(2):
                    dve.wait_ge(lin_free[b], at("norm2", "lin") + 1)
                dve.sem_inc(sem("x_ready"), 1)
                rms_norm(layer * 2 + 1, at("norm2", "aux"), layer * 2 + 1)
                with mine.loop(0, 11) as i:
                    for p in range(2):
                        l, n = at("gu", "lin", i) + p, at("gu", "sg", i) + p
                        dve.wait_ge(sem("sg_done"), n + 1)
                        dve.sem_inc(lin_free[0], 1)
                        lin_wait(1, l)
                        dve.sem_inc(slot_free[p], 1)
                        tell(TT(hid[:, ds(2 * i + p, 1), :].squeeze(1), sg[p][:, :], lin[1], MUL), sem("sg_free"))
                        dve.wait_ge(sem("sg_free"), n + 3)
                        dve.sem_inc(lin_free[1], 1)
                dve.sem_inc(sem("hid_done"), 1)
                with mine.loop(0, 4) as i:
                    for p in range(2):
                        k = 2 * i + p
                        lin_wait(p, at("down", "lin", i))
                        dve.sem_inc(slot_free[p], 1)
                        tell(STT(x[:, ds(k, 1), :].squeeze(1), lin[p], mod[:, ds(k + 40, 1)], x[:, ds(k, 1), :].squeeze(1),
                            MUL, ADD), lin_free[p])
                for b in range(2):
                    dve.wait_ge(lin_free[b], layer * LAYER.total["lin"] + LAYER.total["lin"] + 1)
                dve.sem_inc(sem("x_ready"), 1)

            at = lambda stage, counter, turn=0: SECOND.at(stage, counter, turn)
            R0 = 2 * LAYERS
            with mine.loop(0, 6) as i:
                ada(SECOND, v2d, i, 0)
            gains(None, None, None, at("ln1", "lin"))
            mine.restart()
            layer_norm("ln1", 0, h, R0)

            dve.wait_ge(sem("fd_raw"), 1)
            dve.sem_inc(lin_free[0], 1)
            mine(TS(pr[0][0:16, :], raw[0][0:16, :], -1.0, 0.0, MUL, MAX))
            mine(dve.memset(pr[1][0:16, :], 1.0))
            dve.wait_ge(sem("fd_act"), 3)
            mine(TT(pr[0][0:16, :], pr[0][0:16, :], sm[0][0:16, :], ADD))
            tell(dve.tensor_tensor_scan(negF[0:16, :], pr[1][0:16, :], pr[0][0:16, :], 0.0, MUL, ADD), sem("f_done"))
            dve.wait_ge(sem("fd_raw"), 2)
            dve.sem_inc(lin_free[1], 1)
            mine(TS(pts[0][0:32, :], raw[1][0:32, :], 0.0, None, MAX))
            mine(dve.memset(pts[1][0:32, :], 1.0))
            mine(dve.memset(pts[1][0:32, :].rearrange("p (a b) -> p a b", b=P)[:, :, 0:1], 0.0))
            dve.wait_ge(sem("fd_act"), 6)
            mine(TT(dtT[0:32, :], pts[0][0:32, :], sm[1][0:32, :], ADD))
            dve.wait_ge(sem("a_done"), 1)
            mine(TS(pts[0][0:32, :], dtT[0:32, :], gain[0:32, 0:1], -1.0, MUL, MUL))
            tell(dve.tensor_tensor_scan(acs[0:32, :], pts[1][0:32, :], pts[0][0:32, :], 0.0, MUL, ADD), sem("acs_done"))
            a = at("fd", "aux")
            dve.wait_ge(aux_full, a + 1)
            tell(dve.tensor_copy(ftok, aux[:, 0:QT * 16].rearrange("p (a b) -> p a b", b=16)), aux_free)
            dve.wait_ge(aux_full, a + 2)
            tell(dve.tensor_copy(dt_tok, aux[:, 0:QT * 32].rearrange("p (a b) -> p a b", b=32)), aux_free)
            dve.wait_ge(aux_full, a + 3)
            tell(dve.tensor_copy(acs_tok, aux[:, 0:QT * 32].rearrange("p (a b) -> p a b", b=32)), aux_free)
            dve.wait_ge(aux_free, a + 4)
            dve.sem_inc(sem("acs_tok_done"), 1)
            dve.wait_ge(sem("cd_done"), 1)
            tell(TT(te_tok, aux[:, 0:QT * 32].rearrange("p (a b) -> p a b", b=32), acs_tok, SUB), aux_free)
            dve.wait_ge(aux_free, a + 5)
            dve.sem_inc(sem("te_diff"), 1)
            dve.wait_ge(sem("te_exp"), 1)
            mine(TT(te_tok, te_tok, dt_tok, MUL))
            mine.restart()

            with mine.loop(0, 4) as i:
                for b in range(2):
                    a, r = at("att", "aux", i) + b, at("att", "prep", i) + 3 * b
                    t = 3 * b
                    done(dve, "raw_done", r)
                    dve.sem_inc(lin_free[t % 2], 1)
                    heads = ident[0:16, ds(4 * i + 2 * b, 2)]
                    tell(dve.tensor_copy(fsel[b][0:16, :, :], heads.unsqueeze(2).broadcast_to([16, 2, P])), sem("prep_done"))
                    done(dve, "raw_done", r + 1)
                    dve.sem_inc(lin_free[(t + 1) % 2], 1)
                    tell(dve.tensor_copy(fq[b], ftok[:, :, ds(4 * i + 2 * b, 2)]), sem("prep_done"))
                    done(dve, "raw_done", r + 2)
                    dve.sem_inc(lin_free[t % 2], 1)
                    take_transposed(a, vtok[b], aux.rearrange("p (a b) -> p a b", b=P))
                    attention(at("att", "u", i) + 8 * b, at("att", "s", i) + 4 * b,
                              lambda g, b2, w: STT(sm[b2][:, 0:w], sc_b[b2][:, 0:w],
                                                   fq[b][:, g % QT, g // QT:g // QT + 1],
                                                   causal[:, SEQ - w:SEQ], SUB, ADD))

            def gated(stage, i, p, add):
                l, n = at(stage, "lin", i) + p, at(stage, "sg", i) + p
                dst = merged2[:, ds(2 * i + p, 1), :].squeeze(1)
                dve.wait_ge(sem("sg_done"), n + 1)
                dve.sem_inc(lin_free[0], 1)
                lin_wait(1, l)
                dve.sem_inc(slot_free[p], 1)
                if not add:
                    tell(TT(dst, sg[p][:, :], lin[1], MUL), sem("sg_free"))
                else:
                    mine(TT(tmp[:, :], sg[p][:, :], lin[1], MUL))
                    tell(TT(dst, dst, tmp[:, :], ADD), sem("sg_free"))
                dve.wait_ge(sem("sg_free"), n + 3)
                dve.sem_inc(lin_free[1], 1)

            with mine.loop(0, 4) as i:
                for p in range(2):
                    gated("attout", i, p, False)

            for t in range(2):
                mine(dve.memset(ub[t][:, 0:16], 0.0))
            for g in range(4):
                w = WINDOWS[g]
                for t in range(2):
                    dve.wait_ge(sem("ub_done"), 2 * g + t + 1)
                    dve.sem_inc(lin_free[t], 1)
                    src = ub[t]
                    for step in range(g + 1):
                        lo, dst = 2 ** (step + 1) - 1, level[step % 2]
                        mine(TT(dst[:, lo:], src[:, lo:], src[:, lo - 2 ** step:16 + SEQ - 2 ** step], ADD))
                        src = dst
                    first = pooled[t][:, 0:16]
                    if g:
                        dve.wait_ge(lin_free[1], at("pool", "lin", g) + 1)
                    mine(TT(first, src[:, 16:32], col("recip", 16 * g, 16), MUL))
                    mine(TT(first, first, ub[t][:, 16:32], SUB))
                    mine(STT(pooled[t][:, 16:], src[:, 32:], 1.0 / w, ub[t][:, 32:], MUL, SUB))
                    dve.sem_inc(sem("ub_free"), 1)
                dve.sem_inc(sem("pooled_done"), 1)
                for t in range(2):
                    k, l, n = 2 * g + t, at("pool", "lin", g) + 1 + t, at("pool", "sg", g) + t
                    dve.wait_ge(sem("sg_done"), n + 1)
                    dve.sem_inc(lin_free[0], 1)
                    lin_wait(1, l)
                    if t:
                        dve.sem_inc(slot_free[1], 1)
                    tell(STT(tmp[:, :], lin[1], v2("pool_scale", k), sg[t][:, :], MUL, MUL), sem("sg_free"))
                    dve.wait_ge(sem("sg_free"), n + 3)
                    dve.sem_inc(lin_free[1], 1)
                    mine(TT(merged2[:, k, :], merged2[:, k, :], tmp[:, :], ADD))
            mine.restart()

            with mine.loop(0, 4) as i:
                mine(dve.tensor_copy(gpar, v2d("ssm", i * SP_N, SP_N)))
                for dst, src in ((dtg, dt_tok), (acsg, acs_tok), (teg, te_tok), (cdg, cd_tok)):
                    mine(dve.tensor_copy(dst, src[:, :, ds(i * 8, 8)]))
                heads = ident[0:32, ds(i * 8, 8)]
                mine(dve.tensor_copy(selh[0:32, :, :], heads.unsqueeze(2).broadcast_to([32, 8, P])))
                mine(dve.tensor_copy(selp[0:32, :, :].rearrange("p a b -> p (a b)").rearrange("p (a b) -> p a b", b=HD),
                                     heads.unsqueeze(2).broadcast_to([32, 8, HD])))
                for b in range(2):
                    mine(dve.memset(cin[b][:, 0:3], 0.0))
                dve.sem_inc(sem("gpar_done"), 1)
                for t in range(6):
                    dve.wait_ge(sem("cin_done"), i * 6 + t + 1)
                    dve.sem_inc(lin_free[t % 2], 1)
                    free(dve, "silu_done", i * 6 + t)
                    c, o = cin[t % 2], cv[t % 2]
                    mine(TS(o, c[:, 0:SEQ], gpar[:, 5 * t:5 * t + 1], None, MUL))
                    for tap in range(1, 4):
                        ins = STT(o, c[:, tap:tap + SEQ], gpar[:, 5 * t + tap:5 * t + tap + 1], o, MUL, ADD)
                        if tap < 3:
                            mine(ins)
                    tell(ins, sem("conv_done"))
                for c in range(QT):
                    dve.wait_ge(sem("xt_done"), i * 4 + c + 1)
                    src = pt_b[c % 2].rearrange("p (a b) -> p a b", b=HD)
                    if c < 3:
                        mine(TT(xde[:, c, :].rearrange("p (a b) -> p a b", b=HD), src,
                                teg[:, c, :].unsqueeze(2).broadcast_to([P, 8, HD]), MUL))
                    tell(TT(xdt[:, c, :].rearrange("p (a b) -> p a b", b=HD), src,
                       dtg[:, c, :].unsqueeze(2).broadcast_to([P, 8, HD]), MUL), sem("xd_done"))
                dve.wait_ge(sem("bt_done"), i + 1)
                tell(dve.tensor_copy(btok.rearrange("p a b -> p (a b)"), ob), sem("btok_done"))
                dve.wait_ge(sem("cb_done"), i + 1)
                tell(TT(cbm, sc_b[0].rearrange("p (a b) -> p a b", b=P), tri.unsqueeze(1).broadcast_to([P, QT, P]), MUL), sem("cbm_done"))
                for c in range(3):
                    dve.wait_ge(sem("st_done"), i * 3 + c + 1)
                    if c == 0:
                        tell(dve.tensor_copy(hst[:, 0, :], pt_b[0]), sem("hst_done"))
                    else:
                        dve.wait_ge(sem("hst_done"), i * 3 + c)
                        hv = lambda n: hst[:, n, :].rearrange("p (a b) -> p a b", b=HD)
                        mine(TT(hv(c), hv(c - 1), cdg[:, c, :].unsqueeze(2).broadcast_to([P, 8, HD]), MUL))
                        tell(TT(hst[:, c, :], hst[:, c, :], pt_b[c % 2], ADD), sem("hst_done"))

                def pair(j):
                    done(dve, "yd_done", i * 8 + 2 * j + 1)
                    dve.wait_ge(sem("yoff_done"), i * 4 + j + 1)
                    dve.wait_ge(sem("ea_done"), i * 4 + j + 1)
                    mine(TT(tmp[:, P:], pt_b[0][:, P:], ea[:, P:], MUL))
                    mine(STT(yg[:, j, :], xsT[:, j, :], gpar[:, 30 + j:31 + j], ob, MUL, ADD))
                    tell(TT(yg[:, j, P:], yg[:, j, P:], tmp[:, P:], ADD), sem("yp_done"))

                for hh in range(8):
                    dve.wait_ge(sem("bc_done"), i * 8 + hh + 1)
                    free(dve, "wgt_done", i * 8 + hh)
                    mine(TT(seg[hh % 2].rearrange("p (a b) -> p a b", b=P),
                            sc_b[hh % 2].rearrange("p (a b) -> p a b", b=P),
                            acsg[:, :, hh:hh + 1].broadcast_to([P, QT, P]), SUB))
                    tell(TS(seg[hh % 2], seg[hh % 2], 0.0, None, MIN), sem("seg_done"))
                    if hh % 2 == 0 and hh:
                        pair(hh // 2 - 1)
                pair(3)
                dve.wait_ge(sem("yp_done"), i * 4 + 5)
                for t in range(4):
                    n = at("ssd", "sg", i) + t
                    dve.wait_ge(sem("sg_done"), n + 1)
                    dve.sem_inc(lin_free[t % 2], 1)
                    tell(TT(yg[:, t, :], yg[:, t, :], sg[t % 2][:, :], MUL), sem("sg_free"))
                dve.wait_ge(sem("sg_free"), at("ssd", "sg", i) + 6)
                dve.sem_inc(sem("yz_done"), 1)
                a = at("ssd", "aux", i)
                dve.wait_ge(sem("root_done"), i + (R0 + 2))
                tell(dve.reciprocal(rstd[:, :], rstd[:, :]), aux_free)
                dve.wait_ge(aux_free, a + 2)
                for t in range(4):
                    mine(STT(yT[:, ds(i * 4 + t, 1), :].squeeze(1), yg[:, t, :], gpar[:, 34 + t:35 + t], rstd[:, :],
                             MUL, MUL))
                mine.restart()
                dve.sem_inc(sem("yT_done"), 1)
            with mine.loop(0, 4) as i:
                for p in range(2):
                    gated("ssdout", i, p, True)
                mine.restart()
            dve.sem_inc(sem("merged2_done"), 1)

            for t in range(8):
                lin_wait(t % 2, at("out", "lin") + t // 2)
                if t % 4 == 3:
                    dve.sem_inc(slot_free[t // 4], 1)
                tell(TS(tmp[:, :], lin[t % 2], mod[:, 16 + t:17 + t], None, MUL), lin_free[t % 2])
                dve.wait_ge(lin_free[t % 2], at("out", "lin") + t // 2 + 2)
                mine(STT(x[:, t, :], x[:, t, :], ALPHA, tmp[:, :], MUL, ADD))
            dve.sem_inc(sem("x_ready"), 1)
            layer_norm("ln2", 1, x, R0 + 5)
            dve.wait_ge(sem("x_ready"), 7)
            layer_norm("ln3", 2, h, R0 + 6)

            rep = lambda v: v.unsqueeze(2).broadcast_to([P, QT, E_N])
            probs, sel, ing, e1, e2, t1, t2, small = rt
            s4 = [small[:, :, n:n + 1].squeeze(2) for n in range(16)]
            a = at("router", "aux")
            dve.wait_ge(aux_full, a + 1)
            tell(dve.tensor_copy(probs, aux[:, 0:QT * E_N].rearrange("p (a b) -> p a b", b=E_N)), aux_free)
            dve.wait_ge(aux_free, a + 2)

            def step(ins):
                mine(ins)

            step(dve.tensor_reduce(s4[0], probs, AX.X, MAX))
            tell(TT(probs, probs, rep(s4[0]), SUB), sem("logit_done"))
            dve.wait_ge(sem("probs_exp"), 1)
            step(dve.tensor_reduce(s4[0], probs, AX.X, ADD))
            step(dve.reciprocal(s4[1], s4[0]))
            step(TT(probs, probs, rep(s4[1]), MUL))
            step(TT(sel, probs, v2("b_router", 0, E_N).unsqueeze(1).broadcast_to([P, QT, E_N]), ADD))
            fold = lambda v: v.rearrange("p a b -> p (a b)").rearrange("p (a b) -> p a b", b=4)
            sf, tf, uf = fold(sel), fold(t1), fold(t2)
            step(TT(tf[:, :, 0:3], sf[:, :, 0:3], sf[:, :, 1:4], ADD))
            step(TT(uf[:, :, 0:2], sf[:, :, 0:2], sf[:, :, 2:4], ADD))
            step(TT(uf[:, :, 2:3], sf[:, :, 0:1], sf[:, :, 3:4], ADD))
            step(TT(tf[:, :, 0:3], tf[:, :, 0:3], uf[:, :, 0:3], MAX))
            gs = small.rearrange("p a b -> p (a b)")[:, 0:16]
            step(dve.tensor_reduce(gs.unsqueeze(2), tf[:, :, 0:3], AX.X, MAX))
            gs = gs.rearrange("p (a b) -> p a b", b=4)
            best = small.rearrange("p a b -> p (a b)")[:, 16:20]
            taken = small.rearrange("p a b -> p (a b)")[:, 20:24]
            pick = small.rearrange("p a b -> p (a b)")[:, 24:40].rearrange("p (a b) -> p a b", b=4)
            step(dve.tensor_reduce(best, gs, AX.X, MAX))
            step(TT(pick, gs, best.unsqueeze(2).broadcast_to([P, QT, 4]), ALU.is_equal))
            col4 = lambda v, n: v[:, :, n:n + 1].squeeze(2)
            step(dve.tensor_copy(taken, col4(pick, 0)))
            for n in range(1, 4):
                step(TT(col4(gs, n), col4(pick, n), taken, MUL))
                step(TT(col4(pick, n), col4(pick, n), col4(gs, n), SUB))
                step(TT(taken, taken, col4(pick, n), ADD))
            pk = small.rearrange("p a b -> p (a b)")[:, 24:40]
            step(dve.tensor_copy(fold(ing), pk.unsqueeze(2).broadcast_to([P, 16, 4])))
            step(TT(sel, sel, ing, MUL))
            step(TS(ing, ing, 1.0, -NEG, SUB, MUL))
            step(TT(sel, sel, ing, ADD))
            rev = col("revidx", 0, E_N).unsqueeze(1).broadcast_to([P, QT, E_N])
            for e in (e1, e2):
                step(dve.tensor_reduce(s4[0], sel, AX.X, MAX))
                step(TT(t1, sel, rep(s4[0]), ALU.is_equal))
                step(TT(t1, t1, rev, MUL))
                step(dve.tensor_reduce(s4[0], t1, AX.X, MAX))
                step(TT(e, t1, rep(s4[0]), ALU.is_equal))
                step(STT(sel, e, 4 * NEG, sel, MUL, ADD))
            step(TT(e1, e1, e2, ADD))
            step(TT(gw, e1, probs, MUL))
            step(dve.tensor_reduce(s4[0], gw, AX.X, ADD))
            step(dve.reciprocal(s4[1], s4[0]))
            step(TT(gw, gw, rep(s4[1]), MUL))
            step(dve.memset(moe, 0.0))
            dve.sem_inc(sem("gw_done"), 1)
            mine.restart()

            with mine.loop(0, 8) as i:
                for ex in range(2):
                    l, n = at("moe", "lin", i) + 8 * ex, at("moe", "sg", i) + 4 * ex
                    tell(dve.tensor_copy(esel[ex][0:E_N, :], ident[0:E_N, ds(2 * i + ex, 1)].broadcast_to([E_N, P])), sem("esel_done"))
                    dve.wait_ge(sem("gwb_done"), i * 2 + ex + 1)
                    dve.sem_inc(aux_free, 1)
                    for t in range(4):
                        dve.wait_ge(sem("sg_done"), n + t + 1)
                        dve.sem_inc(lin_free[0], 1)
                        lin_wait(1, l + t)
                        if t == 3:
                            dve.sem_inc(slot_free[(3 * ex + 1) % 2], 1)
                        tell(TT(hid2[:, t, :], sg[t % 2][:, :], lin[1], MUL), sem("sg_free"))
                        dve.wait_ge(sem("sg_free"), n + t + 3)
                        dve.sem_inc(lin_free[1], 1)
                        dve.sem_inc(sem("hid_raw"), 1)
                    for t in range(8):
                        lin_wait(t % 2, l + 4 + t // 2)
                        if t == 7:
                            dve.sem_inc(slot_free[(3 * ex) % 2], 1)
                        tell(TT(moe[:, t, :], moe[:, t, :], lin[t % 2], ADD), lin_free[t % 2])
            for b in range(2):
                dve.wait_ge(lin_free[b], at("ln4", "lin") + 1)
            for t in range(8):
                mine(TS(moe[:, t, :], moe[:, t, :], mod[:, 40 + t:41 + t], None, MUL))
            for t in range(8):
                mine(STT(x[:, t, :], x[:, t, :], ALPHA, moe[:, t, :], MUL, ADD))
            dve.sem_inc(sem("x_ready"), 1)
            layer_norm("ln4", 3, x, R0 + 7)

        @block.gpsimd
        def _(pool):
            mine = Steps(pool, sem("pool_steps"))
            tell = mine.tell
            pool.sem_inc(sem("pn_done"), 2)
            pool.sem_inc(sem("wgt_done"), 2)
            pool.sem_inc(sem("hidw_done"), 1)

            def attention(u):
                for g in range(8):
                    w = P * (g % QT + 1)
                    pool.wait_ge(sem("rcp_done"), u + g + 1)
                    tell(pool.tensor_tensor(pr[g % 2][:, 0:w], pr[g % 2][:, 0:w], rcp[:, g:g + 1].broadcast_to([P, w]),
                                       ALU.mult), sem("pn_done"))

            with mine.loop(0, LAYERS) as layer:
                for stage in ("A", "B"):
                    for j in range(4):
                        attention(LAYER.at(stage, "u", 0, layer) + 8 * j)
            with mine.loop(0, 4) as i:
                for b in range(2):
                    attention(SECOND.at("att", "u", i) + 8 * b)
            with mine.loop(0, 4) as i:
                pool.wait_ge(sem("cbm_done"), i + 1)
                for hh in range(8):
                    pool.wait_ge(sem("e_done"), i * 8 + hh + 1)
                    free(pool, "yd_done", i * 8 + hh)
                    tell(pool.tensor_tensor(wgt[hh % 2], seg[hh % 2], cbm.rearrange("p a b -> p (a b)"), ALU.mult), sem("wgt_done"))
            with mine.loop(0, 8) as i:
                for ex in range(2):
                    for t in range(4):
                        pool.wait_ge(sem("hid_raw"), i * 8 + 4 * ex + t + 1)
                        if t == 0:
                            pool.wait_ge(sem("gwb_done"), i * 2 + ex + 1)
                        tell(pool.tensor_tensor(hid2[:, t, :], hid2[:, t, :], gwb[ex], ALU.mult), sem("hidw_done"))


_INS = ["x", "c", "positions", "w_ada", "b_ada", "g_mix", "w_in", "b_in", "qn_a", "kn_a", "qn_b", "kn_b", "rel_bias",
        "w_oa", "w_ob", "w_out", "g_ffn", "w_gu", "w_down"]


def _constants():
    c = np.zeros((P, NCST), np.float32)

    def put(name, value):
        a, b = CST[name]
        c[:, a:b] = value

    q, k = np.arange(P)[:, None], np.arange(P)[None, :]
    put("ident", q == k)
    put("blockones", q // HD == k // HD)
    put("ones", 1)
    same = q // HD == k // HD
    put("rope", 1.0 * (same & (k % HD >= 8) & (k % HD < 16) & (q == k - 8)) - 1.0 * (same & (k % HD < 8) & (q == k + 8)))
    put("last", q == P - 1)
    adm, causal = np.zeros((P, SEQ)), np.zeros((P, SEQ))
    adm[:, SEQ - P:] = np.where(k // HD > q // HD, NEG, 0)
    causal[:, SEQ - P:] = np.where(k > q, NEG, 0)
    put("adm", adm)
    put("causal", causal)
    put("tri", k >= q)
    put("recip", np.concatenate([1 / np.minimum(np.arange(1, 17), w) for w in WINDOWS])[None])
    inv = np.float32(500000.0) ** (-np.arange(0, 16, 2, dtype=np.float32) / np.float32(16))
    d = np.arange(P) % HD
    put("inv_freq", np.where(d < 16, inv[d % 8], 0).astype(np.float32)[:, None])
    put("revidx", np.arange(E_N, 0, -1)[None])
    return c


def _tiles(v):
    return v.reshape(-1, P).T


def _chunks(w):
    return w.reshape(-1, P, w.shape[1]).transpose(1, 0, 2).reshape(P, -1)


def _slot(*parts):
    return np.concatenate([_chunks(w) for w in parts], axis=1).reshape(-1)


def kernel(**inputs):
    import concourse.bacc as _bacc
    from concourse.bass_utils import run_bass_kernel_spmd as _run

    g = {k: np.asarray(v) for k, v in inputs.items()}
    slots, vec1, rel = [], [], []
    for l in range(LAYERS):
        w_ada, w_in, b_in = g["w_ada"][l], g["w_in"][l], g["b_in"][l]
        cols = lambda at, n: w_in[:, at:at + n]
        tile = lambda w, i: w[:, i * P:(i + 1) * P]
        slots += [_slot(w_ada[:, i * 512:(i + 1) * 512]) for i in range(12)]
        two = lambda a: np.concatenate([a, a], axis=-1)
        slots += [_slot(two(cols(KA, HD)), two(cols(KI, HD))), _slot(cols(VA, HD), cols(WI, 8))]
        slots += [_slot(cols(QI + i * P, P)) for i in range(4)]
        slots += [_slot(cols(QA + i * P, P)) for i in range(4)]
        slots += [_slot(cols(QB + i * P, P), cols(KB + i * P, P), cols(VB + i * P, P)) for i in range(4)]
        slots += [_slot(cols(GA + i * P, P), cols(GB + i * P, P), tile(g["w_oa"][l], i), tile(g["w_ob"][l], i))
                  for i in range(8)]
        slots += [_slot(g["w_out"][l][:, i * 512:(i + 1) * 512]) for i in range(2)]
        slots += [_slot(tile(g["w_gu"][l], i), g["w_gu"][l][:, FF + i * P:FF + (i + 1) * P]) for i in range(FF_T)]
        slots += [_slot(tile(g["w_down"][l], i)) for i in range(8)]
        v = np.zeros((P, NV1), np.float32)

        def put(name, value):
            a, b = VEC1[name]
            v[0:value.shape[0], a:b] = value

        put("b_ada", _tiles(g["b_ada"][l]))
        put("g_mix", _tiles(g["g_mix"][l]))
        put("g_ffn", _tiles(g["g_ffn"][l]))
        for name, at, n in (("qa", QA, 4), ("qi", QI, 4), ("qb", QB, 4), ("kb", KB, 4), ("vb", VB, 4), ("ga", GA, 8),
                            ("gb", GB, 8)):
            put(name, _tiles(b_in[at:at + n * P]))
        put("ka", two(b_in[KA:KA + HD])[:, None])
        put("ki", two(b_in[KI:KI + HD])[:, None])
        put("va", b_in[VA:VA + HD][:, None])
        put("wi", b_in[WI:WI + 8][:, None])
        for name in ("qn_a", "kn_a", "qn_b", "kn_b"):
            put(name, two(g[name][l])[:, None])
        vec1.append(v.reshape(-1))
        at = np.clip(np.arange(P)[:, None] - np.arange(SEQ)[None] + SEQ - P, -63, 256) + 63
        rel.append(g["rel_bias"][l][:, at].transpose(1, 0, 2).reshape(-1))

    w2, tile = g["w_in_2"][0], lambda w, i, n=P: w[:, i * n:(i + 1) * n]
    cols = lambda at, n: w2[:, at:at + n]
    slots += [_slot(tile(g["w_ada_2"][0], i, 512)) for i in range(12)]
    slots += [_slot(cols(F2, 16)), _slot(cols(DT2, 32))]
    slots += [_slot(cols(Q2 + i * P, P), cols(K2 + i * P, P), cols(V2 + i * P, P)) for i in range(8)]
    slots += [_slot(cols(G2 + i * P, P), tile(g["w_attn_o_2"][0], i)) for i in range(8)]
    for i in range(4):
        slots += [_slot(cols(U2 + i * 256, 256)), _slot(cols(G2 + D + i * 256, 256), g["w_pool_2"][0][i])]
    for i in range(4):
        bc = np.concatenate([cols(XBC2 + 2048 + i * P, P), cols(XBC2 + 2560 + i * P, P)], axis=1)
        slots += [_slot(cols(XBC2 + i * 512, 512)), _slot(bc), _slot(cols(Z2 + i * 512, 256)),
                  _slot(cols(Z2 + i * 512 + 256, 256))]
    slots += [_slot(cols(G2 + 2 * D + i * P, P), tile(g["w_ssm_o_2"][0], i)) for i in range(8)]
    slots += [_slot(tile(g["w_out_2"][0], i, 512)) for i in range(2)]
    for e in range(E_N):
        slots += [_slot(g["w_exp_gate_2"][0, e]), _slot(g["w_exp_up_2"][0, e]), _slot(g["w_exp_down_2"][0, e])]

    v2_ = np.zeros((P, NV2), np.float32)

    def put2(name, value):
        a, b = VEC2[name]
        v2_[0:value.shape[0], a:b] = value

    put2("b_ada", _tiles(g["b_ada_2"][0]))
    for name in ("pool_scale", "ln_mix_g", "ln_mix_b", "ln_ffn_g", "ln_ffn_b"):
        put2(name, _tiles(g[name + "_2"][0]))
    for name in ("b_forget", "dt_bias", "a_log"):
        put2(name, g[name + "_2"][0][:, None])
    taps = np.concatenate([g["conv_w_2"][0], g["conv_b_2"]], axis=0).reshape(5, 24, P).transpose(2, 1, 0)
    skip = np.repeat(g["d_skip_2"][0], HD).reshape(16, P).T
    norm = _tiles(g["ssm_norm_w_2"][0])
    for i in range(4):
        a = VEC2["ssm"][0] + i * SP_N
        for n, t in enumerate((4 * i, 4 * i + 1, 4 * i + 2, 4 * i + 3, 16 + i, 20 + i)):
            v2_[:, a + 5 * n:a + 5 * n + 5] = taps[:, t]
        v2_[:, a + 30:a + 34] = skip[:, 4 * i:4 * i + 4]
        v2_[:, a + 34:a + 38] = norm[:, 4 * i:4 * i + 4]
    put2("w_router", _chunks(g["w_router_2"]))
    put2("b_router", np.broadcast_to(g["b_router_2"], (P, E_N)))

    arrays = {
        "w_all": np.concatenate(slots),
        "vec1": np.concatenate(vec1),
        "vec2": v2_,
        "consts": _constants(),
        "x_in": np.ascontiguousarray(g["x"][0].T.reshape(KC, P, SEQ).transpose(1, 0, 2)),
        "pos": np.ascontiguousarray(np.broadcast_to(g["positions"], (P, SEQ))),
        "cond": np.concatenate([_tiles(g["c"][0]), _tiles(g["c_2"][0])], axis=1),
        "rel": np.concatenate(rel),
    }
    nc = _bacc.Bacc("TRN2", target_bir_lowering=False, num_devices=1)
    args = [nc.dram_tensor("in_" + k, a.shape, mybir.dt.from_np(a.dtype), kind="ExternalInput").ap() for k, a in arrays.items()]
    out = nc.dram_tensor("out", (P, KC, SEQ), F32, kind="ExternalOutput").ap()
    two_blocks(nc, *args[:4], *args[4:], out)
    r = _run(nc, [{"in_" + k: a for k, a in arrays.items()}], core_ids=[0])
    y = r.results[0]["out"]
    return np.ascontiguousarray(y.transpose(1, 0, 2).reshape(D, SEQ).T)[None]
```

```python
import numpy as np
import concourse.bass as bass
from concourse import mybir
from contextlib import ExitStack, contextmanager

F32 = mybir.dt.float32
I32 = mybir.dt.int32
ALU = mybir.AluOpType
ACT = mybir.ActivationFunctionType
AX = mybir.AxisListType
ds = bass.ds

P = 128
D, SEQ, KC = 1024, 512, 8
QT = SEQ // P
LAYERS = 2
HD = 64
FF_T = 2816 // P
FF = FF_T * P
TOP_K = 128
IDX_SCALE = 64 ** -0.5 * 8 ** -0.5
EPS, LN_EPS = 1e-6, 1e-5
ALPHA = 2 ** 0.25
NEG = -1e30
TAKEN = -3e38
E_N, E_FF = 16, 512
N_BLK = (2 * SEQ + E_N * (P - 1)) // P
WINDOWS = (2, 4, 8, 16)

QA, KA, VA, QI, KI, WI, QB, KB, VB, GA, GB = 0, 512, 576, 640, 1152, 1216, 1224, 1736, 2248, 2760, 3784
Q2, K2, V2, F2, U2, Z2, XBC2, DT2, G2 = 0, 1024, 2048, 3072, 3088, 4112, 6160, 9232, 9264


def column_map(parts):
    at, out = 0, {}
    for name, n in parts:
        out[name] = (at, at + n)
        at += n
    return out, at


VEC1, NV1 = column_map([("b_ada", 48), ("g_mix", 8), ("g_ffn", 8), ("qa", 4), ("qi", 4), ("ka", 1), ("ki", 1),
                        ("va", 1), ("wi", 1), ("qb", 4), ("kb", 4), ("vb", 4), ("ga", 8), ("gb", 8),
                        ("qn_a", 1), ("kn_a", 1), ("qn_b", 1), ("kn_b", 1)])
SP_N = 38
VEC2, NV2 = column_map([("b_ada", 48), ("pool_scale", 8), ("ln_mix_g", 8), ("ln_mix_b", 8), ("ln_ffn_g", 8),
                        ("ln_ffn_b", 8), ("b_forget", 1), ("dt_bias", 1), ("a_log", 1), ("ssm", 4 * SP_N),
                        ("w_router", KC * E_N), ("b_router", E_N)])
CST, NCST = column_map([("ident", P), ("blockones", P), ("ones", P), ("rope", P), ("last", P), ("adm", SEQ),
                        ("causal", SEQ), ("tri", P), ("recip", 4 * 16), ("inv_freq", 1), 
                        ("revidx", E_N), ("blocks", N_BLK), ("steps", QT)])


class Plan:

    def __init__(self, stages, start=None):
        self.stages, self.inc, self.base, at = stages, {}, {}, dict(start or {})
        for name, turns, inc in stages:
            self.inc[name], self.base[name] = inc, dict(at)
            for k, n in inc.items():
                at[k] = at.get(k, 0) + n * turns
        self.total = at

    def at(self, stage, counter, turn=0, layer=0):
        value = self.base[stage].get(counter, 0) + turn * self.inc[stage].get(counter, 0)
        return layer * self.total.get(counter, 0) + value


LAYER = Plan([
    ("ada", 6, dict(slot=1, lin=1)),
    ("norm1", 1, dict(aux=1)),
    ("misc", 1, dict(slot=1, lin=2, aux=5, prep=4, nrm=1, rope=1)),
    ("idx", 1, dict(slot=2, lin=2, aux=4, prep=4, s=12, iu=24)),
    ("A", 1, dict(slot=2, lin=2, aux=8, prep=4, nrm=4, rope=4, s=16, u=32, o=4)),
    ("B", 1, dict(slot=2, lin=6, aux=12, prep=12, nrm=8, s=16, u=32, o=4)),
    ("gates", 4, dict(slot=1, lin=4, sg=4)),
    ("out", 1, dict(slot=1, lin=4)),
    ("norm2", 1, dict(aux=1)),
    ("gu", 11, dict(slot=1, lin=2, sg=2)),
    ("down", 4, dict(slot=1, lin=1)),
])
SECOND = Plan([
    ("ada", 6, dict(slot=1, lin=1)),
    ("ln1", 1, dict(aux=2)),
    ("fd", 1, dict(slot=1, lin=1, aux=4)),
    ("att", 4, dict(slot=1, lin=3, aux=2, prep=6, s=8, u=16, o=2)),
    ("attout", 4, dict(slot=1, lin=2, sg=2)),
    ("pool", 4, dict(slot=1, lin=3, sg=2)),
    ("ssd", 4, dict(slot=2, lin=5, aux=1, sg=4)),
    ("ssdout", 4, dict(slot=1, lin=2, sg=2)),
    ("out", 1, dict(slot=1, lin=4)),
    ("ln2", 1, dict(aux=2)),
    ("ln3", 1, dict(aux=2)),
    ("router", 1, dict(aux=5)),
    ("ln4", 1, dict(aux=2)),
], {k: LAYERS * n for k, n in LAYER.total.items()})

SLOTS_1 = ([KC * 512] * 12 + [2 * KC * P, KC * 72] + [KC * P] * 8 + [3 * KC * P] * 4 + [2 * KC * P + 8 * P] * 8
           + [KC * 512] * 2 + [2 * KC * P] * 22 + [FF_T * P] * 8)
SLOTS_2 = ([KC * 512] * 12 + [KC * 16, KC * 32] + [3 * KC * P] * 8 + [2 * KC * P] * 8
           + [KC * 256, KC * 256 + 512] * 4 + [KC * 512, KC * 256, KC * 256, KC * 256] * 4 + [KC * P + 16 * P] * 8
           + [KC * 512] * 2)
EXPERT = 3 * D * E_FF
W1_TOTAL = sum(SLOTS_1) * P
EXPERTS_AT = LAYERS * W1_TOTAL + sum(SLOTS_2) * P
assert len(SLOTS_1) == 2 * LAYER.total["slot"], (len(SLOTS_1), LAYER.total)
assert len(SLOTS_2) == 2 * (SECOND.total["slot"] - LAYERS * LAYER.total["slot"])


class Steps:

    def __init__(self, eng, sem):
        self.eng, self.sem, self.n = eng, sem, 0

    def __call__(self, ins):
        self.n += 1
        ins.then_inc(self.sem, 1)
        self.eng.wait_ge(self.sem, self.n)

    def tell(self, ins, signal):
        self(ins)
        self.eng.sem_inc(signal, 1)

    def restart(self):
        if self.n:
            self.eng.sem_clear(self.sem)
            self.n = 0

    @contextmanager
    def loop(self, start, end):
        self.restart()
        with self.eng.Fori(start, end) as i:
            yield i
            self.restart()


def two_blocks(nc, w_all, vec1_all, vec2_all, consts, x_in, pos_in, cond, rel, out):
    ctx = ExitStack()
    with ctx:
        sems = {}

        def sem(name):
            if name not in sems:
                sems[name] = ctx.enter_context(nc.semaphore(name))
            return sems[name]

        def sb(name, *shape, dt=F32):
            t = ctx.enter_context(nc.sbuf_tensor(name, [P, *shape], dt))
            return t[:, :, :] if len(shape) == 2 else t[:, :]

        x = sb("x", KC, SEQ)
        h = sb("h", KC, SEQ)
        ring = [sb("ring0", 4096), sb("ring1", 4096)]
        cst = sb("cst", NCST)
        vec = sb("vec", NV1)
        vec2 = sb("vec2", NV2)
        mod = sb("mod", 48)
        gain = sb("gain", 16)
        csil = sb("csil", 16)
        cosT, sinT = sb("cosT", SEQ), sb("sinT", SEQ)
        rstd = sb("rstd", SEQ)
        tmp = sb("tmp", SEQ)
        sg = [sb("sg0", SEQ), sb("sg1", SEQ)]
        abuf = sb("abuf", 14, SEQ)
        qT, kT = [abuf[:, 0, :], abuf[:, 1, :]], [abuf[:, 2, :], abuf[:, 3, :]]
        vtok = [abuf[:, 4 + b, :].rearrange("p (a b) -> p a b", b=P) for b in range(2)]
        raw = [abuf[:, 6, :], abuf[:, 7, :]]
        sm, pr, pts = ([abuf[:, n, :], abuf[:, n + 1, :]] for n in (8, 10, 12))
        sq, rs = sb("sq", SEQ), sb("rs", SEQ)
        nmax, esum, rcp = sb("nmax", 8), sb("esum", 8), sb("rcp", 8)
        ARENA = 22800
        arena = sb("arena", ARENA)
        cursor = [0]

        def part(*shape):
            n = int(np.prod(shape))
            v = arena[:, cursor[0]:cursor[0] + n]
            cursor[0] += n
            assert cursor[0] <= ARENA, cursor[0]
            if len(shape) == 2:
                v = v.rearrange("p (a b) -> p a b", b=shape[1])
            return v

        attA, attB = part(4, SEQ), part(4, SEQ)
        mask, score = part(QT, SEQ), part(QT, SEQ)
        merged = part(KC, SEQ)
        hid = arena[:, 0:FF_T * SEQ].rearrange("p (a b) -> p a b", b=SEQ)
        relb = part(8, SEQ)
        kaT, kiT, va = part(SEQ), part(SEQ), part(QT, HD)
        wtok, top8 = part(QT, 8), part(8)
        cursor[0] = 0
        merged2 = part(KC, SEQ)
        negF, ftok = part(SEQ), part(QT, 16)
        dtT, acs = part(SEQ), part(SEQ)
        dt_tok, acs_tok, te_tok, cd_tok = part(QT, 32), part(QT, 32), part(QT, 32), part(QT, 32)
        shared_end = cursor[0]
        att2 = part(KC, SEQ)
        fsel = [part(2, P), part(2, P)]
        fq = [part(QT, 2), part(QT, 2)]
        ub = [part(16 + SEQ), part(16 + SEQ)]
        level = [part(16 + SEQ), part(16 + SEQ)]
        pooled = [part(SEQ), part(SEQ)]
        cursor[0] = shared_end
        yT = part(16, SEQ)
        xdt, xde, hst = part(QT, SEQ), part(3, SEQ), part(3, SEQ)
        cin = [hst.rearrange("p a b -> p (a b)")[:, 515 * b:515 * b + 515] for b in range(2)]
        yg, xsT = abuf[:, 0:4, :], abuf[:, 4:8, :]
        seg, wgt, ea, bmT = sm, pr, abuf[:, 12, :], abuf[:, 13, :]
        cv = pr
        cmT = part(SEQ)
        btok, cbm = part(QT, P), part(QT, P)
        selh, selp = part(8, P), part(4, P)
        gpar = part(SP_N)
        dtg, acsg, teg, cdg = part(QT, 8), part(QT, 8), part(QT, 8), part(QT, 8)
        cursor[0] = shared_end
        moe = part(KC, SEQ)
        htok = part(QT, D)
        wdown = part(4 * D)
        gw, rt = part(QT, E_N), [part(QT, E_N) for _ in range(8)]
        weight1, weight2, dest1, dest2 = part(QT), part(QT), part(QT), part(QT)
        n_blocks, ends, base, fits = part(1), part(1), part(1), part(QT)
        past = part(N_BLK)
        row1, row2, expert_of = (part(n).bitcast(I32) for n in (QT, QT, N_BLK))
        flat = lambda v: v.rearrange("p a b -> p (a b)")
        xr, hidb = flat(abuf[:, 0:2, :]), abuf[:, 6, :]
        xT = [flat(abuf[:, n:n + 2, :]) for n in (2, 4)]
        yb = [flat(abuf[:, n:n + 2, :]) for n in (7, 9)]
        position, cum, unit, chosenT = (abuf[:, n, :] for n in (10, 11, 12, 13))
        routed = nc.dram_tensor("routed", ((N_BLK + 1) * P, D), F32, kind="Internal").ap()
        made = nc.dram_tensor("made", (N_BLK * P, D), F32, kind="Internal").ap()

        banks = ctx.enter_context(nc.psum_tensor("banks", [P, 8, SEQ], F32))[:, :, :]
        lin, aux = [banks[:, 0, :], banks[:, 1, :]], banks[:, 2, :]
        sc_b, pt_b, ob = [banks[:, 3, :], banks[:, 4, :]], [banks[:, 5, :], banks[:, 6, :]], banks[:, 7, :]

        def col(name, i=0, n=1):
            at = CST[name][0] + i
            return cst[:, at:at + n]

        def v1(name, i=0, n=1):
            at = VEC1[name][0] + i
            return vec[:, at:at + n]

        def v1d(name, i, n=1):
            return vec[:, ds(i + VEC1[name][0], n)]

        def v2(name, i=0, n=1):
            at = VEC2[name][0] + i
            return vec2[:, at:at + n]

        def v2d(name, i, n=1):
            return vec2[:, ds(i + VEC2[name][0], n)]

        ident, blockones, ones, rope, last = (col(n, 0, P) for n in ("ident", "blockones", "ones", "rope", "last"))
        adm, causal, tri = col("adm", 0, SEQ), col("causal", 0, SEQ), col("tri", 0, P)

        boot, c_in, vec_in, rel_in, out_done = (sem(n) for n in ("boot", "c_in", "vec_in", "rel_in", "out_done"))
        slot_full, slot_free = [sem("slot_full0"), sem("slot_full1")], [sem("slot_free0"), sem("slot_free1")]
        lin_full, lin_free = [sem("lin_full0"), sem("lin_full1")], [sem("lin_free0"), sem("lin_free1")]
        s_full, s_free = [sem("s_full0"), sem("s_full1")], [sem("s_free0"), sem("s_free1")]
        aux_full, aux_free, o_free = sem("aux_full"), sem("aux_free"), sem("o_free")

        def done(eng, name, n):
            eng.wait_ge(sem(name), n + 3)

        def free(eng, name, n):
            eng.wait_ge(sem(name), n + 1)

        def hold(eng):
            eng.sem_inc(sem("held"), 1)

        block = ctx.enter_context(nc.Block())

        @block.sync
        def _(sp):
            def stream(plan, stage, sizes, turn, layer, offset):
                for n, size in enumerate(sizes):
                    use = plan.at(stage, "slot", turn, layer) + n // 2
                    sp.wait_ge(slot_free[n % 2], use + 1)
                    src = w_all[ds(offset, size * P)].rearrange("(p n) -> p n", p=P)
                    sp.dma_start(ring[n % 2][:, 0:size], src).then_inc(slot_full[n % 2], 16)
                    offset = offset + size * P

            def run(plan, sizes_all, stages, layer, offset, loops):
                at = 0
                for stage, turns, inc in stages:
                    n = 2 * inc.get("slot", 0)
                    if not n:
                        continue
                    if stage in loops:
                        sizes = sizes_all[at:at + n]
                        with sp.Fori(0, turns) as i:
                            stream(plan, stage, sizes, i, layer, offset + i * (sum(sizes) * P))
                        offset = offset + turns * sum(sizes) * P
                        at += n * turns
                    else:
                        for i in range(turns):
                            sizes = sizes_all[at:at + n]
                            stream(plan, stage, sizes, i, layer, offset)
                            offset = offset + sum(sizes) * P
                            at += n
                assert at == len(sizes_all)

            with sp.Fori(0, LAYERS) as layer:
                run(LAYER, SLOTS_1, LAYER.stages, layer, layer * W1_TOTAL,
                    ("ada", "gates", "gu", "down"))
            run(SECOND, SLOTS_2, SECOND.stages, 0, LAYERS * W1_TOTAL,
                ("ada", "att", "attout", "ssd", "ssdout"))

            ALL = SECOND.total["slot"]
            def expert_slot(b, n, dst, signal, freed, count):
                e = sp.value_load(expert_of[0:1, ds(b, 1)], min_val=0, max_val=E_N - 1)
                src = w_all[ds(e * EXPERT + (EXPERTS_AT + n * (EXPERT // 3)), EXPERT // 3)]
                sp.wait_ge(freed, count)
                sp.dma_start(dst, src.rearrange("(p n) -> p n", p=P)).then_inc(sem(signal), 16)

            sp.wait_ge(sem("experts_known"), 1)
            expert_slot(0, 0, ring[0], "wg_in", slot_free[0], ALL + 1)
            expert_slot(0, 1, ring[1], "wu_in", slot_free[1], ALL + 1)
            with sp.Fori(1, N_BLK) as b:
                expert_slot(b, 0, ring[0], "wg_in", sem("g_done"), b)
                expert_slot(b - 1, 2, wdown, "wd_in", sem("d_done"), b)
                expert_slot(b, 1, ring[1], "wu_in", sem("u_done"), b)
            expert_slot(N_BLK - 1, 2, wdown, "wd_in", sem("d_done"), N_BLK)

        @block.tensor
        def _(pe):
            for name in ("t_done", "pv_done", "yd_done"):
                pe.sem_inc(sem(name), 2)
            pe.sem_inc(sem("d_done"), 1)

            def hk(k):
                return h[:, k, :]

            def slot_wait(p, use):
                pe.wait_ge(slot_full[p], (use + 1) * 16)

            def product(b, count, w, rhs, kc, m=P):
                pe.wait_ge(lin_free[b], count + 1)
                for k in range(kc):
                    mm = pe.matmul(lin[b][0:m, :], w(k), rhs(k), start=(k == 0), stop=(k == kc - 1))
                mm.then_inc(lin_full[b], 1)

            def packed(p, at, m=P):
                return lambda k: ring[p][:, at + k * m:at + (k + 1) * m]

            def wide(p, ct, n=512):
                return lambda k: ring[p][:, k * n + ct * P:k * n + (ct + 1) * P]

            def ada(plan, c0, i, layer):
                for b in range(2):
                    slot_wait(b, plan.at("ada", "slot", i, layer))
                    pe.wait_ge(lin_free[b], plan.at("ada", "lin", i, layer) + 1)
                    for ct in range(4):
                        for k in range(KC):
                            mm = pe.matmul(lin[b][:, ct:ct + 1], wide(b, ct)(k), csil[:, c0 + k:c0 + k + 1],
                                           start=(k == 0), stop=(k == KC - 1))
                    mm.then_inc(lin_full[b], 1)

            def column_sums(a, src, chunks):
                pe.wait_ge(aux_free, a + 1)
                for k in range(chunks):
                    mm = pe.matmul(aux, ones, src(k), start=(k == 0), stop=(k == chunks - 1))
                mm.then_inc(aux_full, 1)

            def aux_product(a, lhsT, rhs, m=P, n=SEQ):
                pe.wait_ge(aux_free, a + 1)
                pe.matmul(aux[0:m, 0:n], lhsT, rhs, start=True, stop=True).then_inc(aux_full, 1)

            def aux_transposes(a, src, rows, stride):
                pe.wait_ge(aux_free, a + 1)
                hold(pe)
                for t in range(QT):
                    mm = pe.transpose(aux[:, t * stride:t * stride + rows], src[0:rows, t * P:(t + 1) * P],
                                      ident[0:rows, 0:rows])
                mm.then_inc(aux_full, 1)

            def head_norm(a, n):
                pe.wait_ge(sem("sq_done"), n + 1)
                aux_product(a, blockones, sq)

            def rotate(a, src):
                aux_product(a, rope, src)

            def rotate_normed(a, n, dst):
                pe.wait_ge(sem("normed"), n + 1)
                rotate(a, dst)

            def scores(g, bank_use, q, k, w, extra=None):
                h2, i = divmod(g, QT)
                lo = HD * h2
                b = g % 2
                pe.wait_ge(s_free[b], bank_use + 1)
                mm = pe.matmul(sc_b[b][:, 0:w], q[lo:lo + HD, i * P:(i + 1) * P], k[lo:lo + HD, 0:w],
                               start=True, stop=extra is None)
                if extra is not None:
                    mm = pe.matmul(sc_b[b][:, 0:w], extra[0:16, h2, :], negF[0:16, 0:w], start=False, stop=True)
                mm.then_inc(s_full[b], 1)

            def attention(u, s, o, q, k, v, extra=None):
                def turn_over(g):
                    i = g % QT
                    done(pe, "pn_done", u + g)
                    free(pe, "pts_done", u + g)
                    for kt in range(i + 1):
                        mm = pe.transpose(pt_b[g % 2][:, kt * P:(kt + 1) * P], pr[g % 2][:, kt * P:(kt + 1) * P], ident)
                    mm.then_inc(sem("t_done"), 1)

                def values(g):
                    h2, i = divmod(g, QT)
                    done(pe, "pts_done", u + g)
                    if g == 0:
                        pe.wait_ge(o_free, o + 1)
                    for kt in range(i + 1):
                        mm = pe.matmul(ob[HD * h2:HD * h2 + HD, i * P:(i + 1) * P], v(kt, h2),
                                       pts[g % 2][:, kt * P:(kt + 1) * P], start=(kt == 0), stop=(kt == i))
                    mm.then_inc(sem("pv_done"), 1)

                for g in range(2):
                    scores(g, s + g // 2, q, k, P * (g % QT + 1), extra)
                for g in range(8):
                    turn_over(g)
                    if g + 2 < 8:
                        scores(g + 2, s + (g + 2) // 2, q, k, P * ((g + 2) % QT + 1), extra)
                    if g:
                        values(g - 1)
                values(7)

            pe.wait_ge(sem("c_ready"), 1)
            with pe.Fori(0, LAYERS) as layer:
                at = lambda stage, counter, turn=0: LAYER.at(stage, counter, turn, layer)
                with pe.Fori(0, 6) as i:
                    ada(LAYER, 0, i, layer)

                pe.wait_ge(sem("x_squared"), layer * 2 + 1)
                column_sums(at("norm1", "aux"), hk, KC)
                pe.wait_ge(sem("h_ready"), layer * 2 + 1)

                s, l, a, n = at("misc", "slot"), at("misc", "lin"), at("misc", "aux"), at("misc", "nrm")
                r = at("misc", "prep")
                slot_wait(0, s)
                product(0, l, packed(0, 0), hk, KC)
                product(1, l, packed(0, KC * P), hk, KC)
                head_norm(a, n)
                rotate_normed(a + 1, at("misc", "rope"), kaT)
                done(pe, "raw_done", r + 1)
                rotate(a + 2, raw[1])
                slot_wait(1, s)
                product(0, l + 1, packed(1, 0, HD), hk, KC, HD)
                product(1, l + 1, packed(1, KC * HD, 8), hk, KC, 8)
                done(pe, "raw_done", r + 2)
                aux_transposes(a + 3, raw[0], HD, HD)
                done(pe, "raw_done", r + 3)
                aux_transposes(a + 4, raw[1], 8, 8)

                for j in range(4):
                    b = j % 2
                    slot_wait(b, at("idx", "slot") + j // 2)
                    product(b, at("idx", "lin") + j // 2, packed(b, 0), hk, KC)
                    done(pe, "raw_done", at("idx", "prep") + j)
                    rotate(at("idx", "aux") + j, raw[b])
                    done(pe, "prep_done", at("idx", "prep") + j)
                    for g in range(6):
                        h2, i = g // 3, g % 3 + 1
                        pe.wait_ge(s_free[g % 2], at("idx", "s") + 3 * j + g // 2 + 1)
                        pe.matmul(sc_b[g % 2][:, 0:P * (i + 1)], qT[b][HD * h2:HD * h2 + HD, i * P:(i + 1) * P],
                                  kiT[HD * h2:HD * h2 + HD, 0:P * (i + 1)], start=True, stop=True)\
                            .then_inc(s_full[g % 2], 1)

                for j in range(4):
                    b = j % 2
                    slot_wait(b, at("A", "slot") + j // 2)
                    product(b, at("A", "lin") + j // 2, packed(b, 0), hk, KC)
                    head_norm(at("A", "aux") + 2 * j, at("A", "nrm") + j)
                    rotate_normed(at("A", "aux") + 2 * j + 1, at("A", "rope") + j, qT[b])
                    done(pe, "prep_done", at("A", "prep") + j)
                    attention(at("A", "u") + 8 * j, at("A", "s") + 4 * j, at("A", "o") + j, qT[b], kaT,
                              lambda kt, h2: va[:, kt, :])

                for j in range(4):
                    b = j % 2
                    slot_wait(b, at("B", "slot") + j // 2)
                    for n in range(3):
                        t = 3 * j + n
                        product(t % 2, at("B", "lin") + t // 2, packed(b, n * KC * P), hk, KC)
                    for n in range(2):
                        head_norm(at("B", "aux") + 3 * j + n, at("B", "nrm") + 2 * j + n)
                    t = 3 * j + 2
                    done(pe, "raw_done", at("B", "prep") + t)
                    aux_transposes(at("B", "aux") + t, raw[t % 2], P, P)
                    done(pe, "prep_done", at("B", "prep") + t)
                    attention(at("B", "u") + 8 * j, at("B", "s") + 4 * j, at("B", "o") + j, qT[b], kT[b],
                              lambda kt, h2: vtok[b][:, kt, HD * h2:HD * h2 + HD])

                pe.wait_ge(o_free, at("B", "o") + 5)
                hold(pe)
                with pe.Fori(0, 4) as i:
                    for p in range(2):
                        slot_wait(p, at("gates", "slot", i))
                        l = at("gates", "lin", i) + 2 * p
                        product(0, l, packed(p, 0), hk, KC)
                        product(1, l, packed(p, KC * P), hk, KC)
                        product(0, l + 1, packed(p, 2 * KC * P), lambda k: attA[:, k, :], 4)
                        product(1, l + 1, packed(p, 2 * KC * P + 4 * P), lambda k: attB[:, k, :], 4)
                pe.wait_ge(sem("merged_done"), layer + 1)
                for t in range(8):
                    if t % 4 == 0:
                        slot_wait(t // 4, at("out", "slot"))
                    product(t % 2, at("out", "lin") + t // 2, wide(t // 4, t % 4), lambda k: merged[:, k, :], KC)

                pe.wait_ge(sem("x_squared"), layer * 2 + 2)
                column_sums(at("norm2", "aux"), hk, KC)
                pe.wait_ge(sem("h_ready"), layer * 2 + 2)
                hold(pe)
                with pe.Fori(0, 11) as i:
                    for p in range(2):
                        slot_wait(p, at("gu", "slot", i))
                        product(0, at("gu", "lin", i) + p, packed(p, 0), hk, KC)
                        product(1, at("gu", "lin", i) + p, packed(p, KC * P), hk, KC)
                pe.wait_ge(sem("hid_done"), layer + 1)
                hold(pe)
                with pe.Fori(0, 4) as i:
                    for p in range(2):
                        slot_wait(p, at("down", "slot", i))
                        product(p, at("down", "lin", i), packed(p, 0), lambda k: hid[:, k, :], FF_T)

            at = lambda stage, counter, turn=0: SECOND.at(stage, counter, turn)
            H0 = 2 * LAYERS

            def layer_norm(stage, n):
                pe.wait_ge(sem("x_ready"), 5 + n)
                column_sums(at(stage, "aux"), lambda k: x[:, k, :], KC)
                pe.wait_ge(sem("centred_squared"), n + 1)
                column_sums(at(stage, "aux") + 1, lambda k: merged2[:, k, :], KC)

            with pe.Fori(0, 6) as i:
                ada(SECOND, 8, i, 0)
            layer_norm("ln1", 0)
            pe.wait_ge(sem("h_ready"), H0 + 1)

            slot_wait(0, at("fd", "slot"))
            product(0, at("fd", "lin"), packed(0, 0, 16), hk, KC, 16)
            slot_wait(1, at("fd", "slot"))
            product(1, at("fd", "lin"), packed(1, 0, 32), hk, KC, 32)
            pe.wait_ge(sem("f_done"), 1)
            aux_transposes(at("fd", "aux"), negF, 16, 16)
            pe.wait_ge(sem("acs_done"), 1)
            aux_transposes(at("fd", "aux") + 1, dtT, 32, 32)
            aux_transposes(at("fd", "aux") + 2, acs, 32, 32)
            pe.wait_ge(sem("acs_tok_done"), 1)
            aux_product(at("fd", "aux") + 3, last, acs_tok.rearrange("p a b -> p (a b)"), P, QT * 32)

            with pe.Fori(0, 4) as i:
                for b in range(2):
                    slot_wait(b, at("att", "slot", i))
                    for n in range(3):
                        t = 3 * b + n
                        product(t % 2, at("att", "lin", i) + t // 2, packed(b, n * KC * P), hk, KC)
                    t = 3 * b + 2
                    done(pe, "raw_done", at("att", "prep", i) + t)
                    aux_transposes(at("att", "aux", i) + b, raw[t % 2], P, P)
                    done(pe, "prep_done", at("att", "prep", i) + t)
                    attention(at("att", "u", i) + 8 * b, at("att", "s", i) + 4 * b, at("att", "o", i) + b,
                              qT[b], kT[b], lambda kt, h2: vtok[b][:, kt, HD * h2:HD * h2 + HD], fsel[b])
            pe.wait_ge(o_free, at("att", "o") + 9)
            with pe.Fori(0, 4) as i:
                for p in range(2):
                    slot_wait(p, at("attout", "slot", i))
                    product(0, at("attout", "lin", i) + p, packed(p, 0), hk, KC)
                    product(1, at("attout", "lin", i) + p, packed(p, KC * P), lambda k: att2[:, k, :], KC)

            for g in range(4):
                l = at("pool", "lin", g)
                slot_wait(0, at("pool", "slot", g))
                product(0, l, wide(0, 0, 256), hk, KC)
                product(1, l, wide(0, 1, 256), hk, KC)
                slot_wait(1, at("pool", "slot", g))
                product(0, l + 1, wide(1, 0, 256), hk, KC)
                pe.wait_ge(sem("pooled_done"), g + 1)
                wp = lambda ct: (lambda k: ring[1][:, KC * 256 + k * 256 + ct * P:KC * 256 + k * 256 + (ct + 1) * P])
                product(1, l + 1, wp(0), lambda k: pooled[k], 2)
                product(0, l + 2, wide(1, 1, 256), hk, KC)
                product(1, l + 2, wp(1), lambda k: pooled[k], 2)

            with pe.Fori(0, 4) as i:
                l, s = at("ssd", "lin", i), at("ssd", "slot", i)
                slot_wait(0, s)
                for t in range(4):
                    product(t % 2, l + t // 2, wide(0, t), hk, KC)
                slot_wait(1, s)
                for t in range(2):
                    product(t, l + 2, wide(1, t, 256), hk, KC)
                done(pe, "silu_done", i * 6 + 3)
                for c in range(QT):
                    free(pe, "xd_done", i * 4 + c)
                    for t in range(4):
                        mm = pe.transpose(pt_b[c % 2][:, t * P:(t + 1) * P], xsT[:, t, c * P:(c + 1) * P], ident)
                    mm.then_inc(sem("xt_done"), 1)
                done(pe, "silu_done", i * 6 + 5)
                pe.wait_ge(sem("yp_done"), i * 4 + 1)
                for c in range(QT):
                    mm = pe.transpose(ob[:, c * P:(c + 1) * P], bmT[:, c * P:(c + 1) * P], ident)
                mm.then_inc(sem("bt_done"), 1)
                done(pe, "seg_done", i * 8 - 1)
                for c in range(QT):
                    mm = pe.matmul(sc_b[0][:, c * P:(c + 1) * P], bmT[:, c * P:(c + 1) * P],
                                   cmT[:, c * P:(c + 1) * P], start=True, stop=True)
                mm.then_inc(sem("cb_done"), 1)
                pe.wait_ge(sem("btok_done"), i + 1)
                done(pe, "xd_done", i * 4 + 3)
                for c in range(3):
                    if c == 2:
                        pe.wait_ge(sem("hst_done"), i * 3 + 1)
                    pe.matmul(pt_b[c % 2], btok[:, c, :], xde[:, c, :], start=True, stop=True)\
                        .then_inc(sem("st_done"), 1)
                pe.wait_ge(sem("cbm_done"), i + 1)

                def decay_row(hh):
                    free(pe, "seg_done", i * 8 + hh)
                    pe.matmul(sc_b[hh % 2], selh[0:32, hh, :], acs[0:32, :], start=True, stop=True)\
                        .then_inc(sem("bc_done"), 1)

                decay_row(0)
                decay_row(1)
                pe.wait_ge(sem("hst_done"), i * 3 + 3)
                for j in range(4):
                    pe.wait_ge(sem("yp_done"), i * 4 + j + 1)
                    pe.matmul(pt_b[1], selp[0:32, j, :], acs[0:32, :], start=True, stop=True)\
                        .then_inc(sem("eab_done"), 1)
                    for h2 in range(2):
                        for c in range(3):
                            mm = pe.matmul(pt_b[0][HD * h2:HD * h2 + HD, (c + 1) * P:(c + 2) * P],
                                           hst[:, c, (2 * j + h2) * HD:(2 * j + h2 + 1) * HD],
                                           cmT[:, (c + 1) * P:(c + 2) * P], start=True, stop=True)
                    mm.then_inc(sem("yoff_done"), 1)
                    for h2 in range(2):
                        hh = 2 * j + h2
                        done(pe, "wgt_done", i * 8 + hh)
                        for c in range(QT):
                            mm = pe.matmul(ob[HD * h2:HD * h2 + HD, c * P:(c + 1) * P],
                                           xdt[:, c, hh * HD:(hh + 1) * HD], wgt[hh % 2][:, c * P:(c + 1) * P],
                                           start=True, stop=True)
                        mm.then_inc(sem("yd_done"), 1)
                        if hh + 2 < 8:
                            decay_row(hh + 2)
                slot_wait(0, s + 1)
                for t in range(2):
                    product(t, l + 3, wide(0, t, 256), hk, KC)
                slot_wait(1, s + 1)
                for t in range(2):
                    product(t, l + 4, wide(1, t, 256), hk, KC)
                pe.wait_ge(sem("yg_squared"), i + 1)
                column_sums(at("ssd", "aux", i), lambda k: xdt[:, k, :], 4)

            pe.wait_ge(sem("yT_done"), 4)
            with pe.Fori(0, 4) as i:
                for p in range(2):
                    slot_wait(p, at("ssdout", "slot", i))
                    product(0, at("ssdout", "lin", i) + p, packed(p, 0), hk, KC)
                    product(1, at("ssdout", "lin", i) + p, packed(p, KC * P), lambda k: yT[:, k, :], 16)
            pe.wait_ge(sem("merged2_done"), 1)
            for t in range(8):
                if t % 4 == 0:
                    slot_wait(t // 4, at("out", "slot"))
                product(t % 2, at("out", "lin") + t // 2, wide(t // 4, t % 4), lambda k: merged2[:, k, :], KC)
            layer_norm("ln2", 1)
            layer_norm("ln3", 2)
            pe.wait_ge(sem("h_ready"), H0 + 2)

            pe.wait_ge(aux_free, at("router", "aux") + 1)
            for t in range(QT):
                for k in range(KC):
                    mm = pe.matmul(aux[:, t * E_N:(t + 1) * E_N], h[:, k, t * P:(t + 1) * P],
                                   v2("w_router", k * E_N, E_N), start=(k == 0), stop=(k == KC - 1))
            mm.then_inc(aux_full, 1)
            a = at("router", "aux")
            for t in range(QT):
                for half in range(2):
                    n = 2 * t + half
                    if n >= 4:
                        pe.wait_ge(sem("htok_done"), n - 3)
                    bank = (sc_b, pt_b)[half][t % 2]
                    for k in range(4):
                        mm = pe.transpose(bank[:, k * P:(k + 1) * P], h[:, 4 * half + k, t * P:(t + 1) * P], ident)
                    mm.then_inc(sem("ht_done"), 1)
            pe.wait_ge(sem("chosen"), 1)
            pe.wait_ge(aux_free, a + 2)
            for t in range(QT):
                mm = pe.transpose(aux[0:E_N, t * P:(t + 1) * P], gw[:, t, :], ident)
            mm.then_inc(aux_full, 1)
            pe.wait_ge(sem("blocks_counted"), 1)
            pe.wait_ge(aux_free, a + 3)
            pe.matmul(aux[0:E_N, 0:1], tri[0:E_N, 0:E_N], n_blocks[0:E_N, :], start=True, stop=True)\
                .then_inc(aux_full, 1)
            pe.wait_ge(sem("past_done"), 1)
            pe.wait_ge(aux_free, a + 4)
            pe.matmul(aux[:, 0:N_BLK], ones[0:E_N, :], past[0:E_N, :], start=True, stop=True).then_inc(aux_full, 1)
            pe.wait_ge(sem("position_done"), 1)
            pe.wait_ge(aux_free, a + 5)
            for t in range(QT):
                mm = pe.transpose(aux[:, t * E_N:(t + 1) * E_N], position[0:E_N, t * P:(t + 1) * P],
                                  ident[0:E_N, 0:E_N])
            mm.then_inc(aux_full, 1)

            def rows_in(b):
                pe.wait_ge(sem("rows_in"), b * 16 + 16)
                for k in range(KC):
                    mm = pe.transpose(pt_b[k // 4][:, (k % 4) * P:(k % 4 + 1) * P], xr[:, k * P:(k + 1) * P], ident)
                mm.then_inc(sem("rows_turned"), 1)

            def up_products(w, par, bank, signal):
                for ct in range(4):
                    for k in range(KC):
                        mm = pe.matmul(bank[:, ct * P:(ct + 1) * P],
                                       w[:, k * E_FF + ct * P:k * E_FF + (ct + 1) * P],
                                       xT[par][:, k * P:(k + 1) * P], start=(k == 0), stop=(k == KC - 1))
                mm.then_inc(sem(signal), 1)

            def gate_block(b, par):
                pe.wait_ge(sem("wg_in"), b * 16 + 16)
                pe.wait_ge(sem("xTa_done"), b + 1)
                pe.wait_ge(sem("xTd_done"), b + 1)
                up_products(ring[0], par, lin[0], "g_done")

            def up_block(b, par):
                pe.wait_ge(sem("wu_in"), b * 16 + 16)
                up_products(ring[1], par, lin[1], "u_done")

            def down_block(b):
                pe.wait_ge(sem("wd_in"), b * 16 + 16)
                pe.wait_ge(sem("hidden"), b + 1)
                pe.wait_ge(sem("ya_done"), b + 1)
                pe.wait_ge(sem("yd2_done"), b + 1)
                for half in range(2):
                    for k in range(4):
                        mm = pe.matmul(sc_b[half], hidb[:, k * P:(k + 1) * P],
                                       wdown[:, k * D + half * SEQ:k * D + (half + 1) * SEQ],
                                       start=(k == 0), stop=(k == 3))
                mm.then_inc(sem("d_done"), 1)

            for p in range(2):
                pe.wait_ge(lin_free[p], SECOND.total["lin"] + 1)
            pe.wait_ge(sem("htok_done"), 2 * QT)
            rows_in(0)
            gate_block(0, 0)
            rows_in(1)
            up_block(0, 0)
            with pe.Fori(0, (N_BLK - 1) // 2) as i:
                for n in range(2):
                    b, par = 2 * i + (n + 1), (n + 1) % 2
                    pe.wait_ge(sem("silu_read"), b)
                    gate_block(b, par)
                    down_block(b - 1)
                    rows_in(b + 1)
                    up_block(b, par)
            down_block(N_BLK - 1)

            for t in range(QT):
                pe.wait_ge(sem("combined"), t + 1)
                if t >= 2:
                    pe.wait_ge(sem("ffn_done"), 2 * t - 2)
                elif t == 0:
                    pe.wait_ge(sem("ya_done"), N_BLK + 1)
                    pe.wait_ge(sem("yd2_done"), N_BLK + 1)
                    pe.wait_ge(sem("xTa_done"), N_BLK + 1)
                    pe.wait_ge(sem("xTd_done"), N_BLK + 1)
                for half in range(2):
                    bank = (sc_b, pt_b)[half][t % 2]
                    for k in range(4):
                        mm = pe.transpose(bank[:, k * P:(k + 1) * P],
                                          htok[:, t, (4 * half + k) * P:(4 * half + k + 1) * P], ident)
                    mm.then_inc(sem("turned_back"), 1)
            layer_norm("ln4", 3)

        @block.scalar
        def _(act):
            mine = Steps(act, sem("act_steps"))
            tell = mine.tell
            for dst, src in ((cst[:, :], consts), (csil[:, :], cond), (raw[0].bitcast(I32), pos_in),
                             (x[:, :, :], x_in), (vec2[:, :], vec2_all)):
                act.dma_start(dst, src).then_inc(boot, 16)
            for s in (slot_free[0], slot_free[1], o_free):
                act.sem_inc(s, 1)
            for name in ("exp_done", "pts_done", "raw_done", "rl_done", "silu_done"):
                act.sem_inc(sem(name), 2)
            act.sem_inc(sem("ya_done"), 1)

            act.wait_ge(boot, 80)
            tell(act.activation(csil[:, :], csil[:, :], ACT.Silu), sem("c_ready"))
            act.wait_ge(sem("angle_done"), 1)
            mine(act.activation(sinT[:, :], tmp[:, :], ACT.Sin))
            tell(act.activation(cosT[:, :], tmp[:, :], ACT.Sin, scale=0.5), sem("sin_done"))

            def root(out, scale, eps, a):
                act.wait_ge(aux_full, a + 1)
                tell(act.activation(out, aux, ACT.Sqrt, scale=scale, bias=eps), sem("root_done"))

            def affine(dst, scaled, scale, shift, signal):
                for k in range(KC):
                    act.wait_ge(sem("scaled"), scaled + k + 1)
                    mine(act.activation(dst[:, k, :], dst[:, k, :], ACT.Identity, scale=scale(k), bias=shift(k)))
                act.sem_inc(signal, 1)

            def rms_norm(n, a, gain0, shift0):
                act.wait_ge(sem("x_ready"), n + 1)
                for half in range(2):
                    mine(act.activation(h[:, 4 * half:4 * half + 4, :], x[:, 4 * half:4 * half + 4, :], ACT.Square))
                act.sem_inc(sem("x_squared"), 1)
                root(rstd[:, :], 1.0 / D, EPS, a)
                affine(h, n * KC, lambda k: gain[:, gain0 + k:gain0 + k + 1],
                       lambda k: mod[:, shift0 + k:shift0 + k + 1], sem("h_ready"))

            def take_tile(b, count, slot=None):
                act.wait_ge(lin_full[b], count + 1)
                if slot is not None:
                    act.sem_inc(slot_free[slot], 1)

            def project(b, count, r, par, bias, m=P, slot=None, dst=None, scale=1.0):
                take_tile(b, count, slot)
                free(act, "prep_done", r)
                dst = raw[par] if dst is None else dst
                tell(act.activation(dst[0:m, :], lin[b][0:m, :], ACT.Identity, bias=bias, scale=scale), sem("raw_done"))

            def head_root(a):
                act.wait_ge(aux_full, a + 1)
                tell(act.activation(rs[:, :], aux, ACT.Sqrt, scale=1.0 / HD, bias=EPS), sem("rs_done"))

            def attention(u, dst):
                def evacuate(g):
                    w = P * (g % QT + 1)
                    done(act, "t_done", u + g)
                    free(act, "pv_done", u + g)
                    tell(act.activation(pts[g % 2][:, 0:w], pt_b[g % 2][:, 0:w], ACT.Copy), sem("pts_done"))

                for g in range(8):
                    w = P * (g % QT + 1)
                    done(act, "nmax_done", u + g)
                    free(act, "t_done", u + g)
                    tell(act.activation(pr[g % 2][:, 0:w], sm[g % 2][:, 0:w], ACT.Exp, bias=nmax[:, g:g + 1],
                                   accum_out=esum[:, g:g + 1]), sem("exp_done"))
                    if g:
                        evacuate(g - 1)
                evacuate(7)
                done(act, "pv_done", u + 7)
                tell(act.activation(dst, ob, ACT.Copy), o_free)

            def gate(b, count, n, par, func, bias=0.0, slot=None):
                take_tile(b, count, slot)
                act.wait_ge(sem("sg_free"), n + 1)
                tell(act.activation(sg[par][:, :], lin[b], func, bias=bias), sem("sg_done"))

            with mine.loop(0, LAYERS) as layer:
                at = lambda stage, counter, turn=0: LAYER.at(stage, counter, turn, layer)
                act.dma_start(vec[:, :], vec1_all[ds(layer * (P * NV1), P * NV1)].rearrange("(p n) -> p n", p=P))\
                    .then_inc(vec_in, 16)
                act.dma_start(relb, rel[ds(layer * (P * 8 * SEQ), P * 8 * SEQ)]
                              .rearrange("(p a b) -> p a b", p=P, a=8)).then_inc(rel_in, 16)
                act.wait_ge(vec_in, layer * 16 + 16)
                rms_norm(layer * 2, at("norm1", "aux"), 0, 0)

                l, r = at("misc", "lin"), at("misc", "prep")
                project(0, l, r, 0, v1("ka"))
                project(1, l, r + 1, 1, v1("ki"), slot=0)
                head_root(at("misc", "aux"))
                project(0, l + 1, r + 2, 0, v1("va")[0:HD], HD)
                project(1, l + 1, r + 3, 1, v1("wi")[0:8], 8, slot=1)

                for j in range(4):
                    b = j % 2
                    project(b, at("idx", "lin") + j // 2, at("idx", "prep") + j, b, v1("qi", j), slot=b)
                    for g in range(6):
                        w = P * (g % 3 + 2)
                        act.wait_ge(s_full[g % 2], at("idx", "s") + 3 * j + g // 2 + 1)
                        free(act, "acc_done", at("idx", "iu") + 6 * j + g)
                        tell(act.activation(sm[g % 2][:, 0:w], sc_b[g % 2][:, 0:w], ACT.Relu), sem("rl_done"))

                for j in range(4):
                    b = j % 2
                    project(b, at("A", "lin") + j // 2, at("A", "prep") + j, b, v1("qa", j), slot=b)
                    head_root(at("A", "aux") + 2 * j)
                    attention(at("A", "u") + 8 * j, attA[:, j, :])

                for j in range(4):
                    l, r = at("B", "lin"), at("B", "prep")
                    t = 3 * j
                    project(t % 2, l + t // 2, r + t, t % 2, v1("qb", j))
                    project((t + 1) % 2, l + (t + 1) // 2, r + t + 1, (t + 1) % 2, v1("kb", j))
                    head_root(at("B", "aux") + t)
                    head_root(at("B", "aux") + t + 1)
                    project(t % 2, l + (t + 2) // 2, r + t + 2, t % 2, v1("vb", j), slot=j % 2)
                    attention(at("B", "u") + 8 * j, attB[:, j, :])

                with mine.loop(0, 4) as i:
                    for p in range(2):
                        l, n = at("gates", "lin", i) + 2 * p, at("gates", "sg", i) + 2 * p
                        gate(0, l, n, 0, ACT.Sigmoid, v1d("ga", 2 * i + p))
                        gate(1, l, n + 1, 1, ACT.Sigmoid, v1d("gb", 2 * i + p))
                rms_norm(layer * 2 + 1, at("norm2", "aux"), 8, 24)
                with mine.loop(0, 11) as i:
                    for p in range(2):
                        gate(0, at("gu", "lin", i) + p, at("gu", "sg", i) + p, p, ACT.Silu)

            at = lambda stage, counter, turn=0: SECOND.at(stage, counter, turn)
            SC0 = 2 * LAYERS * KC

            def layer_norm(stage, n, dst, scale, shift, signal):
                act.wait_ge(sem("centred"), n + 1)
                tell(act.activation(merged2, dst[:, :, :], ACT.Square), sem("centred_squared"))
                root(rstd[:, :], 1.0 / D, LN_EPS, at(stage, "aux") + 1)
                affine(dst, SC0 + n * KC, scale, shift, signal)

            mod_at = lambda k0: (lambda k: mod[:, k0 + k:k0 + k + 1])
            gain_at = lambda k0: (lambda k: gain[:, k0 + k:k0 + k + 1])
            v2_at = lambda name: (lambda k: v2(name, k))
            layer_norm("ln1", 0, h, gain_at(0), mod_at(0), sem("h_ready"))

            for n, (m, bias) in enumerate(((16, v2("b_forget")[0:16]), (32, v2("dt_bias")[0:32]))):
                take_tile(n, at("fd", "lin"), slot=n)
                tell(act.activation(raw[n][0:m, :], lin[n][0:m, :], ACT.Identity, bias=bias), sem("fd_raw"))
                act.wait_ge(sem("fd_raw"), n + 1)
                tell(act.activation(sm[n][0:m, :], raw[n][0:m, :], ACT.Abs), sem("fd_act"))
                act.wait_ge(sem("fd_act"), 3 * n + 1)
                tell(act.activation(sm[n][0:m, :], sm[n][0:m, :], ACT.Exp, scale=-1.0), sem("fd_act"))
                act.wait_ge(sem("fd_act"), 3 * n + 2)
                tell(act.activation(sm[n][0:m, :], sm[n][0:m, :], ACT.Ln, bias=1.0), sem("fd_act"))
            tell(act.activation(gain[0:32, 0:1], v2("a_log")[0:32], ACT.Exp), sem("a_done"))
            act.wait_ge(aux_full, at("fd", "aux") + 4)
            tell(act.activation(cd_tok.rearrange("p a b -> p (a b)"), aux[:, 0:QT * 32], ACT.Exp), sem("cd_done"))
            act.wait_ge(sem("te_diff"), 1)
            tell(act.activation(te_tok, te_tok, ACT.Exp), sem("te_exp"))

            with mine.loop(0, 4) as i:
                for b in range(2):
                    l, r = at("att", "lin", i), at("att", "prep", i) + 3 * b
                    for n, dst in enumerate((qT[b], kT[b], raw[b])):
                        t = 3 * b + n
                        project(t % 2, l + t // 2, r + n, b, 0.0, slot=b if n == 2 else None, dst=dst,
                                scale=HD ** -0.5 if n == 0 else 1.0)
                    attention(at("att", "u", i) + 8 * b, att2[:, ds(2 * i + b, 1), :])
            with mine.loop(0, 4) as i:
                for p in range(2):
                    gate(0, at("attout", "lin", i) + p, at("attout", "sg", i) + p, p, ACT.Sigmoid)
            for g in range(4):
                l = at("pool", "lin", g)
                for t in range(2):
                    take_tile(t, l, slot=0 if t == 1 else None)
                    act.wait_ge(sem("ub_free"), 2 * g + t + 1)
                    tell(act.activation(ub[t][:, 16:16 + SEQ], lin[t], ACT.Copy), sem("ub_done"))
                gate(0, l + 1, at("pool", "sg", g), 0, ACT.Sigmoid)
                gate(0, l + 2, at("pool", "sg", g) + 1, 1, ACT.Sigmoid)

            with mine.loop(0, 4) as i:
                l = at("ssd", "lin", i)

                def conv_in(t):
                    take_tile(t % 2, l + t // 2, slot={3: 0, 5: 1}.get(t))
                    free(act, "conv_done", i * 6 + t)
                    tell(act.activation(cin[t % 2][:, 3:], lin[t % 2], ACT.Copy), sem("cin_done"))

                def conv_out(t):
                    done(act, "conv_done", i * 6 + t)
                    dst = xsT[:, t, :] if t < 4 else (bmT, cmT)[t - 4]
                    tell(act.activation(dst, cv[t % 2], ACT.Silu, bias=gpar[:, 5 * t + 4:5 * t + 5]), sem("silu_done"))

                act.wait_ge(sem("gpar_done"), i + 1)
                for t in range(6):
                    conv_in(t)
                    if t:
                        conv_out(t - 1)
                conv_out(5)
                for j in range(4):
                    act.wait_ge(sem("eab_done"), i * 4 + j + 1)
                    act.wait_ge(sem("yp_done"), i * 4 + j + 1)
                    tell(act.activation(ea, pt_b[1], ACT.Exp), sem("ea_done"))
                    for hh in (2 * j, 2 * j + 1):
                        done(act, "seg_done", i * 8 + hh)
                        tell(act.activation(seg[hh % 2], seg[hh % 2], ACT.Exp), sem("e_done"))
                for t in range(4):
                    gate(t % 2, l + 3 + t // 2, at("ssd", "sg", i) + t, t % 2, ACT.Silu,
                         slot={1: 0, 3: 1}.get(t))
                act.wait_ge(sem("yz_done"), i + 1)
                tell(act.activation(xdt, yg, ACT.Square), sem("yg_squared"))
                root(rstd[:, :], 1.0 / SEQ, EPS, at("ssd", "aux", i))
            with mine.loop(0, 4) as i:
                for p in range(2):
                    gate(0, at("ssdout", "lin", i) + p, at("ssdout", "sg", i) + p, p, ACT.Sigmoid)

            layer_norm("ln2", 1, x, v2_at("ln_mix_g"), v2_at("ln_mix_b"), sem("x_ready"))
            layer_norm("ln3", 2, h, gain_at(8), mod_at(24), sem("h_ready"))
            act.wait_ge(sem("logit_done"), 1)
            tell(act.activation(rt[0], rt[0], ACT.Exp), sem("probs_exp"))
            for t in range(QT):
                for half in range(2):
                    act.wait_ge(sem("ht_done"), 2 * t + half + 1)
                    tell(act.activation(htok[:, t, half * SEQ:(half + 1) * SEQ], (sc_b, pt_b)[half][t % 2], ACT.Copy),
                         sem("htok_done"))

            def rows_half(b, par):
                act.wait_ge(sem("rows_turned"), b + 1)
                tell(act.activation(xT[par][:, 0:SEQ], pt_b[0], ACT.Copy), sem("xTa_done"))

            def gate_half(b):
                act.wait_ge(sem("g_done"), b + 1)
                tell(act.activation(sg[0][:, :], lin[0], ACT.Silu), sem("silu_read"))

            def made_half(b, par, first=False):
                act.wait_ge(sem("d_done"), b + 2)
                if not first:
                    act.wait_ge(sem("made_out"), (b - 1) * 16)
                tell(act.activation(yb[par][:, 0:SEQ], sc_b[0], ACT.Copy), sem("ya_done"))

            rows_half(0, 0)
            gate_half(0)
            rows_half(1, 1)

            def step(b, par, first=False):
                act.wait_ge(sem("hidden"), b)
                gate_half(b)
                made_half(b - 1, 1 - par, first)
                rows_half(b + 1, 1 - par)

            for b in (1, 2):
                step(b, b % 2, True)
            with mine.loop(1, (N_BLK - 1) // 2) as i:
                for n in range(2):
                    step(2 * i + (n + 1), (n + 1) % 2)
            made_half(N_BLK - 1, (N_BLK - 1) % 2)
            for t in range(QT):
                for half in range(2):
                    act.wait_ge(sem("turned_back"), 2 * t + half + 1)
                    tell(act.activation(moe[:, 4 * half:4 * half + 4, t * P:(t + 1) * P],
                                        (sc_b, pt_b)[half][t % 2].rearrange("p (a b) -> p a b", b=P), ACT.Copy),
                         sem("ffn_done"))
            layer_norm("ln4", 3, x, v2_at("ln_ffn_g"), v2_at("ln_ffn_b"), sem("x_final"))
            act.wait_ge(sem("x_final"), 1)
            act.dma_start(out, x[:, :, :]).then_inc(out_done, 16)
            act.wait_ge(out_done, 16)

        @block.vector
        def _(dve):
            mine = Steps(dve, sem("dve_steps"))
            tell = mine.tell
            TT, TS, STT = dve.tensor_tensor, dve.tensor_scalar, dve.scalar_tensor_tensor
            MUL, ADD, SUB, MAX, MIN = ALU.mult, ALU.add, ALU.subtract, ALU.max, ALU.min

            for s in (lin_free[0], lin_free[1], aux_free, s_free[0], s_free[1], sem("yp_done")):
                dve.sem_inc(s, 1)
            for name in ("nmax_done", "prep_done", "acc_done", "conv_done", "seg_done", "xd_done", "sg_free",
                         "ub_free"):
                dve.sem_inc(sem(name), 2)
            dve.sem_inc(sem("yd2_done"), 1)

            TWO_PI = 2 * np.pi
            c1 = 6.28125
            c2 = float(np.float32(np.round((TWO_PI - c1) * 2 ** 20) / 2 ** 20))
            c3 = float(TWO_PI - c1 - c2)
            MAGIC = 1.5 * 2 ** 23
            ang, turns = sm[0], sm[1]
            dve.wait_ge(boot, 80)
            dve.sem_inc(sem("x_ready"), 1)
            mine(dve.tensor_copy(ang, raw[0].bitcast(I32)))
            mine(TS(ang, ang, col("inv_freq"), None, MUL))
            mine(TS(turns, ang, 1 / TWO_PI, MAGIC, MUL, ADD))
            mine(TS(turns, turns, MAGIC, None, SUB))
            for c in (c1, c2, c3):
                mine(STT(ang, turns, -c, ang, MUL, ADD))
            PI = 3.1415925
            tell(TS(tmp[:, :], ang, PI, -PI, MIN, MAX), sem("angle_done"))
            dve.wait_ge(sem("sin_done"), 1)
            mine(TT(cosT[:, :], cosT[:, :], cosT[:, :], MUL))
            mine(TS(cosT[:, :], cosT[:, :], -2.0, 1.0, MUL, ADD))
            mine.restart()

            def lin_wait(b, count):
                dve.wait_ge(lin_full[b], count + 1)

            def ada(plan, bias, i, layer):
                for b in range(2):
                    lin_wait(b, plan.at("ada", "lin", i, layer))
                    dve.sem_inc(slot_free[b], 1)
                    k0 = 8 * i + 4 * b
                    tell(TT(mod[:, ds(k0, 4)], lin[b][:, 0:4], bias("b_ada", k0, 4), ADD), lin_free[b])

            def gains(g_mix, g_ffn, signal, lin_counts):
                for b in range(2):
                    dve.wait_ge(lin_free[b], lin_counts + 1)
                for at0, k0, g in ((0, 8, g_mix), (8, 32, g_ffn)):
                    if g is None:
                        ins = TS(gain[:, at0:at0 + 8], mod[:, k0:k0 + 8], 1.0, None, ADD)
                    else:
                        ins = STT(gain[:, at0:at0 + 8], mod[:, k0:k0 + 8], 1.0, g, ADD, MUL)
                    mine(ins)

            def scale_tiles(dst, src, n_root, n_aux_free=True):
                dve.wait_ge(sem("root_done"), n_root + 1)
                tell(dve.reciprocal(rstd[:, :], rstd[:, :]), aux_free)

            def rms_norm(n, a, n_root):
                dve.wait_ge(sem("root_done"), n_root + 1)
                tell(dve.reciprocal(rstd[:, :], rstd[:, :]), aux_free)
                dve.wait_ge(aux_free, a + 2)
                for k in range(KC):
                    tell(TT(h[:, k, :], x[:, k, :], rstd[:, :], MUL), sem("scaled"))

            def layer_norm(stage, n, dst, n_root):
                a = SECOND.at(stage, "aux")
                dve.wait_ge(aux_full, a + 1)
                tell(TS(tmp[:, :], aux, 1.0 / D, None, MUL), aux_free)
                dve.wait_ge(aux_free, a + 2)
                tell(TT(dst[:, :, :], x[:, :, :], tmp[:, :].unsqueeze(1).broadcast_to([P, KC, SEQ]), SUB), sem("centred"))
                dve.wait_ge(sem("root_done"), n_root + 1)
                tell(dve.reciprocal(rstd[:, :], rstd[:, :]), aux_free)
                dve.wait_ge(aux_free, a + 3)
                for k in range(KC):
                    tell(TT(dst[:, k, :], dst[:, k, :], rstd[:, :], MUL), sem("scaled"))

            def norm_tile(a, n, r, par, b, count, dst, g, final):
                done(dve, "raw_done", r)
                dve.sem_inc(lin_free[b], 1)
                tell(TT(sq[:, :], raw[par], raw[par], MUL), sem("sq_done"))

            def norm_tile_end(a, n, par, dst, g, signal):
                dve.wait_ge(sem("rs_done"), n + 1)
                tell(dve.reciprocal(rs[:, :], rs[:, :]), aux_free)
                dve.wait_ge(aux_free, a + 2)
                tell(STT(dst, raw[par], g, rs[:, :], MUL, MUL), signal)

            def rotate(a, src, dst):
                dve.wait_ge(aux_full, a + 1)
                tell(TT(tmp[:, :], aux, sinT[:, :], MUL), aux_free)
                mine(TT(dst, src, cosT[:, :], MUL))
                dve.wait_ge(aux_free, a + 2)
                tell(TT(dst, dst, tmp[:, :], ADD), sem("prep_done"))

            def take_transposed(a, dst, src):
                dve.wait_ge(aux_full, a + 1)
                tell(dve.tensor_copy(dst, src), aux_free)
                dve.wait_ge(aux_free, a + 2)
                dve.sem_inc(sem("prep_done"), 1)

            def attention(u, s, masked):
                def reciprocal(g):
                    done(dve, "exp_done", u + g)
                    tell(dve.reciprocal(rcp[:, g:g + 1], esum[:, g:g + 1]), sem("rcp_done"))

                for g in range(8):
                    b, w = g % 2, P * (g % QT + 1)
                    dve.wait_ge(s_full[b], s + g // 2 + 1)
                    free(dve, "exp_done", u + g)
                    tell(masked(g, b, w), s_free[b])
                    dve.wait_ge(s_free[b], s + g // 2 + 2)
                    tell(dve.tensor_reduce(nmax[:, g:g + 1], sm[b][:, 0:w], AX.X, MAX, negate=True), sem("nmax_done"))
                    if g:
                        reciprocal(g - 1)
                reciprocal(7)

            with mine.loop(0, LAYERS) as layer:
                at = lambda stage, counter, turn=0: LAYER.at(stage, counter, turn, layer)
                dve.wait_ge(vec_in, layer * 16 + 16)
                hold(dve)
                with mine.loop(0, 6) as i:
                    ada(LAYER, v1d, i, layer)
                gains(v1("g_mix", 0, 8), v1("g_ffn", 0, 8), None, at("norm1", "lin"))
                rms_norm(layer * 2, at("norm1", "aux"), layer * 2)
                dve.wait_ge(rel_in, layer * 16 + 16)
                mine(dve.memset(relb[0:HD, :, SEQ - HD:SEQ], NEG))

                a, r = at("misc", "aux"), at("misc", "prep")
                done(dve, "raw_done", r)
                dve.sem_inc(lin_free[0], 1)
                tell(TT(sq[:, :], raw[0], raw[0], MUL), sem("sq_done"))
                norm_tile_end(a, at("misc", "nrm"), 0, kaT, v1("kn_a"), sem("normed"))
                dve.wait_ge(sem("normed"), at("misc", "rope") + 1)
                rotate(a + 1, kaT, kaT)
                done(dve, "raw_done", r + 1)
                dve.sem_inc(lin_free[1], 1)
                rotate(a + 2, raw[1], kiT)
                done(dve, "raw_done", r + 2)
                dve.sem_inc(lin_free[0], 1)
                take_transposed(a + 3, va, aux[:, 0:QT * HD].rearrange("p (a b) -> p a b", b=HD))
                done(dve, "raw_done", r + 3)
                dve.sem_inc(lin_free[1], 1)
                take_transposed(a + 4, wtok, aux[:, 0:QT * 8].rearrange("p (a b) -> p a b", b=8))

                for j in range(4):
                    b = j % 2
                    done(dve, "raw_done", at("idx", "prep") + j)
                    dve.sem_inc(lin_free[b], 1)
                    rotate(at("idx", "aux") + j, raw[b], qT[b])
                    for g in range(6):
                        h2, i = g // 3, g % 3 + 1
                        w = P * (i + 1)
                        n = at("idx", "iu") + 6 * j + g
                        done(dve, "rl_done", n)
                        dve.sem_inc(s_free[g % 2], 1)
                        weight = wtok[:, i, 2 * j + h2:2 * j + h2 + 1]
                        if j == 0 and h2 == 0:
                            ins = TS(score[:, i, 0:w], sm[g % 2][:, 0:w], weight, None, MUL)
                        else:
                            done(dve, "acc_done", n - 3)
                            ins = STT(score[:, i, 0:w], sm[g % 2][:, 0:w], weight, score[:, i, 0:w], MUL, ADD)
                        tell(ins, sem("acc_done"))
                done(dve, "acc_done", at("idx", "iu") + 23)
                mine(dve.tensor_copy(mask[:, 0, 0:P], adm[:, SEQ - P:SEQ]))
                for i in range(1, QT):
                    w = P * (i + 1)
                    mine(STT(score[:, i, 0:w], score[:, i, 0:w], IDX_SCALE, adm[:, SEQ - w:SEQ], MUL, ADD))
                mine.restart()
                for i in range(1, QT):
                    w = P * (i + 1)
                    with mine.loop(0, TOP_K // 8) as _round:
                        mine(dve.max(top8, score[:, i, 0:w]))
                        mine(dve.match_replace(score[:, i, 0:w], top8, score[:, i, 0:w], TAKEN))
                        mine.restart()
                    mine(TS(mask[:, i, 0:w], score[:, i, 0:w], 0.5 * TAKEN, NEG, ALU.is_gt, MUL))
                    mine.restart()

                for j in range(4):
                    b, a = j % 2, at("A", "aux") + 2 * j
                    done(dve, "raw_done", at("A", "prep") + j)
                    dve.sem_inc(lin_free[b], 1)
                    tell(TT(sq[:, :], raw[b], raw[b], MUL), sem("sq_done"))
                    norm_tile_end(a, at("A", "nrm") + j, b, qT[b], v1("qn_a"), sem("normed"))
                    dve.wait_ge(sem("normed"), at("A", "rope") + j + 1)
                    rotate(a + 1, qT[b], qT[b])
                    attention(at("A", "u") + 8 * j, at("A", "s") + 4 * j,
                              lambda g, b, w: STT(sm[b][:, 0:w], sc_b[b][:, 0:w], HD ** -0.5,
                                                  mask[:, g % QT, 0:w], MUL, ADD))
                for j in range(4):
                    b, a, r = j % 2, at("B", "aux") + 3 * j, at("B", "prep") + 3 * j
                    for n, (dst, g) in enumerate(((qT[b], v1("qn_b")), (kT[b], v1("kn_b")))):
                        t = 3 * j + n
                        done(dve, "raw_done", r + n)
                        dve.sem_inc(lin_free[t % 2], 1)
                        tell(TT(sq[:, :], raw[t % 2], raw[t % 2], MUL), sem("sq_done"))
                        norm_tile_end(a + n, at("B", "nrm") + 2 * j + n, t % 2, dst, g, sem("prep_done"))
                    t = 3 * j + 2
                    done(dve, "raw_done", r + 2)
                    dve.sem_inc(lin_free[t % 2], 1)
                    take_transposed(a + 2, vtok[b], aux.rearrange("p (a b) -> p a b", b=P))
                    attention(at("B", "u") + 8 * j, at("B", "s") + 4 * j,
                              lambda g, b, w: STT(sm[b][:, 0:w], sc_b[b][:, 0:w], HD ** -0.5,
                                                  relb[:, 2 * j + g // QT, SEQ - w:SEQ], MUL, ADD))

                mine.restart()
                with mine.loop(0, 4) as i:
                    for p in range(2):
                        l, n = at("gates", "lin", i) + 2 * p, at("gates", "sg", i) + 2 * p
                        for b in range(2):
                            dve.wait_ge(sem("sg_done"), n + b + 1)
                            dve.sem_inc(lin_free[b], 1)
                        lin_wait(0, l + 1)
                        tell(TT(tmp[:, :], sg[0][:, :], lin[0], MUL), lin_free[0])
                        lin_wait(1, l + 1)
                        dve.sem_inc(slot_free[p], 1)
                        tell(TT(sg[1][:, :], sg[1][:, :], lin[1], MUL), lin_free[1])
                        dve.wait_ge(lin_free[0], l + 3)
                        dve.sem_inc(sem("sg_free"), 1)
                        dve.wait_ge(lin_free[1], l + 3)
                        tell(TT(merged[:, ds(2 * i + p, 1), :].squeeze(1), tmp[:, :], sg[1][:, :], ADD), sem("sg_free"))
                dve.wait_ge(sem("sg_free"), at("out", "sg") + 2)
                dve.sem_inc(sem("merged_done"), 1)

                def residual(b, l, k, gate_col, slot=None):
                    lin_wait(b, l)
                    if slot is not None:
                        dve.sem_inc(slot_free[slot], 1)
                    tell(STT(x[:, k, :], lin[b], gate_col, x[:, k, :], MUL, ADD), lin_free[b])

                for t in range(8):
                    residual(t % 2, at("out", "lin") + t // 2, t, mod[:, 16 + t:17 + t], {3: 0, 7: 1}.get(t))
                for b in range(2):
                    dve.wait_ge(lin_free[b], at("norm2", "lin") + 1)
                dve.sem_inc(sem("x_ready"), 1)
                rms_norm(layer * 2 + 1, at("norm2", "aux"), layer * 2 + 1)
                with mine.loop(0, 11) as i:
                    for p in range(2):
                        l, n = at("gu", "lin", i) + p, at("gu", "sg", i) + p
                        dve.wait_ge(sem("sg_done"), n + 1)
                        dve.sem_inc(lin_free[0], 1)
                        lin_wait(1, l)
                        dve.sem_inc(slot_free[p], 1)
                        tell(TT(hid[:, ds(2 * i + p, 1), :].squeeze(1), sg[p][:, :], lin[1], MUL), sem("sg_free"))
                        dve.wait_ge(sem("sg_free"), n + 3)
                        dve.sem_inc(lin_free[1], 1)
                dve.sem_inc(sem("hid_done"), 1)
                with mine.loop(0, 4) as i:
                    for p in range(2):
                        k = 2 * i + p
                        lin_wait(p, at("down", "lin", i))
                        dve.sem_inc(slot_free[p], 1)
                        tell(STT(x[:, ds(k, 1), :].squeeze(1), lin[p], mod[:, ds(k + 40, 1)], x[:, ds(k, 1), :].squeeze(1),
                            MUL, ADD), lin_free[p])
                for b in range(2):
                    dve.wait_ge(lin_free[b], layer * LAYER.total["lin"] + LAYER.total["lin"] + 1)
                dve.sem_inc(sem("x_ready"), 1)

            at = lambda stage, counter, turn=0: SECOND.at(stage, counter, turn)
            R0 = 2 * LAYERS
            with mine.loop(0, 6) as i:
                ada(SECOND, v2d, i, 0)
            gains(None, None, None, at("ln1", "lin"))
            mine.restart()
            layer_norm("ln1", 0, h, R0)

            dve.wait_ge(sem("fd_raw"), 1)
            dve.sem_inc(lin_free[0], 1)
            mine(TS(pr[0][0:16, :], raw[0][0:16, :], -1.0, 0.0, MUL, MAX))
            mine(dve.memset(pr[1][0:16, :], 1.0))
            dve.wait_ge(sem("fd_act"), 3)
            mine(TT(pr[0][0:16, :], pr[0][0:16, :], sm[0][0:16, :], ADD))
            tell(dve.tensor_tensor_scan(negF[0:16, :], pr[1][0:16, :], pr[0][0:16, :], 0.0, MUL, ADD), sem("f_done"))
            dve.wait_ge(sem("fd_raw"), 2)
            dve.sem_inc(lin_free[1], 1)
            mine(TS(pts[0][0:32, :], raw[1][0:32, :], 0.0, None, MAX))
            mine(dve.memset(pts[1][0:32, :], 1.0))
            mine(dve.memset(pts[1][0:32, :].rearrange("p (a b) -> p a b", b=P)[:, :, 0:1], 0.0))
            dve.wait_ge(sem("fd_act"), 6)
            mine(TT(dtT[0:32, :], pts[0][0:32, :], sm[1][0:32, :], ADD))
            dve.wait_ge(sem("a_done"), 1)
            mine(TS(pts[0][0:32, :], dtT[0:32, :], gain[0:32, 0:1], -1.0, MUL, MUL))
            tell(dve.tensor_tensor_scan(acs[0:32, :], pts[1][0:32, :], pts[0][0:32, :], 0.0, MUL, ADD), sem("acs_done"))
            a = at("fd", "aux")
            dve.wait_ge(aux_full, a + 1)
            tell(dve.tensor_copy(ftok, aux[:, 0:QT * 16].rearrange("p (a b) -> p a b", b=16)), aux_free)
            dve.wait_ge(aux_full, a + 2)
            tell(dve.tensor_copy(dt_tok, aux[:, 0:QT * 32].rearrange("p (a b) -> p a b", b=32)), aux_free)
            dve.wait_ge(aux_full, a + 3)
            tell(dve.tensor_copy(acs_tok, aux[:, 0:QT * 32].rearrange("p (a b) -> p a b", b=32)), aux_free)
            dve.wait_ge(aux_free, a + 4)
            dve.sem_inc(sem("acs_tok_done"), 1)
            dve.wait_ge(sem("cd_done"), 1)
            tell(TT(te_tok, aux[:, 0:QT * 32].rearrange("p (a b) -> p a b", b=32), acs_tok, SUB), aux_free)
            dve.wait_ge(aux_free, a + 5)
            dve.sem_inc(sem("te_diff"), 1)
            dve.wait_ge(sem("te_exp"), 1)
            mine(TT(te_tok, te_tok, dt_tok, MUL))
            mine.restart()

            with mine.loop(0, 4) as i:
                for b in range(2):
                    a, r = at("att", "aux", i) + b, at("att", "prep", i) + 3 * b
                    t = 3 * b
                    done(dve, "raw_done", r)
                    dve.sem_inc(lin_free[t % 2], 1)
                    heads = ident[0:16, ds(4 * i + 2 * b, 2)]
                    tell(dve.tensor_copy(fsel[b][0:16, :, :], heads.unsqueeze(2).broadcast_to([16, 2, P])), sem("prep_done"))
                    done(dve, "raw_done", r + 1)
                    dve.sem_inc(lin_free[(t + 1) % 2], 1)
                    tell(dve.tensor_copy(fq[b], ftok[:, :, ds(4 * i + 2 * b, 2)]), sem("prep_done"))
                    done(dve, "raw_done", r + 2)
                    dve.sem_inc(lin_free[t % 2], 1)
                    take_transposed(a, vtok[b], aux.rearrange("p (a b) -> p a b", b=P))
                    attention(at("att", "u", i) + 8 * b, at("att", "s", i) + 4 * b,
                              lambda g, b2, w: STT(sm[b2][:, 0:w], sc_b[b2][:, 0:w],
                                                   fq[b][:, g % QT, g // QT:g // QT + 1],
                                                   causal[:, SEQ - w:SEQ], SUB, ADD))

            def gated(stage, i, p, add):
                l, n = at(stage, "lin", i) + p, at(stage, "sg", i) + p
                dst = merged2[:, ds(2 * i + p, 1), :].squeeze(1)
                dve.wait_ge(sem("sg_done"), n + 1)
                dve.sem_inc(lin_free[0], 1)
                lin_wait(1, l)
                dve.sem_inc(slot_free[p], 1)
                if not add:
                    tell(TT(dst, sg[p][:, :], lin[1], MUL), sem("sg_free"))
                else:
                    mine(TT(tmp[:, :], sg[p][:, :], lin[1], MUL))
                    tell(TT(dst, dst, tmp[:, :], ADD), sem("sg_free"))
                dve.wait_ge(sem("sg_free"), n + 3)
                dve.sem_inc(lin_free[1], 1)

            with mine.loop(0, 4) as i:
                for p in range(2):
                    gated("attout", i, p, False)

            for t in range(2):
                mine(dve.memset(ub[t][:, 0:16], 0.0))
            for g in range(4):
                w = WINDOWS[g]
                for t in range(2):
                    dve.wait_ge(sem("ub_done"), 2 * g + t + 1)
                    dve.sem_inc(lin_free[t], 1)
                    src = ub[t]
                    for step in range(g + 1):
                        lo, dst = 2 ** (step + 1) - 1, level[step % 2]
                        mine(TT(dst[:, lo:], src[:, lo:], src[:, lo - 2 ** step:16 + SEQ - 2 ** step], ADD))
                        src = dst
                    first = pooled[t][:, 0:16]
                    if g:
                        dve.wait_ge(lin_free[1], at("pool", "lin", g) + 1)
                    mine(TT(first, src[:, 16:32], col("recip", 16 * g, 16), MUL))
                    mine(TT(first, first, ub[t][:, 16:32], SUB))
                    mine(STT(pooled[t][:, 16:], src[:, 32:], 1.0 / w, ub[t][:, 32:], MUL, SUB))
                    dve.sem_inc(sem("ub_free"), 1)
                dve.sem_inc(sem("pooled_done"), 1)
                for t in range(2):
                    k, l, n = 2 * g + t, at("pool", "lin", g) + 1 + t, at("pool", "sg", g) + t
                    dve.wait_ge(sem("sg_done"), n + 1)
                    dve.sem_inc(lin_free[0], 1)
                    lin_wait(1, l)
                    if t:
                        dve.sem_inc(slot_free[1], 1)
                    tell(STT(tmp[:, :], lin[1], v2("pool_scale", k), sg[t][:, :], MUL, MUL), sem("sg_free"))
                    dve.wait_ge(sem("sg_free"), n + 3)
                    dve.sem_inc(lin_free[1], 1)
                    mine(TT(merged2[:, k, :], merged2[:, k, :], tmp[:, :], ADD))
            mine.restart()

            with mine.loop(0, 4) as i:
                mine(dve.tensor_copy(gpar, v2d("ssm", i * SP_N, SP_N)))
                for dst, src in ((dtg, dt_tok), (acsg, acs_tok), (teg, te_tok), (cdg, cd_tok)):
                    mine(dve.tensor_copy(dst, src[:, :, ds(i * 8, 8)]))
                heads = ident[0:32, ds(i * 8, 8)]
                mine(dve.tensor_copy(selh[0:32, :, :], heads.unsqueeze(2).broadcast_to([32, 8, P])))
                mine(dve.tensor_copy(selp[0:32, :, :].rearrange("p a b -> p (a b)").rearrange("p (a b) -> p a b", b=HD),
                                     heads.unsqueeze(2).broadcast_to([32, 8, HD])))
                for b in range(2):
                    mine(dve.memset(cin[b][:, 0:3], 0.0))
                dve.sem_inc(sem("gpar_done"), 1)
                for t in range(6):
                    dve.wait_ge(sem("cin_done"), i * 6 + t + 1)
                    dve.sem_inc(lin_free[t % 2], 1)
                    free(dve, "silu_done", i * 6 + t)
                    c, o = cin[t % 2], cv[t % 2]
                    mine(TS(o, c[:, 0:SEQ], gpar[:, 5 * t:5 * t + 1], None, MUL))
                    for tap in range(1, 4):
                        ins = STT(o, c[:, tap:tap + SEQ], gpar[:, 5 * t + tap:5 * t + tap + 1], o, MUL, ADD)
                        if tap < 3:
                            mine(ins)
                    tell(ins, sem("conv_done"))
                for c in range(QT):
                    dve.wait_ge(sem("xt_done"), i * 4 + c + 1)
                    src = pt_b[c % 2].rearrange("p (a b) -> p a b", b=HD)
                    if c < 3:
                        mine(TT(xde[:, c, :].rearrange("p (a b) -> p a b", b=HD), src,
                                teg[:, c, :].unsqueeze(2).broadcast_to([P, 8, HD]), MUL))
                    tell(TT(xdt[:, c, :].rearrange("p (a b) -> p a b", b=HD), src,
                       dtg[:, c, :].unsqueeze(2).broadcast_to([P, 8, HD]), MUL), sem("xd_done"))
                dve.wait_ge(sem("bt_done"), i + 1)
                tell(dve.tensor_copy(btok.rearrange("p a b -> p (a b)"), ob), sem("btok_done"))
                dve.wait_ge(sem("cb_done"), i + 1)
                tell(TT(cbm, sc_b[0].rearrange("p (a b) -> p a b", b=P), tri.unsqueeze(1).broadcast_to([P, QT, P]), MUL), sem("cbm_done"))
                for c in range(3):
                    dve.wait_ge(sem("st_done"), i * 3 + c + 1)
                    if c == 0:
                        tell(dve.tensor_copy(hst[:, 0, :], pt_b[0]), sem("hst_done"))
                    else:
                        dve.wait_ge(sem("hst_done"), i * 3 + c)
                        hv = lambda n: hst[:, n, :].rearrange("p (a b) -> p a b", b=HD)
                        mine(TT(hv(c), hv(c - 1), cdg[:, c, :].unsqueeze(2).broadcast_to([P, 8, HD]), MUL))
                        tell(TT(hst[:, c, :], hst[:, c, :], pt_b[c % 2], ADD), sem("hst_done"))

                def pair(j):
                    done(dve, "yd_done", i * 8 + 2 * j + 1)
                    dve.wait_ge(sem("yoff_done"), i * 4 + j + 1)
                    dve.wait_ge(sem("ea_done"), i * 4 + j + 1)
                    mine(TT(tmp[:, P:], pt_b[0][:, P:], ea[:, P:], MUL))
                    mine(STT(yg[:, j, :], xsT[:, j, :], gpar[:, 30 + j:31 + j], ob, MUL, ADD))
                    tell(TT(yg[:, j, P:], yg[:, j, P:], tmp[:, P:], ADD), sem("yp_done"))

                for hh in range(8):
                    dve.wait_ge(sem("bc_done"), i * 8 + hh + 1)
                    free(dve, "wgt_done", i * 8 + hh)
                    mine(TT(seg[hh % 2].rearrange("p (a b) -> p a b", b=P),
                            sc_b[hh % 2].rearrange("p (a b) -> p a b", b=P),
                            acsg[:, :, hh:hh + 1].broadcast_to([P, QT, P]), SUB))
                    tell(TS(seg[hh % 2], seg[hh % 2], 0.0, None, MIN), sem("seg_done"))
                    if hh % 2 == 0 and hh:
                        pair(hh // 2 - 1)
                pair(3)
                dve.wait_ge(sem("yp_done"), i * 4 + 5)
                for t in range(4):
                    n = at("ssd", "sg", i) + t
                    dve.wait_ge(sem("sg_done"), n + 1)
                    dve.sem_inc(lin_free[t % 2], 1)
                    tell(TT(yg[:, t, :], yg[:, t, :], sg[t % 2][:, :], MUL), sem("sg_free"))
                dve.wait_ge(sem("sg_free"), at("ssd", "sg", i) + 6)
                dve.sem_inc(sem("yz_done"), 1)
                a = at("ssd", "aux", i)
                dve.wait_ge(sem("root_done"), i + (R0 + 2))
                tell(dve.reciprocal(rstd[:, :], rstd[:, :]), aux_free)
                dve.wait_ge(aux_free, a + 2)
                for t in range(4):
                    mine(STT(yT[:, ds(i * 4 + t, 1), :].squeeze(1), yg[:, t, :], gpar[:, 34 + t:35 + t], rstd[:, :],
                             MUL, MUL))
                mine.restart()
                dve.sem_inc(sem("yT_done"), 1)
            with mine.loop(0, 4) as i:
                for p in range(2):
                    gated("ssdout", i, p, True)
                mine.restart()
            dve.sem_inc(sem("merged2_done"), 1)

            for t in range(8):
                lin_wait(t % 2, at("out", "lin") + t // 2)
                if t % 4 == 3:
                    dve.sem_inc(slot_free[t // 4], 1)
                tell(TS(tmp[:, :], lin[t % 2], mod[:, 16 + t:17 + t], None, MUL), lin_free[t % 2])
                dve.wait_ge(lin_free[t % 2], at("out", "lin") + t // 2 + 2)
                mine(STT(x[:, t, :], x[:, t, :], ALPHA, tmp[:, :], MUL, ADD))
            dve.sem_inc(sem("x_ready"), 1)
            layer_norm("ln2", 1, x, R0 + 5)
            dve.wait_ge(sem("x_ready"), 7)
            layer_norm("ln3", 2, h, R0 + 6)

            rep = lambda v: v.unsqueeze(2).broadcast_to([P, QT, E_N])
            probs, sel, ing, e1, e2, t1, t2, small = rt
            s4 = [small[:, :, n:n + 1].squeeze(2) for n in range(16)]
            a = at("router", "aux")
            dve.wait_ge(aux_full, a + 1)
            tell(dve.tensor_copy(probs, aux[:, 0:QT * E_N].rearrange("p (a b) -> p a b", b=E_N)), aux_free)
            dve.wait_ge(aux_free, a + 2)

            def step(ins):
                mine(ins)

            step(dve.tensor_reduce(s4[0], probs, AX.X, MAX))
            tell(TT(probs, probs, rep(s4[0]), SUB), sem("logit_done"))
            dve.wait_ge(sem("probs_exp"), 1)
            step(dve.tensor_reduce(s4[0], probs, AX.X, ADD))
            step(dve.reciprocal(s4[1], s4[0]))
            step(TT(probs, probs, rep(s4[1]), MUL))
            step(TT(sel, probs, v2("b_router", 0, E_N).unsqueeze(1).broadcast_to([P, QT, E_N]), ADD))
            fold = lambda v: v.rearrange("p a b -> p (a b)").rearrange("p (a b) -> p a b", b=4)
            sf, tf, uf = fold(sel), fold(t1), fold(t2)
            step(TT(tf[:, :, 0:3], sf[:, :, 0:3], sf[:, :, 1:4], ADD))
            step(TT(uf[:, :, 0:2], sf[:, :, 0:2], sf[:, :, 2:4], ADD))
            step(TT(uf[:, :, 2:3], sf[:, :, 0:1], sf[:, :, 3:4], ADD))
            step(TT(tf[:, :, 0:3], tf[:, :, 0:3], uf[:, :, 0:3], MAX))
            gs = small.rearrange("p a b -> p (a b)")[:, 0:16]
            step(dve.tensor_reduce(gs.unsqueeze(2), tf[:, :, 0:3], AX.X, MAX))
            gs = gs.rearrange("p (a b) -> p a b", b=4)
            best = small.rearrange("p a b -> p (a b)")[:, 16:20]
            taken = small.rearrange("p a b -> p (a b)")[:, 20:24]
            pick = small.rearrange("p a b -> p (a b)")[:, 24:40].rearrange("p (a b) -> p a b", b=4)
            step(dve.tensor_reduce(best, gs, AX.X, MAX))
            step(TT(pick, gs, best.unsqueeze(2).broadcast_to([P, QT, 4]), ALU.is_equal))
            col4 = lambda v, n: v[:, :, n:n + 1].squeeze(2)
            step(dve.tensor_copy(taken, col4(pick, 0)))
            for n in range(1, 4):
                step(TT(col4(gs, n), col4(pick, n), taken, MUL))
                step(TT(col4(pick, n), col4(pick, n), col4(gs, n), SUB))
                step(TT(taken, taken, col4(pick, n), ADD))
            pk = small.rearrange("p a b -> p (a b)")[:, 24:40]
            step(dve.tensor_copy(fold(ing), pk.unsqueeze(2).broadcast_to([P, 16, 4])))
            step(TT(sel, sel, ing, MUL))
            step(TS(ing, ing, 1.0, -NEG, SUB, MUL))
            step(TT(sel, sel, ing, ADD))
            rev = col("revidx", 0, E_N).unsqueeze(1).broadcast_to([P, QT, E_N])
            for e in (e1, e2):
                step(dve.tensor_reduce(s4[0], sel, AX.X, MAX))
                step(TT(t1, sel, rep(s4[0]), ALU.is_equal))
                step(TT(t1, t1, rev, MUL))
                step(dve.tensor_reduce(s4[0], t1, AX.X, MAX))
                step(TT(e, t1, rep(s4[0]), ALU.is_equal))
                step(STT(sel, e, 4 * NEG, sel, MUL, ADD))
            step(TT(gw, e1, e2, ADD))
            dve.sem_inc(sem("chosen"), 1)
            for e, wt in ((e1, weight1), (e2, weight2)):
                step(TT(t1, e, probs, MUL))
                step(dve.tensor_reduce(wt, t1, AX.X, ADD))
            step(TT(s4[0], weight1, weight2, ADD))
            step(dve.reciprocal(s4[1], s4[0]))
            for wt in (weight1, weight2):
                step(TT(wt, wt, s4[1], MUL))
            E = slice(0, E_N)
            step(dve.memset(unit[E], 1.0))
            dve.wait_ge(aux_full, a + 2)
            tell(dve.tensor_copy(chosenT[E], aux[E, :]), aux_free)
            dve.wait_ge(aux_free, a + 3)
            step(dve.tensor_tensor_scan(cum[E], unit[E], chosenT[E], 0.0, MUL, ADD))
            step(TT(fits[E], col("steps", 0, QT)[E], cum[E, SEQ - 1:SEQ].broadcast_to([E_N, QT]), ALU.is_lt))
            tell(dve.tensor_reduce(n_blocks[E], fits[E], AX.X, ADD), sem("blocks_counted"))
            dve.wait_ge(aux_full, a + 3)
            tell(dve.tensor_copy(ends[E], aux[E, 0:1]), aux_free)
            dve.wait_ge(aux_free, a + 4)
            tell(TT(past[E], col("blocks", 0, N_BLK)[E], ends[E].broadcast_to([E_N, N_BLK]), ALU.is_ge), sem("past_done"))
            step(TT(base[E], ends[E], n_blocks[E], SUB))
            step(TS(base[E], base[E], float(P), -1.0, MUL, ADD))
            tell(TS(position[E], cum[E], base[E], None, ADD), sem("position_done"))
            dve.wait_ge(aux_full, a + 4)
            tell(TS(past, aux[:, 0:N_BLK], float(E_N - 1), None, MIN), aux_free)
            dve.wait_ge(aux_free, a + 5)
            tell(dve.tensor_copy(expert_of, past), sem("experts_known"))
            dve.wait_ge(aux_full, a + 5)
            tell(dve.tensor_copy(t2, aux[:, 0:QT * E_N].rearrange("p (a b) -> p a b", b=E_N)), aux_free)
            dve.wait_ge(aux_free, a + 6)
            for e, dest, row in ((e1, dest1, row1), (e2, dest2, row2)):
                step(TT(t1, e, t2, MUL))
                step(dve.tensor_reduce(dest, t1, AX.X, ADD))
                step(dve.tensor_copy(row, dest))
            dve.sem_inc(sem("rows_known"), 1)
            mine.restart()

            def rows_half(b, par):
                dve.wait_ge(sem("rows_turned"), b + 1)
                tell(dve.tensor_copy(xT[par][:, SEQ:], pt_b[1]), sem("xTd_done"))

            def gated_block(b):
                dve.wait_ge(sem("silu_read"), b + 1)
                dve.wait_ge(sem("u_done"), b + 1)
                tell(TT(hidb, sg[0][:, :], lin[1], MUL), sem("hidden"))

            def made_half(b, par, first=False):
                dve.wait_ge(sem("d_done"), b + 2)
                if not first:
                    dve.wait_ge(sem("made_out"), (b - 1) * 16)
                tell(dve.tensor_copy(yb[par][:, SEQ:], sc_b[1]), sem("yd2_done"))

            rows_half(0, 0)
            rows_half(1, 1)
            gated_block(0)

            def block_step(b, par, first=False):
                made_half(b - 1, 1 - par, first)
                rows_half(b + 1, 1 - par)
                gated_block(b)

            for b in (1, 2):
                block_step(b, b % 2, True)
            with mine.loop(1, (N_BLK - 1) // 2) as i:
                for n in range(2):
                    block_step(2 * i + (n + 1), (n + 1) % 2)
            made_half(N_BLK - 1, (N_BLK - 1) % 2)
            second = merged2.rearrange("p a b -> p (a b)").rearrange("p (a b) -> p a b", b=D)
            for t in range(QT):
                dve.wait_ge(sem("gathered%d" % t), 32)
                mine(TS(htok[:, t, :], htok[:, t, :], weight1[:, t:t + 1], None, MUL))
                tell(STT(htok[:, t, :], second[:, t, :], weight2[:, t:t + 1], htok[:, t, :], MUL, ADD), sem("combined"))
            dve.wait_ge(sem("ffn_done"), 2 * QT)
            for t in range(8):
                mine(TS(moe[:, t, :], moe[:, t, :], mod[:, 40 + t:41 + t], None, MUL))
            for t in range(8):
                mine(STT(x[:, t, :], x[:, t, :], ALPHA, moe[:, t, :], MUL, ADD))
            dve.sem_inc(sem("x_ready"), 1)
            layer_norm("ln4", 3, x, R0 + 7)

        @block.gpsimd
        def _(pool):
            mine = Steps(pool, sem("pool_steps"))
            tell = mine.tell
            pool.sem_inc(sem("pn_done"), 2)
            pool.sem_inc(sem("wgt_done"), 2)

            def attention(u):
                for g in range(8):
                    w = P * (g % QT + 1)
                    pool.wait_ge(sem("rcp_done"), u + g + 1)
                    tell(pool.tensor_tensor(pr[g % 2][:, 0:w], pr[g % 2][:, 0:w], rcp[:, g:g + 1].broadcast_to([P, w]),
                                       ALU.mult), sem("pn_done"))

            with mine.loop(0, LAYERS) as layer:
                for stage in ("A", "B"):
                    for j in range(4):
                        attention(LAYER.at(stage, "u", 0, layer) + 8 * j)
            zeros = arena[:, ARENA - D:ARENA]
            tell(pool.memset(zeros, 0.0), sem("zeroed"))
            pool.wait_ge(sem("zeroed"), 1)
            pool.dma_start(routed.rearrange("(a p) n -> p a n", p=P), zeros.unsqueeze(1).broadcast_to([P, N_BLK + 1, D]))\
                .then_inc(sem("zeros_out"), 16)
            pool.wait_ge(sem("zeros_out"), 16)
            with mine.loop(0, 4) as i:
                for b in range(2):
                    attention(SECOND.at("att", "u", i) + 8 * b)
            with mine.loop(0, 4) as i:
                pool.wait_ge(sem("cbm_done"), i + 1)
                for hh in range(8):
                    pool.wait_ge(sem("e_done"), i * 8 + hh + 1)
                    free(pool, "yd_done", i * 8 + hh)
                    tell(pool.tensor_tensor(wgt[hh % 2], seg[hh % 2], cbm.rearrange("p a b -> p (a b)"), ALU.mult), sem("wgt_done"))
            pool.wait_ge(sem("rows_known"), 1)
            pool.wait_ge(sem("htok_done"), 2 * QT)
            for t in range(QT):
                for row in (row1, row2):
                    pool.indirect_dma_start(routed, bass.IndirectOffsetOnAxis(row[:, t:t + 1], 0), htok[:, t, :], None)\
                        .then_inc(sem("scattered"), 16)
            pool.wait_ge(sem("scattered"), 2 * QT * 16)

            def load_rows(b):
                pool.dma_start(xr, routed[ds(b * P, P), :]).then_inc(sem("rows_in"), 16)

            def store_made(b, par):
                pool.wait_ge(sem("ya_done"), b + 2)
                pool.wait_ge(sem("yd2_done"), b + 2)
                pool.dma_start(made[ds(b * P, P), :], yb[par]).then_inc(sem("made_out"), 16)

            load_rows(0)
            pool.wait_ge(sem("rows_turned"), 1)
            load_rows(1)
            pool.wait_ge(sem("rows_turned"), 2)
            load_rows(2)
            with pool.Fori(0, (N_BLK - 1) // 2 - 1) as i:
                for n in range(2):
                    b = 2 * i + (n + 1)
                    store_made(b - 1, n)
                    pool.wait_ge(sem("rows_turned"), b + 2)
                    load_rows(b + 2)
            store_made(N_BLK - 3, 0)
            pool.wait_ge(sem("rows_turned"), N_BLK)
            load_rows(N_BLK)
            store_made(N_BLK - 2, 1)
            store_made(N_BLK - 1, 0)
            pool.wait_ge(sem("made_out"), N_BLK * 16)
            second = merged2.rearrange("p a b -> p (a b)").rearrange("p (a b) -> p a b", b=D)
            for t in range(QT):
                for row, dst in ((row1, htok), (row2, second)):
                    pool.indirect_dma_start(dst[:, t, :], None, made, bass.IndirectOffsetOnAxis(row[:, t:t + 1], 0))\
                        .then_inc(sem("gathered%d" % t), 16)



def _constants():
    c = np.zeros((P, NCST), np.float32)

    def put(name, value):
        a, b = CST[name]
        c[:, a:b] = value

    q, k = np.arange(P)[:, None], np.arange(P)[None, :]
    put("ident", q == k)
    put("blockones", q // HD == k // HD)
    put("ones", 1)
    same = q // HD == k // HD
    put("rope", 1.0 * (same & (k % HD >= 8) & (k % HD < 16) & (q == k - 8)) - 1.0 * (same & (k % HD < 8) & (q == k + 8)))
    put("last", q == P - 1)
    adm, causal = np.zeros((P, SEQ)), np.zeros((P, SEQ))
    adm[:, SEQ - P:] = np.where(k // HD > q // HD, NEG, 0)
    causal[:, SEQ - P:] = np.where(k > q, NEG, 0)
    put("adm", adm)
    put("causal", causal)
    put("tri", k >= q)
    put("recip", np.concatenate([1 / np.minimum(np.arange(1, 17), w) for w in WINDOWS])[None])
    inv = np.float32(500000.0) ** (-np.arange(0, 16, 2, dtype=np.float32) / np.float32(16))
    d = np.arange(P) % HD
    put("inv_freq", np.where(d < 16, inv[d % 8], 0).astype(np.float32)[:, None])
    put("revidx", np.arange(E_N, 0, -1)[None])
    put("blocks", np.arange(N_BLK)[None])
    put("steps", P * np.arange(QT)[None])
    return c


def _tiles(v):
    return v.reshape(-1, P).T


def _chunks(w):
    return w.reshape(-1, P, w.shape[1]).transpose(1, 0, 2).reshape(P, -1)


def _slot(*parts):
    return np.concatenate([_chunks(w) for w in parts], axis=1).reshape(-1)


def kernel(**inputs):
    import concourse.bacc as _bacc
    from concourse.bass_utils import run_bass_kernel_spmd as _run

    g = {k: np.asarray(v) for k, v in inputs.items()}
    slots, vec1, rel = [], [], []
    for l in range(LAYERS):
        w_ada, w_in, b_in = g["w_ada"][l], g["w_in"][l], g["b_in"][l]
        cols = lambda at, n: w_in[:, at:at + n]
        tile = lambda w, i: w[:, i * P:(i + 1) * P]
        slots += [_slot(w_ada[:, i * 512:(i + 1) * 512]) for i in range(12)]
        two = lambda a: np.concatenate([a, a], axis=-1)
        slots += [_slot(two(cols(KA, HD)), two(cols(KI, HD))), _slot(cols(VA, HD), cols(WI, 8))]
        slots += [_slot(cols(QI + i * P, P)) for i in range(4)]
        slots += [_slot(cols(QA + i * P, P)) for i in range(4)]
        slots += [_slot(cols(QB + i * P, P), cols(KB + i * P, P), cols(VB + i * P, P)) for i in range(4)]
        slots += [_slot(cols(GA + i * P, P), cols(GB + i * P, P), tile(g["w_oa"][l], i), tile(g["w_ob"][l], i))
                  for i in range(8)]
        slots += [_slot(g["w_out"][l][:, i * 512:(i + 1) * 512]) for i in range(2)]
        slots += [_slot(tile(g["w_gu"][l], i), g["w_gu"][l][:, FF + i * P:FF + (i + 1) * P]) for i in range(FF_T)]
        slots += [_slot(tile(g["w_down"][l], i)) for i in range(8)]
        v = np.zeros((P, NV1), np.float32)

        def put(name, value):
            a, b = VEC1[name]
            v[0:value.shape[0], a:b] = value

        put("b_ada", _tiles(g["b_ada"][l]))
        put("g_mix", _tiles(g["g_mix"][l]))
        put("g_ffn", _tiles(g["g_ffn"][l]))
        for name, at, n in (("qa", QA, 4), ("qi", QI, 4), ("qb", QB, 4), ("kb", KB, 4), ("vb", VB, 4), ("ga", GA, 8),
                            ("gb", GB, 8)):
            put(name, _tiles(b_in[at:at + n * P]))
        put("ka", two(b_in[KA:KA + HD])[:, None])
        put("ki", two(b_in[KI:KI + HD])[:, None])
        put("va", b_in[VA:VA + HD][:, None])
        put("wi", b_in[WI:WI + 8][:, None])
        for name in ("qn_a", "kn_a", "qn_b", "kn_b"):
            put(name, two(g[name][l])[:, None])
        vec1.append(v.reshape(-1))
        at = np.clip(np.arange(P)[:, None] - np.arange(SEQ)[None] + SEQ - P, -63, 256) + 63
        rel.append(g["rel_bias"][l][:, at].transpose(1, 0, 2).reshape(-1))

    w2, tile = g["w_in_2"][0], lambda w, i, n=P: w[:, i * n:(i + 1) * n]
    cols = lambda at, n: w2[:, at:at + n]
    slots += [_slot(tile(g["w_ada_2"][0], i, 512)) for i in range(12)]
    slots += [_slot(cols(F2, 16)), _slot(cols(DT2, 32))]
    slots += [_slot(cols(Q2 + i * P, P), cols(K2 + i * P, P), cols(V2 + i * P, P)) for i in range(8)]
    slots += [_slot(cols(G2 + i * P, P), tile(g["w_attn_o_2"][0], i)) for i in range(8)]
    for i in range(4):
        slots += [_slot(cols(U2 + i * 256, 256)), _slot(cols(G2 + D + i * 256, 256), g["w_pool_2"][0][i])]
    for i in range(4):
        bc = np.concatenate([cols(XBC2 + 2048 + i * P, P), cols(XBC2 + 2560 + i * P, P)], axis=1)
        slots += [_slot(cols(XBC2 + i * 512, 512)), _slot(bc), _slot(cols(Z2 + i * 512, 256)),
                  _slot(cols(Z2 + i * 512 + 256, 256))]
    slots += [_slot(cols(G2 + 2 * D + i * P, P), tile(g["w_ssm_o_2"][0], i)) for i in range(8)]
    slots += [_slot(tile(g["w_out_2"][0], i, 512)) for i in range(2)]
    for e in range(E_N):
        slots += [_slot(g["w_exp_gate_2"][0, e]), _slot(g["w_exp_up_2"][0, e]), _slot(g["w_exp_down_2"][0, e])]

    v2_ = np.zeros((P, NV2), np.float32)

    def put2(name, value):
        a, b = VEC2[name]
        v2_[0:value.shape[0], a:b] = value

    put2("b_ada", _tiles(g["b_ada_2"][0]))
    for name in ("pool_scale", "ln_mix_g", "ln_mix_b", "ln_ffn_g", "ln_ffn_b"):
        put2(name, _tiles(g[name + "_2"][0]))
    for name in ("b_forget", "dt_bias", "a_log"):
        put2(name, g[name + "_2"][0][:, None])
    taps = np.concatenate([g["conv_w_2"][0], g["conv_b_2"]], axis=0).reshape(5, 24, P).transpose(2, 1, 0)
    skip = np.repeat(g["d_skip_2"][0], HD).reshape(16, P).T
    norm = _tiles(g["ssm_norm_w_2"][0])
    for i in range(4):
        a = VEC2["ssm"][0] + i * SP_N
        for n, t in enumerate((4 * i, 4 * i + 1, 4 * i + 2, 4 * i + 3, 16 + i, 20 + i)):
            v2_[:, a + 5 * n:a + 5 * n + 5] = taps[:, t]
        v2_[:, a + 30:a + 34] = skip[:, 4 * i:4 * i + 4]
        v2_[:, a + 34:a + 38] = norm[:, 4 * i:4 * i + 4]
    put2("w_router", _chunks(g["w_router_2"]))
    put2("b_router", np.broadcast_to(g["b_router_2"], (P, E_N)))

    arrays = {
        "w_all": np.concatenate(slots),
        "vec1": np.concatenate(vec1),
        "vec2": v2_,
        "consts": _constants(),
        "x_in": np.ascontiguousarray(g["x"][0].T.reshape(KC, P, SEQ).transpose(1, 0, 2)),
        "pos": np.ascontiguousarray(np.broadcast_to(g["positions"], (P, SEQ))),
        "cond": np.concatenate([_tiles(g["c"][0]), _tiles(g["c_2"][0])], axis=1),
        "rel": np.concatenate(rel),
    }
    nc = _bacc.Bacc("TRN2", target_bir_lowering=False, num_devices=1)
    args = [nc.dram_tensor("in_" + k, a.shape, mybir.dt.from_np(a.dtype), kind="ExternalInput").ap() for k, a in arrays.items()]
    out = nc.dram_tensor("out", (P, KC, SEQ), F32, kind="ExternalOutput").ap()
    two_blocks(nc, *args[:4], *args[4:], out)
    r = _run(nc, [{"in_" + k: a for k, a in arrays.items()}], core_ids=[0])
    y = r.results[0]["out"]
    return np.ascontiguousarray(y.transpose(1, 0, 2).reshape(D, SEQ).T)[None]
```

```python
import numpy as np
import concourse.bass as bass
from concourse import mybir
from contextlib import ExitStack, contextmanager

F32 = mybir.dt.float32
F32R = mybir.dt.float32r
I32 = mybir.dt.int32
ALU = mybir.AluOpType
ACT = mybir.ActivationFunctionType
AX = mybir.AxisListType
ds = bass.ds

P = 128
D, SEQ, KC = 1024, 512, 8
QT = SEQ // P
LAYERS = 2
HD = 64
FF_T = 2816 // P
FF = FF_T * P
TOP_K = 128
IDX_SCALE = 64 ** -0.5 * 8 ** -0.5
EPS, LN_EPS = 1e-6, 1e-5
ALPHA = 2 ** 0.25
NEG = -1e30
TAKEN = -3e38
E_N, E_FF = 16, 512
N_BLK = (2 * SEQ + E_N * (P - 1)) // P
WINDOWS = (2, 4, 8, 16)

QA, KA, VA, QI, KI, WI, QB, KB, VB, GA, GB = 0, 512, 576, 640, 1152, 1216, 1224, 1736, 2248, 2760, 3784
Q2, K2, V2, F2, U2, Z2, XBC2, DT2, G2 = 0, 1024, 2048, 3072, 3088, 4112, 6160, 9232, 9264


def column_map(parts):
    at, out = 0, {}
    for name, n in parts:
        out[name] = (at, at + n)
        at += n
    return out, at


VEC1, NV1 = column_map([("b_ada", 48), ("g_mix", 8), ("g_ffn", 8), ("qa", 4), ("qi", 4), ("ka", 1), ("ki", 1),
                        ("va", 1), ("wi", 1), ("qb", 4), ("kb", 4), ("vb", 4), ("ga", 8), ("gb", 8),
                        ("qn_a", 1), ("kn_a", 1), ("qn_b", 1), ("kn_b", 1)])
SP_N = 38
VEC2, NV2 = column_map([("b_ada", 48), ("pool_scale", 8), ("ln_mix_g", 8), ("ln_mix_b", 8), ("ln_ffn_g", 8),
                        ("ln_ffn_b", 8), ("b_forget", 1), ("dt_bias", 1), ("a_log", 1), ("ssm", 4 * SP_N),
                        ("w_router", KC * E_N), ("b_router", E_N)])
CST, NCST = column_map([("ident", P), ("blockones", P), ("ones", P), ("rope", P), ("last", P), ("adm", SEQ),
                        ("causal", SEQ), ("tri", P), ("recip", 4 * 16), ("inv_freq", 1), 
                        ("revidx", E_N), ("blocks", N_BLK), ("steps", QT)])


class Plan:

    def __init__(self, stages, start=None):
        self.stages, self.inc, self.base, at = stages, {}, {}, dict(start or {})
        start = dict(at)
        for name, turns, inc in stages:
            self.inc[name], self.base[name] = inc, dict(at)
            for k, n in inc.items():
                at[k] = at.get(k, 0) + n * turns
        self.end, self.total = at, {k: n - start.get(k, 0) for k, n in at.items()}

    def at(self, stage, counter, turn=0, layer=0):
        value = self.base[stage].get(counter, 0) + turn * self.inc[stage].get(counter, 0)
        return layer * self.total.get(counter, 0) + value


ADA0 = Plan([("ada", 2, dict(slot=1))])
LAYER = Plan([
    ("norm1", 1, dict(aux=1)),
    ("misc", 1, dict(slot=1, lin=2, aux=5, prep=4, nrm=1, rope=1)),
    ("idx", 1, dict(slot=2, lin=2, aux=4, prep=4, s=12, iu=24)),
    ("B", 1, dict(slot=2, lin=6, aux=12, prep=12, nrm=8, s=16, u=32, o=4)),
    ("A", 1, dict(slot=2, lin=2, aux=8, prep=4, nrm=4, rope=4, s=16, u=32, o=4)),
    ("gates", 4, dict(slot=1, lin=4, sg=4)),
    ("out", 1, dict(slot=1, lin=4)),
    ("norm2", 1, dict(aux=1)),
    ("gu", 8, dict(slot=1, lin=2, sg=2)),
    ("gu_rest", 3, dict(slot=1, lin=2, sg=2)),
    ("down", 4, dict(slot=1, lin=1)),
], ADA0.end)
SECOND = Plan([
    ("ln1", 1, dict(aux=2)),
    ("fd", 1, dict(slot=1, lin=1, aux=4)),
    ("att", 4, dict(slot=1, lin=3, aux=2, prep=6, s=8, u=16, o=2)),
    ("attout", 4, dict(slot=1, lin=2, sg=2)),
    ("pool", 4, dict(slot=1, lin=3, sg=2)),
    ("ssd", 4, dict(slot=2, lin=5, aux=1, sg=4)),
    ("ssdout", 4, dict(slot=1, lin=2, sg=2)),
    ("out", 1, dict(slot=1, lin=4)),
    ("ln2", 1, dict(aux=2)),
    ("ln3", 1, dict(aux=2)),
    ("router", 1, dict(aux=5)),
    ("ln4", 1, dict(aux=2)),
], {k: ADA0.end.get(k, 0) + LAYERS * n for k, n in LAYER.total.items()})

ADA_SLOTS = [4 * D] * 4
BESIDE = {"gates": (2, 2, 0), "gu": (1, 1, 16), "attout": (2, 2, 0)}
PARTS = 32
SPLIT = FF_T + KC
SLOTS_1 = ([2 * KC * P, KC * 72] + [KC * P] * 4 + [3 * KC * P] * 4 + [KC * P] * 4 + [2 * KC * P + 8 * P] * 8
           + [KC * 512] * 2 + [2 * KC * P] * 22 + [FF_T * P] * 8)
SLOTS_2 = ([KC * 16, KC * 32] + [3 * KC * P] * 8 + [2 * KC * P] * 8
           + [KC * 256, KC * 256 + 512] * 4 + [KC * 512, KC * 256, KC * 256, KC * 256] * 4 + [KC * P + 16 * P] * 8
           + [KC * 512] * 2)
EXPERT = 3 * D * E_FF
ADA0_TOTAL = sum(ADA_SLOTS) * P
W1_TOTAL = (sum(SLOTS_1) + 48 * D) * P
W2_TOTAL = (sum(SLOTS_2) + 32 * D) * P
EXPERTS_AT = ADA0_TOTAL + LAYERS * W1_TOTAL + W2_TOTAL
assert len(SLOTS_1) == 2 * LAYER.total["slot"], (len(SLOTS_1), LAYER.total)
assert len(SLOTS_2) == 2 * SECOND.total["slot"]
assert N_BLK % 2 == 1


class Steps:

    def __init__(self, eng, sem):
        self.eng, self.sem, self.n = eng, sem, 0

    def __call__(self, ins):
        self.n += 1
        ins.then_inc(self.sem, 1)
        self.eng.wait_ge(self.sem, self.n)

    def tell(self, ins, signal):
        self(ins)
        self.eng.sem_inc(signal, 1)

    def restart(self):
        if self.n:
            self.eng.sem_clear(self.sem)
            self.n = 0

    @contextmanager
    def loop(self, start, end):
        self.restart()
        with self.eng.Fori(start, end) as i:
            yield i
            self.restart()


def two_blocks(nc, w_all, vec1_all, vec2_all, consts, x_in, pos_in, cond, rel, out):
    ctx = ExitStack()
    with ctx:
        sems = {}

        def sem(name):
            if name not in sems:
                sems[name] = ctx.enter_context(nc.semaphore(name))
            return sems[name]

        start_of = {}

        def sb(name, *shape, dt=F32):
            t = ctx.enter_context(nc.sbuf_tensor(name, [P, *shape], dt))
            start_of[name] = nc.sbuf_base - 4 * int(np.prod(shape))
            return t[:, :, :] if len(shape) == 2 else t[:, :]

        x = sb("x", KC, SEQ)
        h = sb("h", KC, SEQ)
        ring = [sb("ring0", 4096), sb("ring1", 4096)]
        cst = sb("cst", NCST)
        vec = sb("vec", NV1)
        vec2 = sb("vec2", NV2)
        mod = sb("mod", 48)
        gain = sb("gain", 16)
        cosT, sinT = sb("cosT", SEQ), sb("sinT", SEQ)
        rstd = sb("rstd", SEQ)
        tmp = sb("tmp", SEQ)
        sg = [sb("sg0", SEQ), sb("sg1", SEQ)]
        abuf = sb("abuf", 14, SEQ)
        qT, kT = [abuf[:, 0, :], abuf[:, 1, :]], [abuf[:, 2, :], abuf[:, 3, :]]
        vtok = [abuf[:, 4 + b, :].rearrange("p (a b) -> p a b", b=P) for b in range(2)]
        raw = [abuf[:, 6, :], abuf[:, 7, :]]
        sm, pr, pts = ([abuf[:, n, :], abuf[:, n + 1, :]] for n in (8, 10, 12))
        pbuf = sm + pr
        sq, rs = sb("sq", SEQ), sb("rs", SEQ)
        nmax, esum, rcp = sb("nmax", 8), sb("esum", 8), sb("rcp", 8)
        ARENA = 22800
        arena = sb("arena", ARENA)
        cursor = [0]

        def part(*shape):
            n = int(np.prod(shape))
            v = arena[:, cursor[0]:cursor[0] + n]
            cursor[0] += n
            assert cursor[0] <= ARENA, cursor[0]
            if len(shape) == 2:
                v = v.rearrange("p (a b) -> p a b", b=shape[1])
            return v

        attA, attB = part(4, SEQ), part(4, SEQ)
        mask, score = part(QT, SEQ), part(QT, SEQ)
        merged = part(KC, SEQ)
        hid = arena[:, 0:FF_T * SEQ].rearrange("p (a b) -> p a b", b=SEQ)
        relb = part(8, SEQ)
        kaT, kiT, va = part(SEQ), part(SEQ), part(QT, HD)
        wtok, top8 = part(QT, 8), part(8)
        csil, wada, mod_next, mod_sum = part(D), part(2 * D), part(16), part(4)
        def halves(name, over, skip, *shape):
            t = nc.alloc_sbuf_tensor_at(name, [P, *shape], F32R, offset=start_of[over] + 4 * skip)
            return t[:, :, :] if len(shape) == 2 else t[:, :]

        h_hi, h_lo = halves("h_hi", "abuf", 6 * SEQ, KC, SEQ), halves("h_lo", "h", 0, KC, SEQ)
        w_hi = [halves("w_hi%d" % n, "ring%d" % n, 2 * KC * P, 2 * KC * P) for n in range(2)]
        w_lo = [halves("w_lo%d" % n, "ring%d" % n, 0, 2 * KC * P) for n in range(2)]
        wd_hi = [halves("wd_hi%d" % n, "arena", FF_T * (SEQ + n * P), FF_T * P) for n in range(2)]
        wd_lo = [halves("wd_lo%d" % n, "ring%d" % n, 0, FF_T * P) for n in range(2)]
        hid_lo = halves("hid_lo", "arena", 0, FF_T, SEQ)
        hid_hi = [v[:, k, :] for v, n in ((halves("hid_hi0", "abuf", 2 * SEQ, 4, SEQ), 4),
                                          (halves("hid_hi1", "abuf", 6 * SEQ, 8, SEQ), 8),
                                          (halves("hid_hi2", "h", 0, 8, SEQ), 8)) for k in range(n)]
        hid_hi += [halves("hid_hi3", "sq", 0, SEQ), halves("hid_hi4", "rs", 0, SEQ)]
        cursor[0] = 0
        merged2 = part(KC, SEQ)
        negF, ftok = part(SEQ), part(QT, 16)
        dtT, acs = part(SEQ), part(SEQ)
        dt_tok, acs_tok, te_tok, cd_tok = part(QT, 32), part(QT, 32), part(QT, 32), part(QT, 32)
        shared_end = cursor[0]
        att2 = part(KC, SEQ)
        fsel = [part(2, P), part(2, P)]
        fq = [part(QT, 2), part(QT, 2)]
        ub = [part(16 + SEQ), part(16 + SEQ)]
        level = [part(16 + SEQ), part(16 + SEQ)]
        pooled = [part(SEQ), part(SEQ)]
        cursor[0] = shared_end
        yT = part(16, SEQ)
        xdt, xde, hst = part(QT, SEQ), part(3, SEQ), part(3, SEQ)
        cin = [hst.rearrange("p a b -> p (a b)")[:, 515 * b:515 * b + 515] for b in range(2)]
        yg, xsT = abuf[:, 0:4, :], abuf[:, 4:8, :]
        seg, wgt, ea, bmT = sm, pr, abuf[:, 12, :], abuf[:, 13, :]
        cv = pr
        cmT = part(SEQ)
        btok, cbm = part(QT, P), part(QT, P)
        selh, selp = part(8, P), part(4, P)
        gpar = part(SP_N)
        dtg, acsg, teg, cdg = part(QT, 8), part(QT, 8), part(QT, 8), part(QT, 8)
        cursor[0] = shared_end
        moe = part(KC, SEQ)
        htok = part(QT, D)
        wdown = part(4 * D)
        gw, rt = part(QT, E_N), [part(QT, E_N) for _ in range(8)]
        weight1, weight2, dest1, dest2 = part(QT), part(QT), part(QT), part(QT)
        n_blocks, ends, base, fits = part(1), part(1), part(1), part(QT)
        past = part(N_BLK)
        row1, row2, expert_of = (part(n).bitcast(I32) for n in (QT, QT, N_BLK))
        flat = lambda v: v.rearrange("p a b -> p (a b)")
        xr, hidb = flat(abuf[:, 0:2, :]), abuf[:, 6, :]
        xT = [flat(abuf[:, n:n + 2, :]) for n in (2, 4)]
        yb = [flat(abuf[:, n:n + 2, :]) for n in (7, 9)]
        position, cum, unit, chosenT = (abuf[:, n, :] for n in (10, 11, 12, 13))
        routed = nc.dram_tensor("routed", ((N_BLK + 1) * P, D), F32, kind="Internal").ap()
        made = nc.dram_tensor("made", (N_BLK * P, D), F32, kind="Internal").ap()

        banks = ctx.enter_context(nc.psum_tensor("banks", [P, 8, SEQ], F32))[:, :, :]
        lin, aux = [banks[:, 0, :], banks[:, 1, :]], banks[:, 2, :]
        sc_b, pt_b, ob = [banks[:, 3, :], banks[:, 4, :]], [banks[:, 5, :], banks[:, 6, :]], banks[:, 7, :]

        def col(name, i=0, n=1):
            at = CST[name][0] + i
            return cst[:, at:at + n]

        def v1(name, i=0, n=1):
            at = VEC1[name][0] + i
            return vec[:, at:at + n]

        def v1d(name, i, n=1):
            return vec[:, ds(i + VEC1[name][0], n)]

        def v2(name, i=0, n=1):
            at = VEC2[name][0] + i
            return vec2[:, at:at + n]

        def v2d(name, i, n=1):
            return vec2[:, ds(i + VEC2[name][0], n)]

        ident, blockones, ones, rope, last = (col(n, 0, P) for n in ("ident", "blockones", "ones", "rope", "last"))
        adm, causal, tri = col("adm", 0, SEQ), col("causal", 0, SEQ), col("tri", 0, P)

        boot, c_in, vec_in, rel_in, out_done = (sem(n) for n in ("boot", "c_in", "vec_in", "rel_in", "out_done"))
        slot_full, slot_free = [sem("slot_full0"), sem("slot_full1")], [sem("slot_free0"), sem("slot_free1")]
        lin_full, lin_free = [sem("lin_full0"), sem("lin_full1")], [sem("lin_free0"), sem("lin_free1")]
        s_full, s_free = [sem("s_full0"), sem("s_full1")], [sem("s_free0"), sem("s_free1")]
        aux_full, aux_free, o_free = sem("aux_full"), sem("aux_free"), sem("o_free")

        def done(eng, name, n):
            eng.wait_ge(sem(name), n + 3)

        def free(eng, name, n):
            eng.wait_ge(sem(name), n + 1)

        def hold(eng):
            eng.sem_inc(sem("held"), 1)

        block = ctx.enter_context(nc.Block())

        @block.sync
        def _(sp):
            def stream(plan, stage, sizes, turn, layer, offset):
                for n, size in enumerate(sizes):
                    use = plan.at(stage, "slot", turn, layer) + n // 2
                    sp.wait_ge(slot_free[n % 2], use + 1)
                    src = w_all[ds(offset, size * P)].rearrange("(p n) -> p n", p=P)
                    sp.dma_start(ring[n % 2][:, 0:size], src).then_inc(slot_full[n % 2], 16)
                    offset = offset + size * P

            def beside(plan, stage, i, layer, sizes, offset):
                parts, tiles, before = BESIDE[stage]
                for n, size in enumerate(sizes):
                    sp.wait_ge(slot_free[n], plan.at(stage, "slot", i, 0 if plan is SECOND else layer) + 1)
                    sp.dma_start(ring[n][:, 0:size], w_all[ds(offset, size * P)].rearrange("(p n) -> p n", p=P))\
                        .then_inc(slot_full[n], 16)
                    offset = offset + size * P
                    for m in range(parts):
                        use = layer * PARTS + 2 * parts * i + (before + parts * n + m)
                        sp.wait_ge(sem("wada_free"), use + 1)
                        sp.dma_start(wada[:, 0:tiles * D],
                                     w_all[ds(offset, tiles * D * P)].rearrange("(p n) -> p n", p=P))\
                            .then_inc(sem("wada_in"), 16)
                        offset = offset + tiles * D * P

            def run(plan, sizes_all, stages, layer, offset, loops):
                at = 0
                for stage, turns, inc in stages:
                    n = 2 * inc.get("slot", 0)
                    if not n:
                        continue
                    if stage in BESIDE:
                        sizes = sizes_all[at:at + n]
                        turn_size = (sum(sizes) + 2 * BESIDE[stage][0] * BESIDE[stage][1] * D) * P
                        with sp.Fori(0, turns) as i:
                            beside(plan, stage, i, LAYERS if plan is SECOND else layer, sizes, offset + i * turn_size)
                        offset = offset + turns * turn_size
                        at += n * turns
                        continue
                    if stage in loops:
                        sizes = sizes_all[at:at + n]
                        with sp.Fori(0, turns) as i:
                            stream(plan, stage, sizes, i, layer, offset + i * (sum(sizes) * P))
                        offset = offset + turns * sum(sizes) * P
                        at += n * turns
                    else:
                        for i in range(turns):
                            sizes = sizes_all[at:at + n]
                            stream(plan, stage, sizes, i, layer, offset)
                            offset = offset + sum(sizes) * P
                            at += n
                assert at == len(sizes_all)

            run(ADA0, ADA_SLOTS, ADA0.stages, 0, 0, ("ada",))
            with sp.Fori(0, LAYERS) as layer:
                run(LAYER, SLOTS_1, LAYER.stages, layer, layer * W1_TOTAL + ADA0_TOTAL,
                    ("gu_rest", "down"))
            run(SECOND, SLOTS_2, SECOND.stages, 0, LAYERS * W1_TOTAL + ADA0_TOTAL,
                ("att", "ssd", "ssdout"))

            ALL = SECOND.end["slot"]
            def expert_slot(b, n, dst, signal, freed, count):
                e = sp.value_load(expert_of[0:1, ds(b, 1)], min_val=0, max_val=E_N - 1)
                src = w_all[ds(e * EXPERT + (EXPERTS_AT + n * (EXPERT // 3)), EXPERT // 3)]
                sp.wait_ge(freed, count)
                sp.dma_start(dst, src.rearrange("(p n) -> p n", p=P)).then_inc(sem(signal), 16)

            sp.wait_ge(sem("experts_known"), 1)
            expert_slot(0, 0, ring[0], "wg_in", slot_free[0], ALL + 1)
            expert_slot(0, 1, ring[1], "wu_in", slot_free[1], ALL + 1)
            with sp.Fori(1, N_BLK) as b:
                expert_slot(b, 0, ring[0], "wg_in", sem("g_done"), b)
                expert_slot(b - 1, 2, wdown, "wd_in", sem("d_done"), b)
                expert_slot(b, 1, ring[1], "wu_in", sem("u_done"), b)
            expert_slot(N_BLK - 1, 2, wdown, "wd_in", sem("d_done"), N_BLK)

        @block.tensor
        def _(pe):
            for name in ("pv_done", "yd_done"):
                pe.sem_inc(sem(name), 2)
            pe.sem_inc(sem("t_done"), 4)
            pe.sem_inc(sem("d_done"), 1)

            def hk(k):
                return h[:, k, :]

            def slot_wait(p, use):
                pe.wait_ge(slot_full[p], (use + 1) * 16)

            def product(b, count, w, rhs, kc, m=P, ready=None):
                pe.wait_ge(lin_free[b], count + 1)
                for k in range(kc):
                    if ready is not None:
                        pe.wait_ge(*ready(k))
                    mm = pe.matmul(lin[b][0:m, :], w(k), rhs(k), start=(k == 0), stop=(k == kc - 1))
                mm.then_inc(lin_full[b], 1)

            def split_product(b, count, w_hi, w_lo, hi, lo, kc, ready=None):
                pe.wait_ge(lin_free[b], count + 1)
                for k in range(kc):
                    if ready is not None:
                        pe.wait_ge(*ready(k))
                    pe.matmul(lin[b], w_hi(k), hi(k), start=(k == 0), stop=False)
                    pe.matmul(lin[b], w_hi(k), lo(k), start=False, stop=False)
                    mm = pe.matmul(lin[b], w_lo(k), hi(k), start=False, stop=(k == kc - 1))
                mm.then_inc(lin_full[b], 1)

            def packed(p, at, m=P):
                return lambda k: ring[p][:, at + k * m:at + (k + 1) * m]

            def wide(p, ct, n=512):
                return lambda k: ring[p][:, k * n + ct * P:k * n + (ct + 1) * P]

            def column_sum(a, src, k, chunks, ready=None):
                if k == 0:
                    pe.wait_ge(aux_free, a + 1)
                if ready is not None:
                    pe.wait_ge(*ready(k))
                mm = pe.matmul(aux, ones, src(k), start=(k == 0), stop=(k == chunks - 1))
                if k == chunks - 1:
                    mm.then_inc(aux_full, 1)

            def column_sums(a, src, chunks, ready=None):
                for k in range(chunks):
                    column_sum(a, src, k, chunks, ready)

            def aux_product(a, lhsT, rhs, m=P, n=SEQ):
                pe.wait_ge(aux_free, a + 1)
                pe.matmul(aux[0:m, 0:n], lhsT, rhs, start=True, stop=True).then_inc(aux_full, 1)

            def aux_transposes(a, src, rows, stride):
                pe.wait_ge(aux_free, a + 1)
                hold(pe)
                for t in range(QT):
                    mm = pe.transpose(aux[:, t * stride:t * stride + rows], src[0:rows, t * P:(t + 1) * P],
                                      ident[0:rows, 0:rows])
                mm.then_inc(aux_full, 1)

            def head_norm(a, n):
                pe.wait_ge(sem("sq_done"), n + 1)
                aux_product(a, blockones, sq)

            def rotate(a, src):
                aux_product(a, rope, src)

            def rotate_normed(a, n, dst):
                pe.wait_ge(sem("normed"), n + 1)
                rotate(a, dst)

            def scores(g, bank_use, q, k, w, extra=None):
                h2, i = divmod(g, QT)
                lo = HD * h2
                b = g % 2
                pe.wait_ge(s_free[b], bank_use + 1)
                mm = pe.matmul(sc_b[b][:, 0:w], q[lo:lo + HD, i * P:(i + 1) * P], k[lo:lo + HD, 0:w],
                               start=True, stop=extra is None)
                if extra is not None:
                    mm = pe.matmul(sc_b[b][:, 0:w], extra[0:16, h2, :], negF[0:16, 0:w], start=False, stop=True)
                mm.then_inc(s_full[b], 1)

            def attention(u, s, o, q, k, v, values_ready=None, beside={}, extra=None):
                def turn_over(g):
                    i = g % QT
                    done(pe, "pn_done", u + g)
                    free(pe, "pts_done", u + g)
                    for kt in range(i + 1):
                        mm = pe.transpose(pt_b[g % 2][:, kt * P:(kt + 1) * P], pbuf[g % 4][:, kt * P:(kt + 1) * P],
                                          ident)
                    mm.then_inc(sem("t_done"), 1)

                def values(g):
                    h2, i = divmod(g, QT)
                    done(pe, "pts_done", u + g)
                    if g == 0:
                        pe.wait_ge(o_free, o + 1)
                        if values_ready is not None:
                            done(pe, "prep_done", values_ready)
                    for kt in range(i + 1):
                        mm = pe.matmul(ob[HD * h2:HD * h2 + HD, i * P:(i + 1) * P], v(kt, h2),
                                       pts[g % 2][:, kt * P:(kt + 1) * P], start=(kt == 0), stop=(kt == i))
                    mm.then_inc(sem("pv_done"), 1)

                for g in range(3):
                    scores(g, s + g // 2, q, k, P * (g % QT + 1), extra)
                for g in range(8):
                    if g in beside:
                        beside[g]()
                    turn_over(g)
                    if g + 3 < 8:
                        scores(g + 3, s + (g + 3) // 2, q, k, P * ((g + 3) % QT + 1), extra)
                    if g:
                        values(g - 1)
                if 8 in beside:
                    beside[8]()
                values(7)

            with pe.Fori(0, LAYERS) as layer:
                at = lambda stage, counter, turn=0: LAYER.at(stage, counter, turn, layer)
                column_sums(at("norm1", "aux"), hk, KC, lambda k: (sem("x_squared"), layer * (2 * KC) + (k + 1)))

                s, l, a, n = at("misc", "slot"), at("misc", "lin"), at("misc", "aux"), at("misc", "nrm")
                r = at("misc", "prep")
                slot_wait(0, s)
                product(0, l, packed(0, 0), hk, KC, ready=lambda k: (sem("h_ready"), layer * (2 * KC) + (k + 1)))
                product(1, l, packed(0, KC * P), hk, KC)
                head_norm(a, n)
                rotate_normed(a + 1, at("misc", "rope"), kaT)
                done(pe, "raw_done", r + 1)
                rotate(a + 2, raw[1])
                slot_wait(1, s)
                product(0, l + 1, packed(1, 0, HD), hk, KC, HD)
                product(1, l + 1, packed(1, KC * HD, 8), hk, KC, 8)
                done(pe, "raw_done", r + 2)
                aux_transposes(a + 3, raw[0], HD, HD)
                done(pe, "raw_done", r + 3)
                aux_transposes(a + 4, raw[1], 8, 8)

                def index_queries(j):
                    slot_wait(j % 2, at("idx", "slot") + j // 2)
                    product(j % 2, at("idx", "lin") + j // 2, packed(j % 2, 0), hk, KC)

                index_queries(0)
                for j in range(4):
                    b = j % 2
                    done(pe, "raw_done", at("idx", "prep") + j)
                    rotate(at("idx", "aux") + j, raw[b])
                    done(pe, "prep_done", at("idx", "prep") + j)
                    for g in range(6):
                        h2, i = g // 3, g % 3 + 1
                        pe.wait_ge(s_free[g % 2], at("idx", "s") + 3 * j + g // 2 + 1)
                        pe.matmul(sc_b[g % 2][:, 0:P * (i + 1)], qT[b][HD * h2:HD * h2 + HD, i * P:(i + 1) * P],
                                  kiT[HD * h2:HD * h2 + HD, 0:P * (i + 1)], start=True, stop=True)\
                            .then_inc(s_full[g % 2], 1)
                        if g == 1 and j < 3:
                            index_queries(j + 1)

                def prepare_b(j):
                    def part(n):
                        t = 3 * j + n
                        if n == 0:
                            slot_wait(j % 2, at("B", "slot") + j // 2)
                        else:
                            head_norm(at("B", "aux") + t - 1, at("B", "nrm") + 2 * j + n - 1)
                        product(t % 2, at("B", "lin") + t // 2, packed(j % 2, n * KC * P), hk, KC)

                    def turn_values():
                        t = 3 * j + 2
                        done(pe, "raw_done", at("B", "prep") + t)
                        aux_transposes(at("B", "aux") + t, raw[t % 2], P, P)

                    return {0: lambda: part(0), 3: lambda: part(1), 6: lambda: part(2), 8: turn_values}

                def prepare_a(j):
                    def queries():
                        slot_wait(j % 2, at("A", "slot") + j // 2)
                        product(j % 2, at("A", "lin") + j // 2, packed(j % 2, 0), hk, KC)

                    return {0: queries,
                            3: lambda: head_norm(at("A", "aux") + 2 * j, at("A", "nrm") + j),
                            6: lambda: rotate_normed(at("A", "aux") + 2 * j + 1, at("A", "rope") + j, qT[j % 2])}

                for step in prepare_b(0).values():
                    step()
                for j in range(4):
                    b, r = j % 2, at("B", "prep") + 3 * j
                    done(pe, "prep_done", r + 1)
                    attention(at("B", "u") + 8 * j, at("B", "s") + 4 * j, at("B", "o") + j, qT[b], kT[b],
                              lambda kt, h2: vtok[b][:, kt, HD * h2:HD * h2 + HD], r + 2,
                              prepare_b(j + 1) if j < 3 else prepare_a(0))
                for j in range(4):
                    b = j % 2
                    done(pe, "prep_done", at("A", "prep") + j)
                    attention(at("A", "u") + 8 * j, at("A", "s") + 4 * j, at("A", "o") + j, qT[b], kaT,
                              lambda kt, h2: va[:, kt, :], beside=prepare_a(j + 1) if j < 3 else {})

                pe.wait_ge(o_free, at("A", "o") + 5)
                hold(pe)
                with pe.Fori(0, 4) as i:
                    for p in range(2):
                        slot_wait(p, at("gates", "slot", i))
                        l = at("gates", "lin", i) + 2 * p
                        product(0, l, packed(p, 0), hk, KC)
                        product(1, l, packed(p, KC * P), hk, KC)
                        product(0, l + 1, packed(p, 2 * KC * P), lambda k: attA[:, k, :], 4)
                        product(1, l + 1, packed(p, 2 * KC * P + 4 * P), lambda k: attB[:, k, :], 4)
                pe.wait_ge(sem("merged_done"), layer + 1)
                for t in range(8):
                    if t % 4 == 0:
                        slot_wait(t // 4, at("out", "slot"))
                    product(t % 2, at("out", "lin") + t // 2, wide(t // 4, t % 4), lambda k: merged[:, k, :], KC)
                    for k in ([t - 1] if t in range(1, 7) else [6, 7] if t == 7 else []):
                        column_sum(at("norm2", "aux"), hk, k, KC,
                                   lambda k: (sem("x_squared"), layer * (2 * KC) + (KC + k + 1)))
                for stage, turns, first in (("gu", 8, 0), ("gu_rest", 3, 16)):
                    with pe.Fori(0, turns) as i:
                        for p in range(2):
                            pe.wait_ge(sem("w_split"), layer * SPLIT + 2 * i + (first + p + 1))
                            for b in range(2):
                                split_product(b, at(stage, "lin", i) + p,
                                              lambda k: w_hi[p][:, (b * KC + k) * P:(b * KC + k + 1) * P],
                                              lambda k: w_lo[p][:, (b * KC + k) * P:(b * KC + k + 1) * P],
                                              lambda k: h_hi[:, k, :], lambda k: h_lo[:, k, :], KC,
                                              (lambda k: (sem("h_split"), layer * KC + (k + 1))) if p + b == 0 else None)
                with pe.Fori(0, 4) as i:
                    for p in range(2):
                        pe.wait_ge(sem("w_split"), layer * SPLIT + 2 * i + (FF_T + p + 1))
                        split_product(p, at("down", "lin", i), lambda k: wd_hi[p][:, k * P:(k + 1) * P],
                                      lambda k: wd_lo[p][:, k * P:(k + 1) * P], lambda k: hid_hi[k],
                                      lambda k: hid_lo[:, k, :], FF_T,
                                      (lambda k: (sem("hid_split"), layer * FF_T + (k + 1))) if p == 0 else None)

            at = lambda stage, counter, turn=0: SECOND.at(stage, counter, turn)
            H0 = 2 * LAYERS

            def layer_norm(stage, n):
                pe.wait_ge(sem("x_ready"), 5 + n)
                column_sums(at(stage, "aux"), lambda k: x[:, k, :], KC)
                column_sums(at(stage, "aux") + 1, lambda k: merged2[:, k, :], KC,
                            lambda k: (sem("centred_squared"), n * KC + k + 1))

            layer_norm("ln1", 0)
            pe.wait_ge(sem("h_ready"), KC * (H0 + 1))

            slot_wait(0, at("fd", "slot"))
            product(0, at("fd", "lin"), packed(0, 0, 16), hk, KC, 16)
            slot_wait(1, at("fd", "slot"))
            product(1, at("fd", "lin"), packed(1, 0, 32), hk, KC, 32)
            pe.wait_ge(sem("f_done"), 1)
            aux_transposes(at("fd", "aux"), negF, 16, 16)
            pe.wait_ge(sem("acs_done"), 1)
            aux_transposes(at("fd", "aux") + 1, dtT, 32, 32)
            aux_transposes(at("fd", "aux") + 2, acs, 32, 32)
            pe.wait_ge(sem("acs_tok_done"), 1)
            aux_product(at("fd", "aux") + 3, last, acs_tok.rearrange("p a b -> p (a b)"), P, QT * 32)

            def prepare(i, b):
                def part(n):
                    t = 3 * b + n
                    if n == 0:
                        slot_wait(b, at("att", "slot", i))
                    product(t % 2, at("att", "lin", i) + t // 2, packed(b, n * KC * P), hk, KC)

                def turn_values():
                    t = 3 * b + 2
                    done(pe, "raw_done", at("att", "prep", i) + t)
                    aux_transposes(at("att", "aux", i) + b, raw[b], P, P)

                return {0: lambda: part(0), 3: lambda: part(1), 6: lambda: part(2), 8: turn_values}

            def pair(i, b, beside):
                r = at("att", "prep", i) + 3 * b
                done(pe, "prep_done", r + 1)
                attention(at("att", "u", i) + 8 * b, at("att", "s", i) + 4 * b, at("att", "o", i) + b,
                          qT[b], kT[b], lambda kt, h2: vtok[b][:, kt, HD * h2:HD * h2 + HD], r + 2, beside, fsel[b])

            for step in prepare(0, 0).values():
                step()
            with pe.Fori(0, 3) as i:
                pair(i, 0, prepare(i, 1))
                pair(i, 1, prepare(i + 1, 0))
            pair(3, 0, prepare(3, 1))
            pair(3, 1, {})
            pe.wait_ge(o_free, at("att", "o") + 9)
            with pe.Fori(0, 4) as i:
                for p in range(2):
                    slot_wait(p, at("attout", "slot", i))
                    product(0, at("attout", "lin", i) + p, packed(p, 0), hk, KC)
                    product(1, at("attout", "lin", i) + p, packed(p, KC * P), lambda k: att2[:, k, :], KC)

            for g in range(4):
                l = at("pool", "lin", g)
                slot_wait(0, at("pool", "slot", g))
                product(0, l, wide(0, 0, 256), hk, KC)
                product(1, l, wide(0, 1, 256), hk, KC)
                slot_wait(1, at("pool", "slot", g))
                product(0, l + 1, wide(1, 0, 256), hk, KC)
                pe.wait_ge(sem("pooled_done"), g + 1)
                wp = lambda ct: (lambda k: ring[1][:, KC * 256 + k * 256 + ct * P:KC * 256 + k * 256 + (ct + 1) * P])
                product(1, l + 1, wp(0), lambda k: pooled[k], 2)
                product(0, l + 2, wide(1, 1, 256), hk, KC)
                product(1, l + 2, wp(1), lambda k: pooled[k], 2)

            with pe.Fori(0, 4) as i:
                l, s = at("ssd", "lin", i), at("ssd", "slot", i)
                slot_wait(0, s)
                for t in range(4):
                    product(t % 2, l + t // 2, wide(0, t), hk, KC)
                slot_wait(1, s)
                for t in range(2):
                    product(t, l + 2, wide(1, t, 256), hk, KC)
                slot_wait(0, s + 1)
                for t in range(2):
                    product(t, l + 3, wide(0, t, 256), hk, KC)
                done(pe, "silu_done", i * 6 + 3)
                for c in range(QT):
                    free(pe, "xd_done", i * 4 + c)
                    for t in range(4):
                        mm = pe.transpose(pt_b[c % 2][:, t * P:(t + 1) * P], xsT[:, t, c * P:(c + 1) * P], ident)
                    mm.then_inc(sem("xt_done"), 1)
                done(pe, "silu_done", i * 6 + 5)
                pe.wait_ge(sem("yp_done"), i * 4 + 1)
                for c in range(QT):
                    mm = pe.transpose(ob[:, c * P:(c + 1) * P], bmT[:, c * P:(c + 1) * P], ident)
                mm.then_inc(sem("bt_done"), 1)
                done(pe, "seg_done", i * 8 - 1)
                for c in range(QT):
                    mm = pe.matmul(sc_b[0][:, c * P:(c + 1) * P], bmT[:, c * P:(c + 1) * P],
                                   cmT[:, c * P:(c + 1) * P], start=True, stop=True)
                mm.then_inc(sem("cb_done"), 1)
                pe.wait_ge(sem("btok_done"), i + 1)
                done(pe, "xd_done", i * 4 + 3)
                for c in range(3):
                    if c == 2:
                        pe.wait_ge(sem("hst_done"), i * 3 + 1)
                    pe.matmul(pt_b[c % 2], btok[:, c, :], xde[:, c, :], start=True, stop=True)\
                        .then_inc(sem("st_done"), 1)
                pe.wait_ge(sem("cbm_done"), i + 1)

                def decay_row(hh):
                    free(pe, "seg_done", i * 8 + hh)
                    pe.matmul(sc_b[hh % 2], selh[0:32, hh, :], acs[0:32, :], start=True, stop=True)\
                        .then_inc(sem("bc_done"), 1)

                decay_row(0)
                decay_row(1)
                pe.wait_ge(sem("hst_done"), i * 3 + 3)
                for j in range(4):
                    pe.wait_ge(sem("yp_done"), i * 4 + j + 1)
                    pe.matmul(pt_b[1], selp[0:32, j, :], acs[0:32, :], start=True, stop=True)\
                        .then_inc(sem("eab_done"), 1)
                    for h2 in range(2):
                        for c in range(3):
                            mm = pe.matmul(pt_b[0][HD * h2:HD * h2 + HD, (c + 1) * P:(c + 2) * P],
                                           hst[:, c, (2 * j + h2) * HD:(2 * j + h2 + 1) * HD],
                                           cmT[:, (c + 1) * P:(c + 2) * P], start=True, stop=True)
                    mm.then_inc(sem("yoff_done"), 1)
                    for h2 in range(2):
                        hh = 2 * j + h2
                        done(pe, "wgt_done", i * 8 + hh)
                        for c in range(QT):
                            mm = pe.matmul(ob[HD * h2:HD * h2 + HD, c * P:(c + 1) * P],
                                           xdt[:, c, hh * HD:(hh + 1) * HD], wgt[hh % 2][:, c * P:(c + 1) * P],
                                           start=True, stop=True)
                        mm.then_inc(sem("yd_done"), 1)
                        if hh + 2 < 8:
                            decay_row(hh + 2)
                        if hh == 3:
                            slot_wait(1, s + 1)
                            product(0, l + 4, wide(1, 0, 256), hk, KC)
                product(1, l + 4, wide(1, 1, 256), hk, KC)
                column_sums(at("ssd", "aux", i), lambda k: xdt[:, k, :], 4,
                            lambda k: (sem("yg_squared"), i * 4 + (k + 1)))

            pe.wait_ge(sem("yT_done"), 4)
            with pe.Fori(0, 4) as i:
                for p in range(2):
                    slot_wait(p, at("ssdout", "slot", i))
                    product(0, at("ssdout", "lin", i) + p, packed(p, 0), hk, KC)
                    product(1, at("ssdout", "lin", i) + p, packed(p, KC * P), lambda k: yT[:, k, :], 16)
            pe.wait_ge(sem("merged2_done"), 1)
            for t in range(8):
                if t % 4 == 0:
                    slot_wait(t // 4, at("out", "slot"))
                product(t % 2, at("out", "lin") + t // 2, wide(t // 4, t % 4), lambda k: merged2[:, k, :], KC)
            layer_norm("ln2", 1)
            layer_norm("ln3", 2)
            pe.wait_ge(sem("h_ready"), KC * (H0 + 2))

            pe.wait_ge(aux_free, at("router", "aux") + 1)
            for t in range(QT):
                for k in range(KC):
                    mm = pe.matmul(aux[:, t * E_N:(t + 1) * E_N], h[:, k, t * P:(t + 1) * P],
                                   v2("w_router", k * E_N, E_N), start=(k == 0), stop=(k == KC - 1))
            mm.then_inc(aux_full, 1)
            a = at("router", "aux")
            for t in range(QT):
                for half in range(2):
                    n = 2 * t + half
                    if n >= 4:
                        pe.wait_ge(sem("htok_done"), n - 3)
                    bank = (sc_b, pt_b)[half][t % 2]
                    for k in range(4):
                        mm = pe.transpose(bank[:, k * P:(k + 1) * P], h[:, 4 * half + k, t * P:(t + 1) * P], ident)
                    mm.then_inc(sem("ht_done"), 1)
            pe.wait_ge(sem("chosen"), 1)
            pe.wait_ge(aux_free, a + 2)
            for t in range(QT):
                mm = pe.transpose(aux[0:E_N, t * P:(t + 1) * P], gw[:, t, :], ident)
            mm.then_inc(aux_full, 1)
            pe.wait_ge(sem("blocks_counted"), 1)
            pe.wait_ge(aux_free, a + 3)
            pe.matmul(aux[0:E_N, 0:1], tri[0:E_N, 0:E_N], n_blocks[0:E_N, :], start=True, stop=True)\
                .then_inc(aux_full, 1)
            pe.wait_ge(sem("past_done"), 1)
            pe.wait_ge(aux_free, a + 4)
            pe.matmul(aux[:, 0:N_BLK], ones[0:E_N, :], past[0:E_N, :], start=True, stop=True).then_inc(aux_full, 1)
            pe.wait_ge(sem("position_done"), 1)
            pe.wait_ge(aux_free, a + 5)
            for t in range(QT):
                mm = pe.transpose(aux[:, t * E_N:(t + 1) * E_N], position[0:E_N, t * P:(t + 1) * P],
                                  ident[0:E_N, 0:E_N])
            mm.then_inc(aux_full, 1)

            def rows_in(b):
                pe.wait_ge(sem("rows_in"), b * 16 + 16)
                for k in range(KC):
                    mm = pe.transpose(pt_b[k // 4][:, (k % 4) * P:(k % 4 + 1) * P], xr[:, k * P:(k + 1) * P], ident)
                mm.then_inc(sem("rows_turned"), 1)

            def up_products(w, par, bank, signal):
                for ct in range(4):
                    for k in range(KC):
                        mm = pe.matmul(bank[:, ct * P:(ct + 1) * P],
                                       w[:, k * E_FF + ct * P:k * E_FF + (ct + 1) * P],
                                       xT[par][:, k * P:(k + 1) * P], start=(k == 0), stop=(k == KC - 1))
                mm.then_inc(sem(signal), 1)

            def gate_block(b, par):
                pe.wait_ge(sem("wg_in"), b * 16 + 16)
                pe.wait_ge(sem("xTa_done"), b + 1)
                pe.wait_ge(sem("xTd_done"), b + 1)
                up_products(ring[0], par, lin[0], "g_done")

            def up_block(b, par):
                pe.wait_ge(sem("wu_in"), b * 16 + 16)
                up_products(ring[1], par, lin[1], "u_done")

            def down_block(b):
                pe.wait_ge(sem("wd_in"), b * 16 + 16)
                pe.wait_ge(sem("hidden"), b + 1)
                pe.wait_ge(sem("ya_done"), b + 1)
                pe.wait_ge(sem("yd2_done"), b + 1)
                for half in range(2):
                    for k in range(4):
                        mm = pe.matmul(sc_b[half], hidb[:, k * P:(k + 1) * P],
                                       wdown[:, k * D + half * SEQ:k * D + (half + 1) * SEQ],
                                       start=(k == 0), stop=(k == 3))
                mm.then_inc(sem("d_done"), 1)

            for p in range(2):
                pe.wait_ge(lin_free[p], SECOND.end["lin"] + 1)
            pe.wait_ge(sem("htok_done"), 2 * QT)
            rows_in(0)
            gate_block(0, 0)
            rows_in(1)
            up_block(0, 0)
            with pe.Fori(0, (N_BLK - 1) // 2) as i:
                for n in range(2):
                    b, par = 2 * i + (n + 1), (n + 1) % 2
                    pe.wait_ge(sem("silu_read"), b)
                    gate_block(b, par)
                    down_block(b - 1)
                    rows_in(b + 1)
                    up_block(b, par)
            down_block(N_BLK - 1)

            for t in range(QT):
                pe.wait_ge(sem("combined"), t + 1)
                if t >= 2:
                    pe.wait_ge(sem("ffn_done"), 2 * t - 2)
                elif t == 0:
                    pe.wait_ge(sem("ya_done"), N_BLK + 1)
                    pe.wait_ge(sem("yd2_done"), N_BLK + 1)
                    pe.wait_ge(sem("xTa_done"), N_BLK + 1)
                    pe.wait_ge(sem("xTd_done"), N_BLK + 1)
                for half in range(2):
                    bank = (sc_b, pt_b)[half][t % 2]
                    for k in range(4):
                        mm = pe.transpose(bank[:, k * P:(k + 1) * P],
                                          htok[:, t, (4 * half + k) * P:(4 * half + k + 1) * P], ident)
                    mm.then_inc(sem("turned_back"), 1)
            layer_norm("ln4", 3)

        @block.scalar
        def _(act):
            mine = Steps(act, sem("act_steps"))
            tell = mine.tell
            for dst, src in ((cst[:, :], consts), (csil, cond[:, 0:D]), (raw[0].bitcast(I32), pos_in),
                             (x[:, :, :], x_in), (vec2[:, :], vec2_all)):
                act.dma_start(dst, src).then_inc(boot, 16)
            for s in (slot_free[0], slot_free[1], o_free):
                act.sem_inc(s, 1)
            for name in ("exp_done", "pts_done", "raw_done", "rl_done", "silu_done"):
                act.sem_inc(sem(name), 2)
            act.sem_inc(sem("ya_done"), 1)

            act.wait_ge(boot, 80)
            tell(act.activation(csil, csil, ACT.Silu), sem("c_ready"))
            act.wait_ge(sem("angle_done"), 1)
            mine(act.activation(sinT[:, :], tmp[:, :], ACT.Sin))
            tell(act.activation(cosT[:, :], tmp[:, :], ACT.Sin, scale=0.5), sem("sin_done"))

            def root(out, scale, eps, a):
                act.wait_ge(aux_full, a + 1)
                tell(act.activation(out, aux, ACT.Sqrt, scale=scale, bias=eps), sem("root_done"))

            def affine(dst, scaled, scale, shift, signal=None, upper=None):
                for k in range(KC):
                    act.wait_ge(sem("scaled"), scaled + k + 1)
                    mine(act.activation(dst[:, k, :], dst[:, k, :], ACT.Identity, scale=scale(k), bias=shift(k)))
                    if signal is None:
                        act.sem_inc(sem("h_ready"), 1)
                    if upper is not None:
                        tell(act.activation(upper[:, k, :], dst[:, k, :], ACT.Copy), sem("h_upper"))
                if signal is not None:
                    act.sem_inc(signal, 1)

            def rms_norm(n, a, gain0, shift0, upper=None, meanwhile=None, whole=False):
                for k in range(KC):
                    act.wait_ge(sem("x_tiles"), n * KC + (KC if whole else k + 1))
                    act.activation(h[:, k, :], x[:, k, :], ACT.Square).then_inc(sem("x_squared"), 1)
                if meanwhile is not None:
                    meanwhile()
                root(rstd[:, :], 1.0 / D, EPS, a)
                affine(h, n * KC, lambda k: gain[:, gain0 + k:gain0 + k + 1],
                       lambda k: mod[:, shift0 + k:shift0 + k + 1], upper=upper)

            def take_tile(b, count, slot=None):
                act.wait_ge(lin_full[b], count + 1)
                if slot is not None:
                    act.sem_inc(slot_free[slot], 1)

            def project(b, count, r, par, bias, m=P, slot=None, dst=None, scale=1.0):
                take_tile(b, count, slot)
                free(act, "prep_done", r)
                dst = raw[par] if dst is None else dst
                act.activation(dst[0:m, :], lin[b][0:m, :], ACT.Identity, bias=bias, scale=scale).then_inc(sem("raw_done"), 1)

            def head_root(a):
                act.wait_ge(aux_full, a + 1)
                act.activation(rs[:, :], aux, ACT.Sqrt, scale=1.0 / HD, bias=EPS).then_inc(sem("rs_done"), 1)

            def attention(u, dst, beside={}):
                def evacuate(g):
                    w = P * (g % QT + 1)
                    act.wait_ge(sem("t_done"), u + g + 5)
                    free(act, "pv_done", u + g)
                    act.activation(pts[g % 2][:, 0:w], pt_b[g % 2][:, 0:w], ACT.Copy).then_inc(sem("pts_done"), 1)

                for g in range(8):
                    p = pbuf[g % 4][:, 0:P * (g % QT + 1)]
                    done(act, "nmax_done", u + g)
                    act.activation(p, p, ACT.Exp, bias=nmax[:, g:g + 1], accum_out=esum[:, g:g + 1])\
                        .then_inc(sem("exp_done"), 1)
                    if g in beside:
                        beside[g]()
                    if g >= 2:
                        evacuate(g - 2)
                if 8 in beside:
                    beside[8]()
                evacuate(6)
                evacuate(7)
                done(act, "pv_done", u + 7)
                act.activation(dst, ob, ACT.Copy).then_inc(o_free, 1)

            def gate(b, count, n, par, func, bias=0.0, slot=None):
                take_tile(b, count, slot)
                act.wait_ge(sem("sg_free"), n + 1)
                act.activation(sg[par][:, :], lin[b], func, bias=bias).then_inc(sem("sg_done"), 1)

            with mine.loop(0, LAYERS) as layer:
                at = lambda stage, counter, turn=0: LAYER.at(stage, counter, turn, layer)
                act.dma_start(vec[:, :], vec1_all[ds(layer * (P * NV1), P * NV1)].rearrange("(p n) -> p n", p=P))\
                    .then_inc(vec_in, 16)
                act.wait_ge(vec_in, layer * 16 + 16)

                def load_bias():
                    act.dma_start(relb, rel[ds(layer * (P * 8 * SEQ), P * 8 * SEQ)]
                                  .rearrange("(p a b) -> p a b", p=P, a=8)).then_inc(rel_in, 16)

                rms_norm(layer * 2, at("norm1", "aux"), 0, 0, meanwhile=load_bias, whole=True)

                l, r = at("misc", "lin"), at("misc", "prep")
                project(0, l, r, 0, v1("ka"))
                project(1, l, r + 1, 1, v1("ki"), slot=0)
                head_root(at("misc", "aux"))
                project(0, l + 1, r + 2, 0, v1("va")[0:HD], HD)
                project(1, l + 1, r + 3, 1, v1("wi")[0:8], 8, slot=1)

                def index_queries(j):
                    b = j % 2
                    project(b, at("idx", "lin") + j // 2, at("idx", "prep") + j, b, v1("qi", j), slot=b)

                index_queries(0)
                for j in range(4):
                    for g in range(6):
                        w = P * (g % 3 + 2)
                        act.wait_ge(s_full[g % 2], at("idx", "s") + 3 * j + g // 2 + 1)
                        free(act, "acc_done", at("idx", "iu") + 6 * j + g)
                        act.activation(sm[g % 2][:, 0:w], sc_b[g % 2][:, 0:w], ACT.Relu).then_inc(sem("rl_done"), 1)
                        if g == 1 and j < 3:
                            index_queries(j + 1)

                def prepare_b(j):
                    def part(n):
                        t = 3 * j + n
                        if n:
                            head_root(at("B", "aux") + t - 1)
                        project(t % 2, at("B", "lin") + t // 2, at("B", "prep") + t, t % 2,
                                v1(("qb", "kb", "vb")[n], j), slot=j % 2 if n == 2 else None)

                    return {2: lambda: part(0), 5: lambda: part(1), 8: lambda: part(2)}

                def prepare_a(j):
                    b = j % 2
                    return {2: lambda: project(b, at("A", "lin") + j // 2, at("A", "prep") + j, b, v1("qa", j), slot=b),
                            5: lambda: head_root(at("A", "aux") + 2 * j)}

                for step in prepare_b(0).values():
                    step()
                for j in range(4):
                    attention(at("B", "u") + 8 * j, attB[:, j, :], prepare_b(j + 1) if j < 3 else prepare_a(0))
                for j in range(4):
                    attention(at("A", "u") + 8 * j, attA[:, j, :], prepare_a(j + 1) if j < 3 else {})

                with mine.loop(0, 4) as i:
                    for p in range(2):
                        l, n = at("gates", "lin", i) + 2 * p, at("gates", "sg", i) + 2 * p
                        gate(0, l, n, 0, ACT.Sigmoid, v1d("ga", 2 * i + p))
                        gate(1, l, n + 1, 1, ACT.Sigmoid, v1d("gb", 2 * i + p))

                def upper_half(stage, i, p):
                    act.wait_ge(slot_full[p], at(stage, "slot", i) * 16 + 16)
                    tell(act.activation(w_hi[p], ring[p][:, 0:2 * KC * P], ACT.Copy), sem("w_upper"))

                act.wait_ge(sem("mod_summed"), layer + 1)
                act.dma_start(csil, cond[:, ds(layer * D + D, D)]).then_inc(sem("c_in"), 16)

                def before_root():
                    upper_half("gu", 0, 0)
                    act.wait_ge(sem("c_in"), layer * 16 + 16)
                    tell(act.activation(csil, csil, ACT.Silu), sem("c_ready"))

                rms_norm(layer * 2 + 1, at("norm2", "aux"), 8, 24, h_hi, before_root)

                def turn(stage, i, last=False):
                    for p in range(2):
                        if p == 0:
                            upper_half(stage, i, 1)
                        elif not last:
                            upper_half(stage, i + 1, 0)
                        gate(0, at(stage, "lin", i) + p, at(stage, "sg", i) + p, p, ACT.Silu)

                with mine.loop(0, 8) as i:
                    turn("gu", i)
                with mine.loop(0, 2) as i:
                    turn("gu_rest", i)
                turn("gu_rest", 2, last=True)

                def upper_down(i, p):
                    act.wait_ge(slot_full[p], at("down", "slot", i) * 16 + 16)
                    tell(act.activation(wd_hi[p], ring[p][:, 0:FF_T * P], ACT.Copy), sem("w_upper"))

                upper_down(0, 0)
                act.wait_ge(sem("hid_done"), layer + 1)
                for k in range(FF_T):
                    act.activation(hid_hi[k], hid[:, k, :], ACT.Copy).then_inc(sem("hid_upper"), 1)
                mine.restart()
                with mine.loop(0, 3) as i:
                    upper_down(i, 1)
                    upper_down(i + 1, 0)
                upper_down(3, 1)

            at = lambda stage, counter, turn=0: SECOND.at(stage, counter, turn)
            SC0 = 2 * LAYERS * KC

            def layer_norm(stage, n, dst, scale, shift, signal):
                for k in range(KC):
                    act.wait_ge(sem("centred"), n * KC + k + 1)
                    act.activation(merged2[:, k, :], dst[:, k, :], ACT.Square).then_inc(sem("centred_squared"), 1)
                root(rstd[:, :], 1.0 / D, LN_EPS, at(stage, "aux") + 1)
                affine(dst, SC0 + n * KC, scale, shift, signal)

            mod_at = lambda k0: (lambda k: mod[:, k0 + k:k0 + k + 1])
            gain_at = lambda k0: (lambda k: gain[:, k0 + k:k0 + k + 1])
            v2_at = lambda name: (lambda k: v2(name, k))
            layer_norm("ln1", 0, h, gain_at(0), mod_at(0), None)

            for n, (m, bias) in enumerate(((16, v2("b_forget")[0:16]), (32, v2("dt_bias")[0:32]))):
                take_tile(n, at("fd", "lin"), slot=n)
                tell(act.activation(raw[n][0:m, :], lin[n][0:m, :], ACT.Identity, bias=bias), sem("fd_raw"))
                act.wait_ge(sem("fd_raw"), n + 1)
                tell(act.activation(sm[n][0:m, :], raw[n][0:m, :], ACT.Abs), sem("fd_act"))
                act.wait_ge(sem("fd_act"), 3 * n + 1)
                tell(act.activation(sm[n][0:m, :], sm[n][0:m, :], ACT.Exp, scale=-1.0), sem("fd_act"))
                act.wait_ge(sem("fd_act"), 3 * n + 2)
                tell(act.activation(sm[n][0:m, :], sm[n][0:m, :], ACT.Ln, bias=1.0), sem("fd_act"))
            tell(act.activation(gain[0:32, 0:1], v2("a_log")[0:32], ACT.Exp), sem("a_done"))
            act.wait_ge(aux_full, at("fd", "aux") + 4)
            tell(act.activation(cd_tok.rearrange("p a b -> p (a b)"), aux[:, 0:QT * 32], ACT.Exp), sem("cd_done"))
            act.wait_ge(sem("te_diff"), 1)
            tell(act.activation(te_tok, te_tok, ACT.Exp), sem("te_exp"))

            act.wait_ge(sem("zeros_out"), 16)
            def prepare(i, b):
                def part(n):
                    t = 3 * b + n
                    project(t % 2, at("att", "lin", i) + t // 2, at("att", "prep", i) + t, b, 0.0,
                            slot=b if n == 2 else None, dst=(qT[b], kT[b], raw[b])[n], scale=HD ** -0.5 if n == 0 else 1.0)

                return {2: lambda: part(0), 5: lambda: part(1), 8: lambda: part(2)}

            def pair(i, b, beside):
                dst = att2[:, 2 * i + b, :] if isinstance(i, int) else att2[:, ds(2 * i + b, 1), :]
                attention(at("att", "u", i) + 8 * b, dst, beside)

            for step in prepare(0, 0).values():
                step()
            with mine.loop(0, 3) as i:
                pair(i, 0, prepare(i, 1))
                pair(i, 1, prepare(i + 1, 0))
            pair(3, 0, prepare(3, 1))
            pair(3, 1, {})
            with mine.loop(0, 4) as i:
                for p in range(2):
                    gate(0, at("attout", "lin", i) + p, at("attout", "sg", i) + p, p, ACT.Sigmoid)
            for g in range(4):
                l = at("pool", "lin", g)
                for t in range(2):
                    take_tile(t, l, slot=0 if t == 1 else None)
                    act.wait_ge(sem("ub_free"), 2 * g + t + 1)
                    tell(act.activation(ub[t][:, 16:16 + SEQ], lin[t], ACT.Copy), sem("ub_done"))
                gate(0, l + 1, at("pool", "sg", g), 0, ACT.Sigmoid)
                gate(0, l + 2, at("pool", "sg", g) + 1, 1, ACT.Sigmoid)

            with mine.loop(0, 4) as i:
                l = at("ssd", "lin", i)

                def conv_in(t):
                    take_tile(t % 2, l + t // 2, slot={3: 0, 5: 1}.get(t))
                    free(act, "conv_done", i * 6 + t)
                    tell(act.activation(cin[t % 2][:, 3:], lin[t % 2], ACT.Copy), sem("cin_done"))

                def conv_out(t):
                    done(act, "conv_done", i * 6 + t)
                    dst = xsT[:, t, :] if t < 4 else (bmT, cmT)[t - 4]
                    tell(act.activation(dst, cv[t % 2], ACT.Silu, bias=gpar[:, 5 * t + 4:5 * t + 5]), sem("silu_done"))

                act.wait_ge(sem("gpar_done"), i + 1)
                for t in range(6):
                    conv_in(t)
                    if t:
                        conv_out(t - 1)
                conv_out(5)

                def gate_z(t):
                    gate(t % 2, l + 3 + t // 2, at("ssd", "sg", i) + t, t % 2, ACT.Silu, slot={1: 0, 3: 1}.get(t))

                for t in range(2):
                    gate_z(t)
                for j in range(4):
                    act.wait_ge(sem("eab_done"), i * 4 + j + 1)
                    act.wait_ge(sem("yp_done"), i * 4 + j + 1)
                    tell(act.activation(ea, pt_b[1], ACT.Exp), sem("ea_done"))
                    for hh in (2 * j, 2 * j + 1):
                        done(act, "seg_done", i * 8 + hh)
                        tell(act.activation(seg[hh % 2], seg[hh % 2], ACT.Exp), sem("e_done"))
                for t in range(2, 4):
                    gate_z(t)
                for t in range(4):
                    act.wait_ge(sem("yz_done"), i * 4 + (t + 1))
                    tell(act.activation(xdt[:, t, :], yg[:, t, :], ACT.Square), sem("yg_squared"))
                root(rstd[:, :], 1.0 / SEQ, EPS, at("ssd", "aux", i))
            with mine.loop(0, 4) as i:
                for p in range(2):
                    gate(0, at("ssdout", "lin", i) + p, at("ssdout", "sg", i) + p, p, ACT.Sigmoid)

            layer_norm("ln2", 1, x, v2_at("ln_mix_g"), v2_at("ln_mix_b"), sem("x_ready"))
            layer_norm("ln3", 2, h, gain_at(8), mod_at(24), None)
            act.wait_ge(sem("logit_done"), 1)
            tell(act.activation(rt[0], rt[0], ACT.Exp), sem("probs_exp"))
            for t in range(QT):
                for half in range(2):
                    act.wait_ge(sem("ht_done"), 2 * t + half + 1)
                    tell(act.activation(htok[:, t, half * SEQ:(half + 1) * SEQ], (sc_b, pt_b)[half][t % 2], ACT.Copy),
                         sem("htok_done"))

            def rows_half(b, par):
                act.wait_ge(sem("rows_turned"), b + 1)
                tell(act.activation(xT[par][:, 0:SEQ], pt_b[0], ACT.Copy), sem("xTa_done"))

            def gate_half(b):
                act.wait_ge(sem("g_done"), b + 1)
                tell(act.activation(sg[0][:, :], lin[0], ACT.Silu), sem("silu_read"))

            def made_half(b, par, first=False):
                act.wait_ge(sem("d_done"), b + 2)
                if not first:
                    act.wait_ge(sem("made_out"), (b - 1) * 16)
                tell(act.activation(yb[par][:, 0:SEQ], sc_b[0], ACT.Copy), sem("ya_done"))

            rows_half(0, 0)
            gate_half(0)
            rows_half(1, 1)

            def step(b, par, first=False):
                act.wait_ge(sem("hidden"), b)
                gate_half(b)
                made_half(b - 1, 1 - par, first)
                rows_half(b + 1, 1 - par)

            for b in (1, 2):
                step(b, b % 2, True)
            with mine.loop(1, (N_BLK - 1) // 2) as i:
                for n in range(2):
                    step(2 * i + (n + 1), (n + 1) % 2)
            made_half(N_BLK - 1, (N_BLK - 1) % 2)
            for t in range(QT):
                for half in range(2):
                    act.wait_ge(sem("turned_back"), 2 * t + half + 1)
                    tell(act.activation(moe[:, 4 * half:4 * half + 4, t * P:(t + 1) * P],
                                        (sc_b, pt_b)[half][t % 2].rearrange("p (a b) -> p a b", b=P), ACT.Copy),
                         sem("ffn_done"))
            layer_norm("ln4", 3, x, v2_at("ln_ffn_g"), v2_at("ln_ffn_b"), sem("x_final"))
            act.wait_ge(sem("x_final"), 1)
            act.dma_start(out, x[:, :, :]).then_inc(out_done, 16)
            act.wait_ge(out_done, 16)

        @block.vector
        def _(dve):
            mine = Steps(dve, sem("dve_steps"))
            tell = mine.tell
            TT, TS, STT = dve.tensor_tensor, dve.tensor_scalar, dve.scalar_tensor_tensor
            MUL, ADD, SUB, MAX, MIN = ALU.mult, ALU.add, ALU.subtract, ALU.max, ALU.min

            for s in (lin_free[0], lin_free[1], aux_free, s_free[0], s_free[1], sem("yp_done")):
                dve.sem_inc(s, 1)
            for name in ("nmax_done", "prep_done", "acc_done", "conv_done", "seg_done", "xd_done", "sg_free",
                         "ub_free"):
                dve.sem_inc(sem(name), 2)
            dve.sem_inc(sem("yd2_done"), 1)
            dve.sem_inc(sem("wada_free"), 1)

            TWO_PI = 2 * np.pi
            c1 = 6.28125
            c2 = float(np.float32(np.round((TWO_PI - c1) * 2 ** 20) / 2 ** 20))
            c3 = float(TWO_PI - c1 - c2)
            MAGIC = 1.5 * 2 ** 23
            ang, turns = sm[0], sm[1]
            dve.wait_ge(boot, 80)
            dve.sem_inc(sem("x_ready"), 1)
            dve.sem_inc(sem("x_tiles"), KC)
            mine(dve.tensor_copy(ang, raw[0].bitcast(I32)))
            mine(TS(ang, ang, col("inv_freq"), None, MUL))
            mine(TS(turns, ang, 1 / TWO_PI, MAGIC, MUL, ADD))
            mine(TS(turns, turns, MAGIC, None, SUB))
            for c in (c1, c2, c3):
                mine(STT(ang, turns, -c, ang, MUL, ADD))
            PI = 3.1415925
            tell(TS(tmp[:, :], ang, PI, -PI, MIN, MAX), sem("angle_done"))
            dve.wait_ge(sem("sin_done"), 1)
            mine(TT(cosT[:, :], cosT[:, :], cosT[:, :], MUL))
            mine(TS(cosT[:, :], cosT[:, :], -2.0, 1.0, MUL, ADD))
            mine.restart()

            def lin_wait(b, count):
                dve.wait_ge(lin_full[b], count + 1)

            def modulate(weights, k0, tiles, signal, bias=None):
                for n in range(tiles):
                    w = weights[:, n * D:(n + 1) * D]
                    mine(dve.tensor_tensor_reduce(w, w, csil, 1.0, 0.0, MUL, ADD, mod_sum[:, n:n + 1]))
                dve.sem_inc(signal, 1)
                if bias is None:
                    mine(dve.tensor_copy(mod_next[:, ds(k0, tiles)], mod_sum[:, 0:tiles]))
                else:
                    mine(TT(mod[:, ds(k0, tiles)], mod_sum[:, 0:tiles], bias("b_ada", k0, tiles), ADD))

            def modulate_beside(stage, i, p, layer, bias=None):
                parts, tiles, before = BESIDE[stage]
                for m in range(parts):
                    n = 2 * parts * i + (parts * p + m)
                    dve.wait_ge(sem("wada_in"), layer * (16 * PARTS) + n * 16 + (16 * before + 16))
                    modulate(wada, n * tiles + (0 if bias is None else 16), tiles, sem("wada_free"), bias)

            def gains(at0, k0, g):
                if g is None:
                    mine(TS(gain[:, at0:at0 + 8], mod[:, k0:k0 + 8], 1.0, None, ADD))
                else:
                    mine(STT(gain[:, at0:at0 + 8], mod[:, k0:k0 + 8], 1.0, g, ADD, MUL))

            def rms_norm(n, a, n_root, split=None):
                dve.wait_ge(sem("root_done"), n_root + 1)
                tell(dve.reciprocal(rstd[:, :], rstd[:, :]), aux_free)
                dve.wait_ge(aux_free, a + 2)
                for k in range(KC):
                    TT(h[:, k, :], x[:, k, :], rstd[:, :], MUL).then_inc(sem("scaled"), 1)
                    if split is not None and k >= 2:
                        split(k - 2)
                if split is not None:
                    split(KC - 2)
                    split(KC - 1)

            def layer_norm(stage, n, dst, n_root):
                a = SECOND.at(stage, "aux")
                dve.wait_ge(aux_full, a + 1)
                tell(TS(tmp[:, :], aux, 1.0 / D, None, MUL), aux_free)
                dve.wait_ge(aux_free, a + 2)
                for k in range(KC):
                    TT(dst[:, k, :], x[:, k, :], tmp[:, :], SUB).then_inc(sem("centred"), 1)
                dve.wait_ge(sem("root_done"), n_root + 1)
                tell(dve.reciprocal(rstd[:, :], rstd[:, :]), aux_free)
                dve.wait_ge(aux_free, a + 3)
                for k in range(KC):
                    TT(dst[:, k, :], dst[:, k, :], rstd[:, :], MUL).then_inc(sem("scaled"), 1)

            def norm_tile_end(a, n, par, dst, g, signal):
                dve.wait_ge(sem("rs_done"), n + 1)
                tell(dve.reciprocal(rs[:, :], rs[:, :]), aux_free)
                dve.wait_ge(aux_free, a + 2)
                tell(STT(dst, raw[par], g, rs[:, :], MUL, MUL), signal)

            def rotate(a, src, dst):
                dve.wait_ge(aux_full, a + 1)
                tell(TT(tmp[:, :], aux, sinT[:, :], MUL), aux_free)
                mine(TT(dst, src, cosT[:, :], MUL))
                dve.wait_ge(aux_free, a + 2)
                tell(TT(dst, dst, tmp[:, :], ADD), sem("prep_done"))

            def take_transposed(a, dst, src):
                dve.wait_ge(aux_full, a + 1)
                tell(dve.tensor_copy(dst, src), aux_free)
                dve.wait_ge(aux_free, a + 2)
                dve.sem_inc(sem("prep_done"), 1)

            def attention(u, s, masked, beside={}):
                def reciprocal(g):
                    done(dve, "exp_done", u + g)
                    dve.reciprocal(rcp[:, g:g + 1], esum[:, g:g + 1]).then_inc(sem("rcp_done"), 1)

                for g in range(8):
                    b, w = g % 2, P * (g % QT + 1)
                    dst = pbuf[g % 4][:, 0:w]
                    dve.wait_ge(s_full[b], s + g // 2 + 1)
                    dve.wait_ge(sem("t_done"), u + g + 1)
                    masked(g, dst, sc_b[b][:, 0:w], w).then_inc(s_free[b], 1)
                    dve.wait_ge(s_free[b], s + g // 2 + 2)
                    dve.tensor_reduce(nmax[:, g:g + 1], dst, AX.X, MAX, negate=True).then_inc(sem("nmax_done"), 1)
                    if g:
                        reciprocal(g - 1)
                    if g in beside:
                        beside[g]()
                reciprocal(7)
                if 8 in beside:
                    beside[8]()

            dve.wait_ge(sem("c_ready"), 1)
            hold(dve)
            with mine.loop(0, 2) as i:
                for b in range(2):
                    dve.wait_ge(slot_full[b], i * 16 + 16)
                    modulate(ring[b], 8 * i + 4 * b, 4, slot_free[b])

            with mine.loop(0, LAYERS) as layer:
                at = lambda stage, counter, turn=0: LAYER.at(stage, counter, turn, layer)
                dve.wait_ge(vec_in, layer * 16 + 16)
                mine(TT(mod[:, 0:16], mod_next, v1("b_ada", 0, 16), ADD))
                gains(0, 8, v1("g_mix", 0, 8))
                rms_norm(layer * 2, at("norm1", "aux"), layer * 2)
                dve.wait_ge(rel_in, layer * 16 + 16)
                mine(dve.memset(relb[0:HD, :, SEQ - HD:SEQ], NEG))

                a, r = at("misc", "aux"), at("misc", "prep")
                done(dve, "raw_done", r)
                dve.sem_inc(lin_free[0], 1)
                tell(TT(sq[:, :], raw[0], raw[0], MUL), sem("sq_done"))
                norm_tile_end(a, at("misc", "nrm"), 0, kaT, v1("kn_a"), sem("normed"))
                dve.wait_ge(sem("normed"), at("misc", "rope") + 1)
                rotate(a + 1, kaT, kaT)
                done(dve, "raw_done", r + 1)
                dve.sem_inc(lin_free[1], 1)
                rotate(a + 2, raw[1], kiT)
                done(dve, "raw_done", r + 2)
                dve.sem_inc(lin_free[0], 1)
                take_transposed(a + 3, va, aux[:, 0:QT * HD].rearrange("p (a b) -> p a b", b=HD))
                done(dve, "raw_done", r + 3)
                dve.sem_inc(lin_free[1], 1)
                take_transposed(a + 4, wtok, aux[:, 0:QT * 8].rearrange("p (a b) -> p a b", b=8))

                for j in range(4):
                    b = j % 2
                    done(dve, "raw_done", at("idx", "prep") + j)
                    dve.sem_inc(lin_free[b], 1)
                    rotate(at("idx", "aux") + j, raw[b], qT[b])
                    for g in range(6):
                        h2, i = g // 3, g % 3 + 1
                        w = P * (i + 1)
                        n = at("idx", "iu") + 6 * j + g
                        done(dve, "rl_done", n)
                        dve.sem_inc(s_free[g % 2], 1)
                        weight = wtok[:, i, 2 * j + h2:2 * j + h2 + 1]
                        if j == 0 and h2 == 0:
                            ins = TS(score[:, i, 0:w], sm[g % 2][:, 0:w], weight, None, MUL)
                        else:
                            done(dve, "acc_done", n - 3)
                            ins = STT(score[:, i, 0:w], sm[g % 2][:, 0:w], weight, score[:, i, 0:w], MUL, ADD)
                        ins.then_inc(sem("acc_done"), 1)
                done(dve, "acc_done", at("idx", "iu") + 23)
                mine(dve.tensor_copy(mask[:, 0, 0:P], adm[:, SEQ - P:SEQ]))
                for i in range(1, QT):
                    w = P * (i + 1)
                    mine(STT(score[:, i, 0:w], score[:, i, 0:w], IDX_SCALE, adm[:, SEQ - w:SEQ], MUL, ADD))
                mine.restart()
                ROUNDS = TOP_K // 8

                def top_k(r):
                    i = 1 + r // ROUNDS
                    s_i = score[:, i, 0:P * (i + 1)]
                    mine(dve.max(top8, s_i))
                    mine(dve.match_replace(s_i, top8, s_i, TAKEN))
                    if r % ROUNDS == ROUNDS - 1:
                        mine(TS(mask[:, i, 0:P * (i + 1)], s_i, 0.5 * TAKEN, NEG, ALU.is_gt, MUL))

                def prepare_b(j):
                    a, r = at("B", "aux") + 3 * j, at("B", "prep") + 3 * j

                    def square(n):
                        t = 3 * j + n
                        done(dve, "raw_done", r + n)
                        dve.sem_inc(lin_free[t % 2], 1)
                        tell(TT(sq[:, :], raw[t % 2], raw[t % 2], MUL), sem("sq_done"))

                    def normed(n):
                        norm_tile_end(a + n, at("B", "nrm") + 2 * j + n, (3 * j + n) % 2, (qT, kT)[n][j % 2],
                                      v1(("qn_b", "kn_b")[n]), sem("prep_done"))

                    def queries_done():
                        normed(0)
                        square(1)

                    def keys_done():
                        normed(1)
                        done(dve, "raw_done", r + 2)
                        dve.sem_inc(lin_free[(3 * j + 2) % 2], 1)
                        take_transposed(a + 2, vtok[j % 2], aux.rearrange("p (a b) -> p a b", b=P))

                    return {2: lambda: square(0), 5: queries_done, 8: keys_done}

                def prepare_a(j):
                    b, a = j % 2, at("A", "aux") + 2 * j

                    def square():
                        done(dve, "raw_done", at("A", "prep") + j)
                        dve.sem_inc(lin_free[b], 1)
                        tell(TT(sq[:, :], raw[b], raw[b], MUL), sem("sq_done"))

                    def turn():
                        dve.wait_ge(sem("normed"), at("A", "rope") + j + 1)
                        rotate(a + 1, qT[b], qT[b])

                    return {2: square,
                            5: lambda: norm_tile_end(a, at("A", "nrm") + j, b, qT[b], v1("qn_a"), sem("normed")),
                            8: turn}

                def with_top_k(j, steps):
                    def step(g):
                        if g in steps:
                            steps[g]()
                        if g < 8:
                            for r in range((8 * j + g) * 3 * ROUNDS // 32, (8 * j + g + 1) * 3 * ROUNDS // 32):
                                top_k(r)

                    return {g: (lambda g=g: step(g)) for g in range(9)}

                for step in prepare_b(0).values():
                    step()
                for j in range(4):
                    attention(at("B", "u") + 8 * j, at("B", "s") + 4 * j,
                              lambda g, dst, src, w: STT(dst, src, HD ** -0.5, relb[:, 2 * j + g // QT, SEQ - w:SEQ],
                                                         MUL, ADD),
                              with_top_k(j, prepare_b(j + 1) if j < 3 else prepare_a(0)))
                for j in range(4):
                    attention(at("A", "u") + 8 * j, at("A", "s") + 4 * j,
                              lambda g, dst, src, w: STT(dst, src, HD ** -0.5, mask[:, g % QT, 0:w], MUL, ADD),
                              prepare_a(j + 1) if j < 3 else {})

                mine.restart()
                with mine.loop(0, 4) as i:
                    for p in range(2):
                        modulate_beside("gates", i, p, layer, v1d)
                        l, n = at("gates", "lin", i) + 2 * p, at("gates", "sg", i) + 2 * p
                        for b in range(2):
                            dve.wait_ge(sem("sg_done"), n + b + 1)
                            dve.sem_inc(lin_free[b], 1)
                        lin_wait(0, l + 1)
                        tell(TT(tmp[:, :], sg[0][:, :], lin[0], MUL), lin_free[0])
                        lin_wait(1, l + 1)
                        dve.sem_inc(slot_free[p], 1)
                        tell(TT(sg[1][:, :], sg[1][:, :], lin[1], MUL), lin_free[1])
                        dve.wait_ge(lin_free[0], l + 3)
                        dve.sem_inc(sem("sg_free"), 1)
                        dve.wait_ge(lin_free[1], l + 3)
                        tell(TT(merged[:, ds(2 * i + p, 1), :].squeeze(1), tmp[:, :], sg[1][:, :], ADD), sem("sg_free"))
                dve.wait_ge(sem("sg_free"), at("out", "sg") + 2)
                dve.sem_inc(sem("merged_done"), 1)
                dve.sem_inc(sem("mod_summed"), 1)
                gains(8, 32, v1("g_ffn", 0, 8))

                def residual(b, l, k, gate_col, slot=None):
                    lin_wait(b, l)
                    if slot is not None:
                        dve.sem_inc(slot_free[slot], 1)
                    tell(STT(x[:, k, :], lin[b], gate_col, x[:, k, :], MUL, ADD), lin_free[b])
                    dve.sem_inc(sem("x_tiles"), 1)

                for t in range(8):
                    residual(t % 2, at("out", "lin") + t // 2, t, mod[:, 16 + t:17 + t], {3: 0, 7: 1}.get(t))
                for b in range(2):
                    dve.wait_ge(lin_free[b], at("norm2", "lin") + 1)
                dve.sem_inc(sem("x_ready"), 1)
                def split_h(k):
                    dve.wait_ge(sem("h_upper"), layer * KC + (k + 1))
                    TT(h_lo[:, k, :], h[:, k, :], h_hi[:, k, :], SUB).then_inc(sem("h_split"), 1)

                def lower_half(n, p):
                    dve.wait_ge(sem("w_upper"), layer * SPLIT + n + 1)
                    tell(TT(w_lo[p], ring[p][:, 0:2 * KC * P], w_hi[p], SUB), sem("w_split"))

                lower_half(0, 0)
                rms_norm(layer * 2 + 1, at("norm2", "aux"), layer * 2 + 1, split_h)
                def hidden_tile(stage, i, p, k):
                    l, n = at(stage, "lin", i) + p, at(stage, "sg", i) + p
                    dve.wait_ge(sem("sg_done"), n + 1)
                    dve.sem_inc(lin_free[0], 1)
                    lin_wait(1, l)
                    dve.sem_inc(slot_free[p], 1)
                    tell(TT(hid[:, ds(k, 1), :].squeeze(1), sg[p][:, :], lin[1], MUL), sem("sg_free"))
                    dve.wait_ge(sem("sg_free"), n + 3)
                    dve.sem_inc(lin_free[1], 1)

                dve.wait_ge(sem("c_ready"), layer + 2)
                hold(dve)
                mine.restart()
                with mine.loop(0, 8) as i:
                    for p in range(2):
                        modulate_beside("gu", i, p, layer)
                        lower_half(2 * i + (p + 1), 1 - p)
                        hidden_tile("gu", i, p, 2 * i + p)
                with mine.loop(0, 2) as i:
                    for p in range(2):
                        lower_half(2 * i + (p + 17), 1 - p)
                        hidden_tile("gu_rest", i, p, 2 * i + (16 + p))
                lower_half(FF_T - 1, 1)
                hidden_tile("gu_rest", 2, 0, FF_T - 2)
                hidden_tile("gu_rest", 2, 1, FF_T - 1)
                mine.restart()
                dve.sem_inc(sem("hid_done"), 1)
                def lower_down(n, p):
                    dve.wait_ge(sem("w_upper"), layer * SPLIT + n + (FF_T + 1))
                    tell(TT(wd_lo[p], ring[p][:, 0:FF_T * P], wd_hi[p], SUB), sem("w_split"))

                def residual_down(i, p):
                    k = 2 * i + p
                    xk = x[:, k, :] if isinstance(i, int) else x[:, ds(k, 1), :].squeeze(1)
                    gate = mod[:, k + 40:k + 41] if isinstance(i, int) else mod[:, ds(k + 40, 1)]
                    lin_wait(p, at("down", "lin", i))
                    dve.sem_inc(slot_free[p], 1)
                    tell(STT(xk, lin[p], gate, xk, MUL, ADD), lin_free[p])
                    dve.sem_inc(sem("x_tiles"), 1)

                lower_down(0, 0)
                for k in range(FF_T):
                    dve.wait_ge(sem("hid_upper"), layer * FF_T + (k + 1))
                    TT(hid_lo[:, k, :], hid[:, k, :], hid_hi[k], SUB).then_inc(sem("hid_split"), 1)
                mine.restart()
                with mine.loop(0, 3) as i:
                    lower_down(2 * i + 1, 1)
                    residual_down(i, 0)
                    lower_down(2 * i + 2, 0)
                    residual_down(i, 1)
                lower_down(7, 1)
                residual_down(3, 0)
                residual_down(3, 1)
                for b in range(2):
                    dve.wait_ge(lin_free[b], layer * LAYER.total["lin"] + LAYER.total["lin"] + 1)
                dve.sem_inc(sem("x_ready"), 1)

            at = lambda stage, counter, turn=0: SECOND.at(stage, counter, turn)
            R0 = 2 * LAYERS
            mine(TT(mod[:, 0:16], mod_next, v2("b_ada", 0, 16), ADD))
            gains(0, 8, None)
            layer_norm("ln1", 0, h, R0)

            dve.wait_ge(sem("fd_raw"), 1)
            dve.sem_inc(lin_free[0], 1)
            mine(TS(pr[0][0:16, :], raw[0][0:16, :], -1.0, 0.0, MUL, MAX))
            mine(dve.memset(pr[1][0:16, :], 1.0))
            dve.wait_ge(sem("fd_act"), 3)
            mine(TT(pr[0][0:16, :], pr[0][0:16, :], sm[0][0:16, :], ADD))
            tell(dve.tensor_tensor_scan(negF[0:16, :], pr[1][0:16, :], pr[0][0:16, :], 0.0, MUL, ADD), sem("f_done"))
            dve.wait_ge(sem("fd_raw"), 2)
            dve.sem_inc(lin_free[1], 1)
            mine(TS(pts[0][0:32, :], raw[1][0:32, :], 0.0, None, MAX))
            mine(dve.memset(pts[1][0:32, :], 1.0))
            mine(dve.memset(pts[1][0:32, :].rearrange("p (a b) -> p a b", b=P)[:, :, 0:1], 0.0))
            dve.wait_ge(sem("fd_act"), 6)
            mine(TT(dtT[0:32, :], pts[0][0:32, :], sm[1][0:32, :], ADD))
            dve.wait_ge(sem("a_done"), 1)
            mine(TS(pts[0][0:32, :], dtT[0:32, :], gain[0:32, 0:1], -1.0, MUL, MUL))
            tell(dve.tensor_tensor_scan(acs[0:32, :], pts[1][0:32, :], pts[0][0:32, :], 0.0, MUL, ADD), sem("acs_done"))
            a = at("fd", "aux")
            dve.wait_ge(aux_full, a + 1)
            tell(dve.tensor_copy(ftok, aux[:, 0:QT * 16].rearrange("p (a b) -> p a b", b=16)), aux_free)
            dve.wait_ge(aux_full, a + 2)
            tell(dve.tensor_copy(dt_tok, aux[:, 0:QT * 32].rearrange("p (a b) -> p a b", b=32)), aux_free)
            dve.wait_ge(aux_full, a + 3)
            tell(dve.tensor_copy(acs_tok, aux[:, 0:QT * 32].rearrange("p (a b) -> p a b", b=32)), aux_free)
            dve.wait_ge(aux_free, a + 4)
            dve.sem_inc(sem("acs_tok_done"), 1)
            dve.wait_ge(sem("cd_done"), 1)
            tell(TT(te_tok, aux[:, 0:QT * 32].rearrange("p (a b) -> p a b", b=32), acs_tok, SUB), aux_free)
            dve.wait_ge(aux_free, a + 5)
            dve.sem_inc(sem("te_diff"), 1)
            dve.wait_ge(sem("te_exp"), 1)
            mine(TT(te_tok, te_tok, dt_tok, MUL))
            mine.restart()

            def prepare(i, b):
                r = at("att", "prep", i) + 3 * b
                h0 = 4 * i + 2 * b
                two = lambda: slice(h0, h0 + 2) if isinstance(i, int) else ds(h0, 2)

                def projected(n):
                    done(dve, "raw_done", r + n)
                    dve.sem_inc(lin_free[(3 * b + n) % 2], 1)

                def row_of_ones():
                    projected(0)
                    heads = ident[0:16, two()]
                    tell(dve.tensor_copy(fsel[b][0:16, :, :], heads.unsqueeze(2).broadcast_to([16, 2, P])),
                         sem("prep_done"))

                def forget():
                    projected(1)
                    tell(dve.tensor_copy(fq[b], ftok[:, :, two()]), sem("prep_done"))

                def values():
                    projected(2)
                    take_transposed(at("att", "aux", i) + b, vtok[b], aux.rearrange("p (a b) -> p a b", b=P))

                return {2: row_of_ones, 5: forget, 8: values}

            def attend(i, b, beside):
                attention(at("att", "u", i) + 8 * b, at("att", "s", i) + 4 * b,
                          lambda g, dst, src, w: STT(dst, src, fq[b][:, g % QT, g // QT:g // QT + 1],
                                                     causal[:, SEQ - w:SEQ], SUB, ADD), beside)

            for step in prepare(0, 0).values():
                step()
            with mine.loop(0, 3) as i:
                attend(i, 0, prepare(i, 1))
                attend(i, 1, prepare(i + 1, 0))
            attend(3, 0, prepare(3, 1))
            attend(3, 1, {})

            def gated(stage, i, p, add):
                l, n = at(stage, "lin", i) + p, at(stage, "sg", i) + p
                dst = merged2[:, ds(2 * i + p, 1), :].squeeze(1)
                dve.wait_ge(sem("sg_done"), n + 1)
                dve.sem_inc(lin_free[0], 1)
                lin_wait(1, l)
                dve.sem_inc(slot_free[p], 1)
                if not add:
                    tell(TT(dst, sg[p][:, :], lin[1], MUL), sem("sg_free"))
                else:
                    mine(TT(tmp[:, :], sg[p][:, :], lin[1], MUL))
                    tell(TT(dst, dst, tmp[:, :], ADD), sem("sg_free"))
                dve.wait_ge(sem("sg_free"), n + 3)
                dve.sem_inc(lin_free[1], 1)

            with mine.loop(0, 4) as i:
                for p in range(2):
                    modulate_beside("attout", i, p, LAYERS, v2d)
                    gated("attout", i, p, False)
            gains(8, 32, None)

            for t in range(2):
                mine(dve.memset(ub[t][:, 0:16], 0.0))
            for g in range(4):
                w = WINDOWS[g]
                for t in range(2):
                    dve.wait_ge(sem("ub_done"), 2 * g + t + 1)
                    dve.sem_inc(lin_free[t], 1)
                    src = ub[t]
                    for step in range(g + 1):
                        lo, dst = 2 ** (step + 1) - 1, level[step % 2]
                        mine(TT(dst[:, lo:], src[:, lo:], src[:, lo - 2 ** step:16 + SEQ - 2 ** step], ADD))
                        src = dst
                    first = pooled[t][:, 0:16]
                    if g:
                        dve.wait_ge(lin_free[1], at("pool", "lin", g) + 1)
                    mine(TT(first, src[:, 16:32], col("recip", 16 * g, 16), MUL))
                    mine(TT(first, first, ub[t][:, 16:32], SUB))
                    mine(STT(pooled[t][:, 16:], src[:, 32:], 1.0 / w, ub[t][:, 32:], MUL, SUB))
                    dve.sem_inc(sem("ub_free"), 1)
                dve.sem_inc(sem("pooled_done"), 1)
                for t in range(2):
                    k, l, n = 2 * g + t, at("pool", "lin", g) + 1 + t, at("pool", "sg", g) + t
                    dve.wait_ge(sem("sg_done"), n + 1)
                    dve.sem_inc(lin_free[0], 1)
                    lin_wait(1, l)
                    if t:
                        dve.sem_inc(slot_free[1], 1)
                    tell(STT(tmp[:, :], lin[1], v2("pool_scale", k), sg[t][:, :], MUL, MUL), sem("sg_free"))
                    dve.wait_ge(sem("sg_free"), n + 3)
                    dve.sem_inc(lin_free[1], 1)
                    mine(TT(merged2[:, k, :], merged2[:, k, :], tmp[:, :], ADD))
            mine.restart()

            with mine.loop(0, 4) as i:
                mine(dve.tensor_copy(gpar, v2d("ssm", i * SP_N, SP_N)))
                for dst, src in ((dtg, dt_tok), (acsg, acs_tok), (teg, te_tok), (cdg, cd_tok)):
                    mine(dve.tensor_copy(dst, src[:, :, ds(i * 8, 8)]))
                heads = ident[0:32, ds(i * 8, 8)]
                mine(dve.tensor_copy(selh[0:32, :, :], heads.unsqueeze(2).broadcast_to([32, 8, P])))
                mine(dve.tensor_copy(selp[0:32, :, :].rearrange("p a b -> p (a b)").rearrange("p (a b) -> p a b", b=HD),
                                     heads.unsqueeze(2).broadcast_to([32, 8, HD])))
                for b in range(2):
                    mine(dve.memset(cin[b][:, 0:3], 0.0))
                dve.sem_inc(sem("gpar_done"), 1)
                for t in range(6):
                    dve.wait_ge(sem("cin_done"), i * 6 + t + 1)
                    dve.sem_inc(lin_free[t % 2], 1)
                    free(dve, "silu_done", i * 6 + t)
                    c, o = cin[t % 2], cv[t % 2]
                    mine(TS(o, c[:, 0:SEQ], gpar[:, 5 * t:5 * t + 1], None, MUL))
                    for tap in range(1, 4):
                        ins = STT(o, c[:, tap:tap + SEQ], gpar[:, 5 * t + tap:5 * t + tap + 1], o, MUL, ADD)
                        if tap < 3:
                            mine(ins)
                    tell(ins, sem("conv_done"))
                for c in range(QT):
                    dve.wait_ge(sem("xt_done"), i * 4 + c + 1)
                    src = pt_b[c % 2].rearrange("p (a b) -> p a b", b=HD)
                    if c < 3:
                        mine(TT(xde[:, c, :].rearrange("p (a b) -> p a b", b=HD), src,
                                teg[:, c, :].unsqueeze(2).broadcast_to([P, 8, HD]), MUL))
                    tell(TT(xdt[:, c, :].rearrange("p (a b) -> p a b", b=HD), src,
                       dtg[:, c, :].unsqueeze(2).broadcast_to([P, 8, HD]), MUL), sem("xd_done"))
                dve.wait_ge(sem("bt_done"), i + 1)
                tell(dve.tensor_copy(btok.rearrange("p a b -> p (a b)"), ob), sem("btok_done"))
                dve.wait_ge(sem("cb_done"), i + 1)
                tell(TT(cbm, sc_b[0].rearrange("p (a b) -> p a b", b=P), tri.unsqueeze(1).broadcast_to([P, QT, P]), MUL), sem("cbm_done"))
                for t in range(2):
                    dve.wait_ge(sem("sg_done"), at("ssd", "sg", i) + t + 1)
                    dve.sem_inc(lin_free[t], 1)
                for c in range(3):
                    dve.wait_ge(sem("st_done"), i * 3 + c + 1)
                    if c == 0:
                        tell(dve.tensor_copy(hst[:, 0, :], pt_b[0]), sem("hst_done"))
                    else:
                        dve.wait_ge(sem("hst_done"), i * 3 + c)
                        hv = lambda n: hst[:, n, :].rearrange("p (a b) -> p a b", b=HD)
                        mine(TT(hv(c), hv(c - 1), cdg[:, c, :].unsqueeze(2).broadcast_to([P, 8, HD]), MUL))
                        tell(TT(hst[:, c, :], hst[:, c, :], pt_b[c % 2], ADD), sem("hst_done"))

                def pair(j):
                    done(dve, "yd_done", i * 8 + 2 * j + 1)
                    dve.wait_ge(sem("yoff_done"), i * 4 + j + 1)
                    dve.wait_ge(sem("ea_done"), i * 4 + j + 1)
                    mine(TT(tmp[:, P:], pt_b[0][:, P:], ea[:, P:], MUL))
                    mine(STT(yg[:, j, :], xsT[:, j, :], gpar[:, 30 + j:31 + j], ob, MUL, ADD))
                    tell(TT(yg[:, j, P:], yg[:, j, P:], tmp[:, P:], ADD), sem("yp_done"))

                for hh in range(8):
                    dve.wait_ge(sem("bc_done"), i * 8 + hh + 1)
                    free(dve, "wgt_done", i * 8 + hh)
                    mine(TT(seg[hh % 2].rearrange("p (a b) -> p a b", b=P),
                            sc_b[hh % 2].rearrange("p (a b) -> p a b", b=P),
                            acsg[:, :, hh:hh + 1].broadcast_to([P, QT, P]), SUB))
                    tell(TS(seg[hh % 2], seg[hh % 2], 0.0, None, MIN), sem("seg_done"))
                    if hh % 2 == 0 and hh:
                        pair(hh // 2 - 1)
                pair(3)
                dve.wait_ge(sem("yp_done"), i * 4 + 5)
                for t in range(4):
                    n = at("ssd", "sg", i) + t
                    dve.wait_ge(sem("sg_done"), n + 1)
                    if t >= 2:
                        dve.sem_inc(lin_free[t % 2], 1)
                    tell(TT(yg[:, t, :], yg[:, t, :], sg[t % 2][:, :], MUL), sem("sg_free"))
                    dve.sem_inc(sem("yz_done"), 1)
                a = at("ssd", "aux", i)
                dve.wait_ge(sem("root_done"), i + (R0 + 2))
                tell(dve.reciprocal(rstd[:, :], rstd[:, :]), aux_free)
                dve.wait_ge(aux_free, a + 2)
                for t in range(4):
                    mine(STT(yT[:, ds(i * 4 + t, 1), :].squeeze(1), yg[:, t, :], gpar[:, 34 + t:35 + t], rstd[:, :],
                             MUL, MUL))
                mine.restart()
                dve.sem_inc(sem("yT_done"), 1)
            with mine.loop(0, 4) as i:
                for p in range(2):
                    gated("ssdout", i, p, True)
                mine.restart()
            dve.sem_inc(sem("merged2_done"), 1)

            for t in range(8):
                lin_wait(t % 2, at("out", "lin") + t // 2)
                if t % 4 == 3:
                    dve.sem_inc(slot_free[t // 4], 1)
                tell(TS(tmp[:, :], lin[t % 2], mod[:, 16 + t:17 + t], None, MUL), lin_free[t % 2])
                dve.wait_ge(lin_free[t % 2], at("out", "lin") + t // 2 + 2)
                mine(STT(x[:, t, :], x[:, t, :], ALPHA, tmp[:, :], MUL, ADD))
            dve.sem_inc(sem("x_ready"), 1)
            layer_norm("ln2", 1, x, R0 + 5)
            dve.wait_ge(sem("x_ready"), 7)
            layer_norm("ln3", 2, h, R0 + 6)

            rep = lambda v: v.unsqueeze(2).broadcast_to([P, QT, E_N])
            probs, sel, ing, e1, e2, t1, t2, small = rt
            s4 = [small[:, :, n:n + 1].squeeze(2) for n in range(16)]
            a = at("router", "aux")
            dve.wait_ge(aux_full, a + 1)
            tell(dve.tensor_copy(probs, aux[:, 0:QT * E_N].rearrange("p (a b) -> p a b", b=E_N)), aux_free)
            dve.wait_ge(aux_free, a + 2)

            def step(ins):
                mine(ins)

            step(dve.tensor_reduce(s4[0], probs, AX.X, MAX))
            tell(TT(probs, probs, rep(s4[0]), SUB), sem("logit_done"))
            dve.wait_ge(sem("probs_exp"), 1)
            step(dve.tensor_reduce(s4[0], probs, AX.X, ADD))
            step(dve.reciprocal(s4[1], s4[0]))
            step(TT(probs, probs, rep(s4[1]), MUL))
            step(TT(sel, probs, v2("b_router", 0, E_N).unsqueeze(1).broadcast_to([P, QT, E_N]), ADD))
            fold = lambda v: v.rearrange("p a b -> p (a b)").rearrange("p (a b) -> p a b", b=4)
            sf, tf, uf = fold(sel), fold(t1), fold(t2)
            step(TT(tf[:, :, 0:3], sf[:, :, 0:3], sf[:, :, 1:4], ADD))
            step(TT(uf[:, :, 0:2], sf[:, :, 0:2], sf[:, :, 2:4], ADD))
            step(TT(uf[:, :, 2:3], sf[:, :, 0:1], sf[:, :, 3:4], ADD))
            step(TT(tf[:, :, 0:3], tf[:, :, 0:3], uf[:, :, 0:3], MAX))
            gs = small.rearrange("p a b -> p (a b)")[:, 0:16]
            step(dve.tensor_reduce(gs.unsqueeze(2), tf[:, :, 0:3], AX.X, MAX))
            gs = gs.rearrange("p (a b) -> p a b", b=4)
            best = small.rearrange("p a b -> p (a b)")[:, 16:20]
            taken = small.rearrange("p a b -> p (a b)")[:, 20:24]
            pick = small.rearrange("p a b -> p (a b)")[:, 24:40].rearrange("p (a b) -> p a b", b=4)
            step(dve.tensor_reduce(best, gs, AX.X, MAX))
            step(TT(pick, gs, best.unsqueeze(2).broadcast_to([P, QT, 4]), ALU.is_equal))
            col4 = lambda v, n: v[:, :, n:n + 1].squeeze(2)
            step(dve.tensor_copy(taken, col4(pick, 0)))
            for n in range(1, 4):
                step(TT(col4(gs, n), col4(pick, n), taken, MUL))
                step(TT(col4(pick, n), col4(pick, n), col4(gs, n), SUB))
                step(TT(taken, taken, col4(pick, n), ADD))
            pk = small.rearrange("p a b -> p (a b)")[:, 24:40]
            step(dve.tensor_copy(fold(ing), pk.unsqueeze(2).broadcast_to([P, 16, 4])))
            step(TT(sel, sel, ing, MUL))
            step(TS(ing, ing, 1.0, -NEG, SUB, MUL))
            step(TT(sel, sel, ing, ADD))
            rev = col("revidx", 0, E_N).unsqueeze(1).broadcast_to([P, QT, E_N])
            for e in (e1, e2):
                step(dve.tensor_reduce(s4[0], sel, AX.X, MAX))
                step(TT(t1, sel, rep(s4[0]), ALU.is_equal))
                step(TT(t1, t1, rev, MUL))
                step(dve.tensor_reduce(s4[0], t1, AX.X, MAX))
                step(TT(e, t1, rep(s4[0]), ALU.is_equal))
                step(STT(sel, e, 4 * NEG, sel, MUL, ADD))
            step(TT(gw, e1, e2, ADD))
            dve.sem_inc(sem("chosen"), 1)
            for e, wt in ((e1, weight1), (e2, weight2)):
                step(TT(t1, e, probs, MUL))
                step(dve.tensor_reduce(wt, t1, AX.X, ADD))
            step(TT(s4[0], weight1, weight2, ADD))
            step(dve.reciprocal(s4[1], s4[0]))
            for wt in (weight1, weight2):
                step(TT(wt, wt, s4[1], MUL))
            E = slice(0, E_N)
            step(dve.memset(unit[E], 1.0))
            dve.wait_ge(aux_full, a + 2)
            tell(dve.tensor_copy(chosenT[E], aux[E, :]), aux_free)
            dve.wait_ge(aux_free, a + 3)
            step(dve.tensor_tensor_scan(cum[E], unit[E], chosenT[E], 0.0, MUL, ADD))
            step(TT(fits[E], col("steps", 0, QT)[E], cum[E, SEQ - 1:SEQ].broadcast_to([E_N, QT]), ALU.is_lt))
            tell(dve.tensor_reduce(n_blocks[E], fits[E], AX.X, ADD), sem("blocks_counted"))
            dve.wait_ge(aux_full, a + 3)
            tell(dve.tensor_copy(ends[E], aux[E, 0:1]), aux_free)
            dve.wait_ge(aux_free, a + 4)
            tell(TT(past[E], col("blocks", 0, N_BLK)[E], ends[E].broadcast_to([E_N, N_BLK]), ALU.is_ge), sem("past_done"))
            step(TT(base[E], ends[E], n_blocks[E], SUB))
            step(TS(base[E], base[E], float(P), -1.0, MUL, ADD))
            tell(TS(position[E], cum[E], base[E], None, ADD), sem("position_done"))
            dve.wait_ge(aux_full, a + 4)
            tell(TS(past, aux[:, 0:N_BLK], float(E_N - 1), None, MIN), aux_free)
            dve.wait_ge(aux_free, a + 5)
            tell(dve.tensor_copy(expert_of, past), sem("experts_known"))
            dve.wait_ge(aux_full, a + 5)
            tell(dve.tensor_copy(t2, aux[:, 0:QT * E_N].rearrange("p (a b) -> p a b", b=E_N)), aux_free)
            dve.wait_ge(aux_free, a + 6)
            for e, dest, row in ((e1, dest1, row1), (e2, dest2, row2)):
                step(TT(t1, e, t2, MUL))
                step(dve.tensor_reduce(dest, t1, AX.X, ADD))
                step(dve.tensor_copy(row, dest))
            dve.sem_inc(sem("rows_known"), 1)
            mine.restart()

            def rows_half(b, par):
                dve.wait_ge(sem("rows_turned"), b + 1)
                tell(dve.tensor_copy(xT[par][:, SEQ:], pt_b[1]), sem("xTd_done"))

            def gated_block(b):
                dve.wait_ge(sem("silu_read"), b + 1)
                dve.wait_ge(sem("u_done"), b + 1)
                tell(TT(hidb, sg[0][:, :], lin[1], MUL), sem("hidden"))

            def made_half(b, par, first=False):
                dve.wait_ge(sem("d_done"), b + 2)
                if not first:
                    dve.wait_ge(sem("made_out"), (b - 1) * 16)
                tell(dve.tensor_copy(yb[par][:, SEQ:], sc_b[1]), sem("yd2_done"))

            rows_half(0, 0)
            rows_half(1, 1)
            gated_block(0)

            def block_step(b, par, first=False):
                made_half(b - 1, 1 - par, first)
                rows_half(b + 1, 1 - par)
                gated_block(b)

            for b in (1, 2):
                block_step(b, b % 2, True)
            with mine.loop(1, (N_BLK - 1) // 2) as i:
                for n in range(2):
                    block_step(2 * i + (n + 1), (n + 1) % 2)
            made_half(N_BLK - 1, (N_BLK - 1) % 2)
            second = merged2.rearrange("p a b -> p (a b)").rearrange("p (a b) -> p a b", b=D)
            for t in range(QT):
                dve.wait_ge(sem("gathered%d" % t), 32)
                mine(TS(htok[:, t, :], htok[:, t, :], weight1[:, t:t + 1], None, MUL))
                tell(STT(htok[:, t, :], second[:, t, :], weight2[:, t:t + 1], htok[:, t, :], MUL, ADD), sem("combined"))
            dve.wait_ge(sem("ffn_done"), 2 * QT)
            for t in range(8):
                mine(TS(moe[:, t, :], moe[:, t, :], mod[:, 40 + t:41 + t], None, MUL))
            for t in range(8):
                mine(STT(x[:, t, :], x[:, t, :], ALPHA, moe[:, t, :], MUL, ADD))
            dve.sem_inc(sem("x_ready"), 1)
            layer_norm("ln4", 3, x, R0 + 7)

        @block.gpsimd
        def _(pool):
            mine = Steps(pool, sem("pool_steps"))
            tell = mine.tell
            pool.sem_inc(sem("pn_done"), 2)
            pool.sem_inc(sem("wgt_done"), 2)

            def attention(u):
                for g in range(8):
                    w = P * (g % QT + 1)
                    pool.wait_ge(sem("rcp_done"), u + g + 1)
                    pool.tensor_tensor(pbuf[g % 4][:, 0:w], pbuf[g % 4][:, 0:w], rcp[:, g:g + 1].broadcast_to([P, w]),
                                       ALU.mult).then_inc(sem("pn_done"), 1)

            with mine.loop(0, LAYERS) as layer:
                for stage in ("B", "A"):
                    for j in range(4):
                        attention(LAYER.at(stage, "u", 0, layer) + 8 * j)
            zeros = abuf[:, 0:2, :].rearrange("p a b -> p (a b)")
            tell(pool.memset(zeros, 0.0), sem("zeroed"))
            pool.wait_ge(sem("zeroed"), 1)
            pool.dma_start(routed.rearrange("(a p) n -> p a n", p=P), zeros.unsqueeze(1).broadcast_to([P, N_BLK + 1, D]))\
                .then_inc(sem("zeros_out"), 16)
            pool.wait_ge(sem("zeros_out"), 16)
            with mine.loop(0, 4) as i:
                for b in range(2):
                    attention(SECOND.at("att", "u", i) + 8 * b)
            with mine.loop(0, 4) as i:
                pool.wait_ge(sem("cbm_done"), i + 1)
                for hh in range(8):
                    pool.wait_ge(sem("e_done"), i * 8 + hh + 1)
                    free(pool, "yd_done", i * 8 + hh)
                    tell(pool.tensor_tensor(wgt[hh % 2], seg[hh % 2], cbm.rearrange("p a b -> p (a b)"), ALU.mult), sem("wgt_done"))
            pool.wait_ge(sem("rows_known"), 1)
            pool.wait_ge(sem("htok_done"), 2 * QT)
            for t in range(QT):
                for row in (row1, row2):
                    pool.indirect_dma_start(routed, bass.IndirectOffsetOnAxis(row[:, t:t + 1], 0), htok[:, t, :], None)\
                        .then_inc(sem("scattered"), 16)
            pool.wait_ge(sem("scattered"), 2 * QT * 16)

            def load_rows(b):
                pool.dma_start(xr, routed[ds(b * P, P), :]).then_inc(sem("rows_in"), 16)

            def store_made(b, par):
                pool.wait_ge(sem("ya_done"), b + 2)
                pool.wait_ge(sem("yd2_done"), b + 2)
                pool.dma_start(made[ds(b * P, P), :], yb[par]).then_inc(sem("made_out"), 16)

            load_rows(0)
            pool.wait_ge(sem("rows_turned"), 1)
            load_rows(1)
            pool.wait_ge(sem("rows_turned"), 2)
            load_rows(2)
            with pool.Fori(0, (N_BLK - 1) // 2 - 1) as i:
                for n in range(2):
                    b = 2 * i + (n + 1)
                    store_made(b - 1, n)
                    pool.wait_ge(sem("rows_turned"), b + 2)
                    load_rows(b + 2)
            store_made(N_BLK - 3, 0)
            pool.wait_ge(sem("rows_turned"), N_BLK)
            load_rows(N_BLK)
            store_made(N_BLK - 2, 1)
            store_made(N_BLK - 1, 0)
            pool.wait_ge(sem("made_out"), N_BLK * 16)
            second = merged2.rearrange("p a b -> p (a b)").rearrange("p (a b) -> p a b", b=D)
            for t in range(QT):
                for row, dst in ((row1, htok), (row2, second)):
                    pool.indirect_dma_start(dst[:, t, :], None, made, bass.IndirectOffsetOnAxis(row[:, t:t + 1], 0))\
                        .then_inc(sem("gathered%d" % t), 16)



def _constants():
    c = np.zeros((P, NCST), np.float32)

    def put(name, value):
        a, b = CST[name]
        c[:, a:b] = value

    q, k = np.arange(P)[:, None], np.arange(P)[None, :]
    put("ident", q == k)
    put("blockones", q // HD == k // HD)
    put("ones", 1)
    same = q // HD == k // HD
    put("rope", 1.0 * (same & (k % HD >= 8) & (k % HD < 16) & (q == k - 8)) - 1.0 * (same & (k % HD < 8) & (q == k + 8)))
    put("last", q == P - 1)
    adm, causal = np.zeros((P, SEQ)), np.zeros((P, SEQ))
    adm[:, SEQ - P:] = np.where(k // HD > q // HD, NEG, 0)
    causal[:, SEQ - P:] = np.where(k > q, NEG, 0)
    put("adm", adm)
    put("causal", causal)
    put("tri", k >= q)
    put("recip", np.concatenate([1 / np.minimum(np.arange(1, 17), w) for w in WINDOWS])[None])
    inv = np.float32(500000.0) ** (-np.arange(0, 16, 2, dtype=np.float32) / np.float32(16))
    d = np.arange(P) % HD
    put("inv_freq", np.where(d < 16, inv[d % 8], 0).astype(np.float32)[:, None])
    put("revidx", np.arange(E_N, 0, -1)[None])
    put("blocks", np.arange(N_BLK)[None])
    put("steps", P * np.arange(QT)[None])
    return c


def _tiles(v):
    return v.reshape(-1, P).T


def _chunks(w):
    return w.reshape(-1, P, w.shape[1]).transpose(1, 0, 2).reshape(P, -1)


def _slot(*parts):
    return np.concatenate([_chunks(w) for w in parts], axis=1).reshape(-1)


def kernel(**inputs):
    import concourse.bacc as _bacc
    from concourse.bass_utils import run_bass_kernel_spmd as _run

    g = {k: np.asarray(v) for k, v in inputs.items()}
    slots, vec1, rel = [], [], []
    ada = lambda w, a, b: w[:, a * P:b * P].T.reshape(b - a, P, D).transpose(1, 0, 2).reshape(-1)
    slots += [ada(g["w_ada"][0], 4 * i, 4 * i + 4) for i in range(4)]
    for l in range(LAYERS):
        w_in, b_in = g["w_in"][l], g["b_in"][l]
        cols = lambda at, n: w_in[:, at:at + n]
        tile = lambda w, i: w[:, i * P:(i + 1) * P]
        two = lambda a: np.concatenate([a, a], axis=-1)
        slots += [_slot(two(cols(KA, HD)), two(cols(KI, HD))), _slot(cols(VA, HD), cols(WI, 8))]
        slots += [_slot(cols(QI + i * P, P)) for i in range(4)]
        slots += [_slot(cols(QB + i * P, P), cols(KB + i * P, P), cols(VB + i * P, P)) for i in range(4)]
        slots += [_slot(cols(QA + i * P, P)) for i in range(4)]
        for i in range(8):
            slots += [_slot(cols(GA + i * P, P), cols(GB + i * P, P), tile(g["w_oa"][l], i), tile(g["w_ob"][l], i))]
            slots += [ada(g["w_ada"][l], a, a + 2) for a in (16 + 4 * i, 18 + 4 * i)]
        slots += [_slot(g["w_out"][l][:, i * 512:(i + 1) * 512]) for i in range(2)]
        w_ada_next = g["w_ada"][l + 1] if l + 1 < LAYERS else g["w_ada_2"][0]
        for i in range(FF_T):
            slots += [_slot(tile(g["w_gu"][l], i), g["w_gu"][l][:, FF + i * P:FF + (i + 1) * P])]
            slots += [ada(w_ada_next, i, i + 1)] if i < 16 else []
        slots += [_slot(tile(g["w_down"][l], i)) for i in range(8)]
        v = np.zeros((P, NV1), np.float32)

        def put(name, value):
            a, b = VEC1[name]
            v[0:value.shape[0], a:b] = value

        put("b_ada", _tiles(g["b_ada"][l]))
        put("g_mix", _tiles(g["g_mix"][l]))
        put("g_ffn", _tiles(g["g_ffn"][l]))
        for name, at, n in (("qa", QA, 4), ("qi", QI, 4), ("qb", QB, 4), ("kb", KB, 4), ("vb", VB, 4), ("ga", GA, 8),
                            ("gb", GB, 8)):
            put(name, _tiles(b_in[at:at + n * P]))
        put("ka", two(b_in[KA:KA + HD])[:, None])
        put("ki", two(b_in[KI:KI + HD])[:, None])
        put("va", b_in[VA:VA + HD][:, None])
        put("wi", b_in[WI:WI + 8][:, None])
        for name in ("qn_a", "kn_a", "qn_b", "kn_b"):
            put(name, two(g[name][l])[:, None])
        vec1.append(v.reshape(-1))
        at = np.clip(np.arange(P)[:, None] - np.arange(SEQ)[None] + SEQ - P, -63, 256) + 63
        rel.append(g["rel_bias"][l][:, at].transpose(1, 0, 2).reshape(-1))

    w2, tile = g["w_in_2"][0], lambda w, i, n=P: w[:, i * n:(i + 1) * n]
    cols = lambda at, n: w2[:, at:at + n]
    slots += [_slot(cols(F2, 16)), _slot(cols(DT2, 32))]
    slots += [_slot(cols(Q2 + i * P, P), cols(K2 + i * P, P), cols(V2 + i * P, P)) for i in range(8)]
    for i in range(8):
        slots += [_slot(cols(G2 + i * P, P), tile(g["w_attn_o_2"][0], i))]
        slots += [ada(g["w_ada_2"][0], a, a + 2) for a in (16 + 4 * i, 18 + 4 * i)]
    for i in range(4):
        slots += [_slot(cols(U2 + i * 256, 256)), _slot(cols(G2 + D + i * 256, 256), g["w_pool_2"][0][i])]
    for i in range(4):
        bc = np.concatenate([cols(XBC2 + 2048 + i * P, P), cols(XBC2 + 2560 + i * P, P)], axis=1)
        slots += [_slot(cols(XBC2 + i * 512, 512)), _slot(bc), _slot(cols(Z2 + i * 512, 256)),
                  _slot(cols(Z2 + i * 512 + 256, 256))]
    slots += [_slot(cols(G2 + 2 * D + i * P, P), tile(g["w_ssm_o_2"][0], i)) for i in range(8)]
    slots += [_slot(tile(g["w_out_2"][0], i, 512)) for i in range(2)]
    for e in range(E_N):
        slots += [_slot(g["w_exp_gate_2"][0, e]), _slot(g["w_exp_up_2"][0, e]), _slot(g["w_exp_down_2"][0, e])]

    v2_ = np.zeros((P, NV2), np.float32)

    def put2(name, value):
        a, b = VEC2[name]
        v2_[0:value.shape[0], a:b] = value

    put2("b_ada", _tiles(g["b_ada_2"][0]))
    for name in ("pool_scale", "ln_mix_g", "ln_mix_b", "ln_ffn_g", "ln_ffn_b"):
        put2(name, _tiles(g[name + "_2"][0]))
    for name in ("b_forget", "dt_bias", "a_log"):
        put2(name, g[name + "_2"][0][:, None])
    taps = np.concatenate([g["conv_w_2"][0], g["conv_b_2"]], axis=0).reshape(5, 24, P).transpose(2, 1, 0)
    skip = np.repeat(g["d_skip_2"][0], HD).reshape(16, P).T
    norm = _tiles(g["ssm_norm_w_2"][0])
    for i in range(4):
        a = VEC2["ssm"][0] + i * SP_N
        for n, t in enumerate((4 * i, 4 * i + 1, 4 * i + 2, 4 * i + 3, 16 + i, 20 + i)):
            v2_[:, a + 5 * n:a + 5 * n + 5] = taps[:, t]
        v2_[:, a + 30:a + 34] = skip[:, 4 * i:4 * i + 4]
        v2_[:, a + 34:a + 38] = norm[:, 4 * i:4 * i + 4]
    put2("w_router", _chunks(g["w_router_2"]))
    put2("b_router", np.broadcast_to(g["b_router_2"], (P, E_N)))

    arrays = {
        "w_all": np.concatenate(slots),
        "vec1": np.concatenate(vec1),
        "vec2": v2_,
        "consts": _constants(),
        "x_in": np.ascontiguousarray(g["x"][0].T.reshape(KC, P, SEQ).transpose(1, 0, 2)),
        "pos": np.ascontiguousarray(np.broadcast_to(g["positions"], (P, SEQ))),
        "cond": np.ascontiguousarray(np.broadcast_to(np.concatenate([g["c"][0], g["c"][0], g["c_2"][0]]), (P, 3 * D))),
        "rel": np.concatenate(rel),
    }
    nc = _bacc.Bacc("TRN2", target_bir_lowering=False, num_devices=1)
    args = [nc.dram_tensor("in_" + k, a.shape, mybir.dt.from_np(a.dtype), kind="ExternalInput").ap() for k, a in arrays.items()]
    out = nc.dram_tensor("out", (P, KC, SEQ), F32, kind="ExternalOutput").ap()
    two_blocks(nc, *args[:4], *args[4:], out)
    r = _run(nc, [{"in_" + k: a for k, a in arrays.items()}], core_ids=[0])
    y = r.results[0]["out"]
    return np.ascontiguousarray(y.transpose(1, 0, 2).reshape(D, SEQ).T)[None]
```
